# Optimizing a Trainium2 kernel written in Bass

```python
import jax, jax.numpy as jnp
from jax import lax
import numpy as np

D_MODEL = 1024
BATCH = 1
SEQ = 256
DEPTH = 1

MEM_LEN = 256
MOBA_HEADS = D_MODEL // 128
MOBA_HEAD_DIM = 64
MOBA_WIDTH = MOBA_HEADS * MOBA_HEAD_DIM
MOBA_BLOCK = 256
MOBA_TOPK = 3
MOBA_Q_CHUNK = 32
GLA_HEADS = 4
GLA_VAL_DIM = (D_MODEL // 2) // GLA_HEADS
GLA_KEY_DIM = GLA_VAL_DIM // 2
GLA_K_WIDTH = GLA_HEADS * GLA_KEY_DIM
GLA_V_WIDTH = GLA_HEADS * GLA_VAL_DIM
GLA_GATE_RANK = 16
GLA_GATE_TEMP = 16.0
GLA_CHUNK = 64
MIX_WIDTH = MOBA_WIDTH + GLA_V_WIDTH
IN_SPLITS = (MOBA_WIDTH, MOBA_WIDTH, MOBA_WIDTH, GLA_K_WIDTH, GLA_K_WIDTH, GLA_V_WIDTH, GLA_V_WIDTH, GLA_GATE_RANK)
IN_WIDTH = 3 * MOBA_WIDTH + 2 * GLA_K_WIDTH + 2 * GLA_V_WIDTH + GLA_GATE_RANK
XATTN_HEADS = 4
XATTN_HEAD_DIM = D_MODEL // XATTN_HEADS
D_FF = 4 * D_MODEL
LN_EPS = 1e-5
RMS_EPS = 1e-6
DEEPNORM_ALPHA = (2.0 * DEPTH) ** 0.25
DEEPNORM_BETA = (8.0 * DEPTH) ** -0.25

kernel_name = "hymba_moba_gla_deepnorm_layer"

def _heads(t, n_heads):
    b, s, _ = t.shape
    return t.reshape(b, s, n_heads, -1).transpose(0, 2, 1, 3)

def _merge(t):
    b, h, s, d = t.shape
    return t.transpose(0, 2, 1, 3).reshape(b, s, h * d)

def _layer_norm(x, g, b):
    xf = x.astype(jnp.float32)
    mu = jnp.mean(xf, axis=-1, keepdims=True)
    var = jnp.mean(jnp.square(xf - mu), axis=-1, keepdims=True)
    return ((xf - mu) * lax.rsqrt(var + LN_EPS) * g + b).astype(x.dtype)

def _alibi_slopes(n_heads):
    return 2.0 ** (-8.0 * jnp.arange(1, n_heads + 1, dtype=jnp.float32) / n_heads)

def _moba(q, k, v):
    B, H, S, dh = q.shape
    s_pad = -(-S // MOBA_BLOCK) * MOBA_BLOCK
    pad = [(0, 0), (0, 0), (0, s_pad - S), (0, 0)]
    q, k, v = jnp.pad(q, pad), jnp.pad(k, pad), jnp.pad(v, pad)
    nb = s_pad // MOBA_BLOCK
    topk = min(MOBA_TOPK, nb)
    scale = dh ** -0.5
    slopes = _alibi_slopes(H)
    kb = k.reshape(B, H, nb, MOBA_BLOCK, dh)
    vb = v.reshape(B, H, nb, MOBA_BLOCK, dh)
    kmean = jnp.mean(kb.astype(jnp.float32), axis=3)
    gate = jnp.einsum('bhsd,bhnd->bhsn', q.astype(jnp.float32), kmean)
    qblk = jnp.arange(s_pad) // MOBA_BLOCK
    past = jnp.arange(nb)[None, :] < qblk[:, None]
    gate = jnp.where(past, gate, -jnp.inf)
    gval, gidx = lax.top_k(gate, topk)
    gvalid = jnp.isfinite(gval)
    bi = jnp.arange(B)[:, None, None, None]
    hi = jnp.arange(H)[None, :, None, None]
    blk_off = jnp.arange(MOBA_BLOCK)

    def chunk(c):
        t0 = c * MOBA_Q_CHUNK
        qc = lax.dynamic_slice_in_dim(q, t0, MOBA_Q_CHUNK, axis=2)
        idx = lax.dynamic_slice_in_dim(gidx, t0, MOBA_Q_CHUNK, axis=2)
        valid = lax.dynamic_slice_in_dim(gvalid, t0, MOBA_Q_CHUNK, axis=2)
        tpos = t0 + jnp.arange(MOBA_Q_CHUNK)
        blk = t0 // MOBA_BLOCK
        k_own = lax.dynamic_index_in_dim(kb, blk, axis=2, keepdims=False)
        v_own = lax.dynamic_index_in_dim(vb, blk, axis=2, keepdims=False)
        dist_own = tpos[:, None] - (blk * MOBA_BLOCK + blk_off)[None, :]
        s_own = jnp.einsum('bhqd,bhkd->bhqk', qc, k_own).astype(jnp.float32) * scale
        s_own = s_own - slopes[:, None, None] * dist_own.astype(jnp.float32)
        s_own = jnp.where(dist_own >= 0, s_own, -jnp.inf)
        k_sel = kb[bi, hi, idx]
        v_sel = vb[bi, hi, idx]
        dist_sel = tpos[:, None, None] - (idx[..., None] * MOBA_BLOCK + blk_off)
        s_sel = jnp.einsum('bhqd,bhqjkd->bhqjk', qc, k_sel).astype(jnp.float32) * scale
        s_sel = s_sel - slopes[None, :, None, None, None] * dist_sel.astype(jnp.float32)
        s_sel = jnp.where(valid[..., None], s_sel, -jnp.inf)
        s_all = jnp.concatenate([s_own, s_sel.reshape(B, H, MOBA_Q_CHUNK, topk * MOBA_BLOCK)], axis=-1)
        p = jax.nn.softmax(s_all, axis=-1).astype(v.dtype)
        p_own = p[..., :MOBA_BLOCK]
        p_sel = p[..., MOBA_BLOCK:].reshape(B, H, MOBA_Q_CHUNK, topk, MOBA_BLOCK)
        o = jnp.einsum('bhqk,bhkd->bhqd', p_own, v_own) + jnp.einsum('bhqjk,bhqjkd->bhqd', p_sel, v_sel)
        return o

    out = lax.map(chunk, jnp.arange(s_pad // MOBA_Q_CHUNK))
    out = out.transpose(1, 2, 0, 3, 4).reshape(B, H, s_pad, dh)
    return out[:, :, :S].astype(q.dtype)

def _gla(q, k, v, log_a):
    B, H, S, dk = q.shape
    dv = v.shape[-1]
    C = GLA_CHUNK
    n = S // C

    def to_chunks(t):
        return t.astype(jnp.float32).reshape(B, H, n, C, t.shape[-1]).transpose(2, 0, 1, 3, 4)

    xs = (to_chunks(q * (dk ** -0.5)), to_chunks(k), to_chunks(v), to_chunks(log_a))
    causal = jnp.tril(jnp.ones((C, C), dtype=bool))

    def step(state, inp):
        qc, kc, vc, gc = inp
        b = jnp.cumsum(gc, axis=2)
        o_inter = jnp.einsum('bhtd,bhde->bhte', qc * jnp.exp(b), state)
        diff = b[:, :, :, None, :] - b[:, :, None, :, :]
        decay = jnp.exp(jnp.where(causal[:, :, None], diff, -jnp.inf))
        attn = jnp.einsum('bhtd,bhsd,bhtsd->bhts', qc, kc, decay)
        o_intra = jnp.einsum('bhts,bhse->bhte', attn, vc)
        b_last = b[:, :, -1:, :]
        new_state = jnp.exp(b_last[:, :, 0, :])[..., None] * state + jnp.einsum('bhsd,bhse->bhde', kc * jnp.exp(b_last - b), vc)
        return new_state, o_inter + o_intra

    init = jnp.zeros((B, H, dk, dv), jnp.float32)
    _, out = lax.scan(step, init, xs)
    return out.transpose(1, 2, 0, 3, 4).reshape(B, H, S, dv)

def _hybrid_mixer(h, w_in, w_gate_up, b_gate, gla_norm_g, w_mix_o):
    proj = h @ w_in
    cuts = np.cumsum(IN_SPLITS)[:-1].tolist()
    qa, ka, va, qg, kg, vg, rg, glr = jnp.split(proj, cuts, axis=-1)
    moba_o = _merge(_moba(_heads(qa, MOBA_HEADS), _heads(ka, MOBA_HEADS), _heads(va, MOBA_HEADS)))
    log_a = jax.nn.log_sigmoid((glr @ w_gate_up + b_gate).astype(jnp.float32)) / GLA_GATE_TEMP
    o = _gla(_heads(qg, GLA_HEADS), _heads(kg, GLA_HEADS), _heads(vg, GLA_HEADS), _heads(log_a, GLA_HEADS))
    o = o * lax.rsqrt(jnp.mean(jnp.square(o), axis=-1, keepdims=True) + RMS_EPS) * gla_norm_g
    gla_o = (_merge(o) * jax.nn.silu(rg.astype(jnp.float32))).astype(h.dtype)
    mix = jnp.concatenate([moba_o, gla_o], axis=-1)
    return mix @ w_mix_o

def _mem_xattn(h, mem, w_xq, w_xkv, w_xo):
    q = _heads(h @ w_xq, XATTN_HEADS)
    k, v = jnp.split(mem @ w_xkv, 2, axis=-1)
    k, v = _heads(k, XATTN_HEADS), _heads(v, XATTN_HEADS)
    s = jnp.einsum('bhsd,bhmd->bhsm', q, k).astype(jnp.float32) * (XATTN_HEAD_DIM ** -0.5)
    p = jax.nn.softmax(s, axis=-1).astype(v.dtype)
    return _merge(jnp.einsum('bhsm,bhmd->bhsd', p, v)) @ w_xo

def _sq_relu_mlp(h, w_ff1, w_ff2):
    return jnp.square(jax.nn.relu(h @ w_ff1)) @ w_ff2

def setup_inputs(seed: int = 0) -> dict:
    key = jax.random.key(seed)
    ks = jax.random.split(key, 32)
    f32 = jnp.float32

    def nrm(k, shape, fan_in, gain=1.0):
        return jax.random.normal(k, shape, f32) * (gain * fan_in ** -0.5)

    L = DEPTH
    b = DEEPNORM_BETA
    in_gains = (1.0, 1.0, b, 1.0, 1.0, b, 1.0, 1.0)
    pieces = [nrm(ks[10 + i], (L, D_MODEL, w), D_MODEL, g) for i, (w, g) in enumerate(zip(IN_SPLITS, in_gains))]
    w_in = jnp.concatenate(pieces, axis=-1)
    xkv = jnp.concatenate([nrm(ks[20], (L, D_MODEL, D_MODEL), D_MODEL), nrm(ks[21], (L, D_MODEL, D_MODEL), D_MODEL, b)], axis=-1)
    return {
        "x": jax.random.normal(ks[0], (BATCH, SEQ, D_MODEL), f32),
        "mem": jax.random.normal(ks[1], (BATCH, MEM_LEN, D_MODEL), f32),
        "w_in": w_in,
        "w_gate_up": nrm(ks[2], (L, GLA_GATE_RANK, GLA_K_WIDTH), GLA_GATE_RANK),
        "b_gate": 0.1 * jax.random.normal(ks[3], (L, GLA_K_WIDTH), f32),
        "gla_norm_g": 1.0 + 0.02 * jax.random.normal(ks[4], (L, GLA_VAL_DIM), f32),
        "w_mix_o": nrm(ks[5], (L, MIX_WIDTH, D_MODEL), MIX_WIDTH, b),
        "ln1_g": 1.0 + 0.02 * jax.random.normal(ks[6], (L, D_MODEL), f32),
        "ln1_b": 0.02 * jax.random.normal(ks[7], (L, D_MODEL), f32),
        "w_xq": nrm(ks[8], (L, D_MODEL, D_MODEL), D_MODEL),
        "w_xkv": xkv,
        "w_xo": nrm(ks[9], (L, D_MODEL, D_MODEL), D_MODEL, b),
        "ln2_g": 1.0 + 0.02 * jax.random.normal(ks[22], (L, D_MODEL), f32),
        "ln2_b": 0.02 * jax.random.normal(ks[23], (L, D_MODEL), f32),
        "w_ff1": nrm(ks[24], (L, D_MODEL, D_FF), D_MODEL, b),
        "w_ff2": nrm(ks[25], (L, D_FF, D_MODEL), D_FF, b),
        "ln3_g": 1.0 + 0.02 * jax.random.normal(ks[26], (L, D_MODEL), f32),
        "ln3_b": 0.02 * jax.random.normal(ks[27], (L, D_MODEL), f32),
    }

def reference(x, mem, w_in, w_gate_up, b_gate, gla_norm_g, w_mix_o, ln1_g, ln1_b, w_xq, w_xkv, w_xo, ln2_g, ln2_b, w_ff1, w_ff2, ln3_g, ln3_b):
    for l in range(DEPTH):
        mix = _hybrid_mixer(x, w_in[l], w_gate_up[l], b_gate[l], gla_norm_g[l], w_mix_o[l])
        x = _layer_norm(DEEPNORM_ALPHA * x + mix, ln1_g[l], ln1_b[l])
        xa = _mem_xattn(x, mem, w_xq[l], w_xkv[l], w_xo[l])
        x = _layer_norm(DEEPNORM_ALPHA * x + xa, ln2_g[l], ln2_b[l])
        ff = _sq_relu_mlp(x, w_ff1[l], w_ff2[l])
        x = _layer_norm(DEEPNORM_ALPHA * x + ff, ln3_g[l], ln3_b[l])
    return x


_drawn_inputs = setup_inputs


def setup_inputs(seed=0):
    import zlib

    import numpy as np

    out = dict(_drawn_inputs(seed))
    spreads = {}
    factors = {'w_gate_up': 2.839,
     'b_gate': 7.089,
     'gla_norm_g': 25.296,
     'ln1_g': 2.716,
     'ln1_b': 2.861,
     'ln2_g': 7.664,
     'ln2_b': 7.863,
     'ln3_g': 7.821,
     'ln3_b': 8.73}
    for name, (base, spread) in spreads.items():
        noise = np.random.default_rng([zlib.crc32(name.encode()), seed]).standard_normal(out[name].shape)
        drawn = base * np.exp(spread * noise) if base else spread * noise
        out[name] = __import__('jax').numpy.asarray(drawn.astype(out[name].dtype))
    for name, factor in factors.items():
        out[name] = (out[name] * factor).astype(out[name].dtype)
    return out
```

```python
from contextlib import ExitStack

import numpy as np
import concourse.bass as bass
from concourse import mybir

D = 1024
S = 256
P = 128
HA, DA = 8, 64
HG, DK, DV = 4, 64, 128
CHUNK = 64
RANK = 16
HX, DX = 4, 256
F = 4 * D
GATE_TEMP = 16.0
LN_EPS, RMS_EPS = 1e-5, 1e-6
ALPHA = 2.0 ** 0.25
QA, KA, VA, QG, KG, VG, RG, GL = 0, 512, 1024, 1536, 1792, 2048, 2560, 3072
LEVELS = [64, 32, 16, 8, 4, 2, 1]
SLOPES = [2.0 ** (-8.0 * (h + 1) / HA) for h in range(HA)]
MASKED = -1e36
C_ID, C_DIST, C_MASK = 0, P, P + 3 * P
N_CONST = C_MASK + len(LEVELS) * P
G = 8


def shape_constants():
    c = np.zeros((P, N_CONST), np.float32)
    c[:, C_ID:C_ID + P] = np.eye(P)
    q, k = np.arange(P)[:, None], np.arange(S)[None, :]
    c[:, C_DIST:C_DIST + P] = np.where(k[:, :P] <= q, k[:, :P] - q, MASKED)
    c[:, C_DIST + P:C_DIST + 3 * P] = np.where(k <= q + P, k - q - P, MASKED)
    s, t = np.arange(P)[:, None], np.arange(P)[None, :]
    for n, w in enumerate(LEVELS):
        own = (s // (2 * w) == t // (2 * w)) & (s % (2 * w) < w) & (t % (2 * w) >= w)
        c[:, C_MASK + n * P:C_MASK + (n + 1) * P] = own
    return c


CHUNKS = [
    ("w_in", "cols", QG), ("w_in", "cols", QA), ("w_in", "cols", KA), ("w_in", "cols", VA),
    ("w_in", "cols", VG), ("w_in", "cols", RG),
    ("w_xkv", "cols", 0), ("w_xkv", "cols", 512), ("w_xkv", "cols", 1024),
    ("w_mix_o", "rows", 0), ("w_mix_o", "rows", 512),
    ("w_xkv", "cols", 1536),
    ("w_xq", "cols", 0), ("w_xq", "cols", 512),
    ("w_xo", "rows", 0), ("w_xo", "rows", 512),
]
N_FRONT = len(CHUNKS)
C_FF1_0, C_FF1_1, C_FF2_0, C_LOOP = N_FRONT, N_FRONT + 1, N_FRONT + 2, N_FRONT + 3
C_LAST = C_LOOP + 2 * (G - 2)
MEM_CHUNK = 6


def unit(chunk, half):
    return 1 + 2 * chunk + half + (chunk >= MEM_CHUNK)


MEM_UNIT = unit(MEM_CHUNK, 0) - 1
RAW = 4

FRONT_FILLS = (
    [("glr", 4), ("qg", 0), ("z", 5), ("kg", 1), ("qa0", 2), ("qa1", 3), ("ka0", 0), ("ka1", 1), ("va0", 2)]
    + [(f"score{h}", 4 + h) for h in range(4)] + [("va1", 3), ("vg0", 0)]
    + [(f"score{h}", h) for h in range(4, 8)] + [("vg1", 1)]
    + [(f"pt{h}", 4 + h) for h in range(4)] + [("rg0", 2)] + [(f"pt{h}", h) for h in range(4, 8)]
    + [("rg1", 3), ("pv0", 4), ("pv1", 5), ("diag", 6), ("xk0", 0), ("lv0r0", 4), ("lv0r1", 5), ("xk1", 1)]
    + [("lv1r0", 6), ("lv1r1", 7), ("lv2r0", 4), ("lv2r1", 5), ("xk2", 2), ("lv3r0", 6), ("lv3r1", 7),
       ("lv4r0", 4), ("lv4r1", 5), ("xk3", 3), ("lv5r0", 6), ("lv5r1", 7), ("lv6r0", 4), ("lv6r1", 5),
       ("xv00", 0), ("off0", 6), ("off1", 7), ("xv01", 1), ("av0", 4), ("av1", 5)]
    + [("mo00", 2), ("mo01", 3), ("mo10", 0), ("mo11", 1), ("gt0", 6), ("gt1", 7)]
    + [("xv10", 2), ("xt00", 4), ("xt01", 5), ("xv11", 3), ("xt10", 6), ("xt11", 7)]
    + [("xq0", 0), ("xq1", 1), ("cs0", 4), ("xq2", 2), ("cs1", 5), ("xq3", 3), ("cs2", 6), ("cpt0", 4), ("cs3", 7)]
    + [("cpv0", 4), ("cpt1", 5), ("cpv1", 5), ("cpt2", 6), ("cpv2", 6), ("cpt3", 7)]
    + [("xo00", 0), ("xo01", 1), ("cpv3", 7), ("xo10", 2), ("xo11", 3)]
    + [("yt00", 4), ("yt01", 5), ("yt10", 6), ("yt11", 7)]
)
FILL = {}
for _name, _bank in FRONT_FILLS:
    FILL[_name] = (_bank, sum(b == _bank for b, _ in FILL.values()))
CHUNK_END = {0: "kg", 1: "qa1", 2: "ka1", 3: "va1", 4: "vg1", 5: "rg1", 6: "xk1", 7: "xk3", 8: "xv01",
             10: "mo11", 11: "xv11", 12: "xq1", 13: "xq3", 15: "xo11"}
ROWS_END = {9: 1, 14: 2, C_FF2_0: 3}
FF_BASE = [sum(b == bank for b, _ in FILL.values()) for bank in range(8)]


def build(nc, x, xT, memT, w_in, w_gate_up, b_gate, gla_norm_g, w_mix_o, ln1_g, ln1_b, w_xq, w_xkv,
          w_xo, ln2_g, ln2_b, w_ff1, w_ff2, ln3_g, ln3_b, consts, out):
    f32, f32r, i32 = mybir.dt.float32, mybir.dt.float32r, mybir.dt.int32
    ALU, ACT, AX = mybir.AluOpType, mybir.ActivationFunctionType, mybir.AxisListType
    weights = {"w_in": w_in, "w_xkv": w_xkv, "w_mix_o": w_mix_o, "w_xq": w_xq, "w_xo": w_xo}
    ln_rows = [(ln1_g, ln1_b), (ln2_g, ln2_b), (ln3_g, ln3_b)]

    ctx = ExitStack()
    with ctx:
        def sb(name, shape, dt=f32):
            return ctx.enter_context(nc.sbuf_tensor(name, shape, dt))

        def sem(name):
            return ctx.enter_context(nc.semaphore(name))

        raw = sb("raw", [P, RAW, 2048])
        w_hi = sb("w_hi", [P, 2, 2, 2048], f32r)
        w_lo = sb("w_lo", [P, 2, 2, 2048], f32r)
        actA_hi = sb("actA_hi", [P, 8, S], f32r)
        actA_lo = sb("actA_lo", [P, 8, S], f32r)
        actB_hi = sb("actB_hi", [P, 8, S], f32r)
        actB_lo = sb("actB_lo", [P, 8, S], f32r)
        X = sb("X", [P, 2, D])
        const = sb("const", [P, N_CONST])
        probs = sb("probs", [P, HA * 384])
        probsT = sb("probsT", [P, HA * 384])
        qk = sb("qk", [P, 2048])
        values = sb("values", [P, 2048])
        gla = sb("gla", [P, 2560])
        att = sb("att", [P, 1536])
        reset = sb("reset", [P, 512])
        qkdiag = sb("qkdiag", [P, 512])
        wglr = sb("wglr", [P, 8, RANK])
        wgu = sb("wgu", [RANK, 256])
        glrT = sb("glrT", [RANK, S])
        bgate = sb("bgate", [P, 2])
        headsel = sb("headsel", [P, 2])
        gnorm = sb("gnorm", [P, DV])
        negmax = sb("negmax", [P, 2 * HA])
        sums = sb("sums", [P, 2 * HA])
        rsums = sb("rsums", [P, 2 * HA])
        diag = sb("diag", [P, 8])
        ssq = sb("ssq", [P, 8])
        meansq = sb("meansq", [P, 8])
        rms = sb("rms", [P, 8])
        minus_half = sb("minus_half", [P, 8])
        stats = sb("stats", [P, 3, 2, 2, 6])
        mv = sb("mv", [P, 3, 2, 2])
        vareps = sb("vareps", [P, 3, 2, 1])
        rstd = sb("rstd", [P, 3, 2, 1])
        cmax = sb("cmax", [P, 2 * HX])
        cneg = sb("cneg", [P, 2 * HX])
        csum = sb("csum", [P, 2 * HX])
        crec = sb("crec", [P, 2 * HX])

        ident = const[:, C_ID:C_ID + P]
        qaT = qk[:, 0:1024].rearrange("p (m s) -> p m s", m=4)
        kaT = qk[:, 1024:2048].rearrange("p (m s) -> p m s", m=4)
        expo = [qk[:, 512 * b:512 * b + 512] for b in range(2)]
        lev = [qk[:, 1024 + 512 * b:1536 + 512 * b] for b in range(2)]
        va = values[:, 0:1024].rearrange("p (t n) -> p t n", t=2)
        vg = values[:, 1024:2048].rearrange("p (t n) -> p t n", t=2)
        sg = gla[:, 0:1024].rearrange("p (t n) -> p t n", t=2)
        qgT, kgT, cum = gla[:, 1024:1536], gla[:, 1536:2048], gla[:, 2048:2560]
        attT = att[:, 0:1024].rearrange("p (t h s) -> p t h s", t=2, h=HG)
        attT_r = att[:, 0:1024].rearrange("p (a r s) -> p a r s", a=4, r=2)
        attoff = att[:, 1024:1536].rearrange("p (h s) -> p h s", h=HG)
        zlin, zabs = att[:, 0:512], att[:, 512:1024]
        memkT = probs[:, 0:2048].rearrange("p (m s) -> p m s", m=8)
        lng = probs[:, 2048:3072]
        memv = probsT[:, 0:2048].rearrange("p (t n) -> p t n", t=2)
        lnb = probsT[:, 2048:3072]
        cqT = values[:, :].rearrange("p (m s) -> p m s", m=8)
        cprobs = qk[:, :].rearrange("p (h t m) -> p h t m", h=HX, t=2)
        cprobsT = gla[:, 0:2048].rearrange("p (h m s) -> p h m s", h=HX, m=2)
        relu = att[:, 0:1024].rearrange("p (b n) -> p b n", b=2)

        def level_mask(n):
            return const[:, C_MASK + n * P:C_MASK + (n + 1) * P].bitcast(i32)

        bank = [ctx.enter_context(nc.psum_tensor(f"bank{b}", [P, 512], f32)) for b in range(8)]

        bank_full = [sem(f"bank_full{b}") for b in range(8)]
        bank_free = [sem(f"bank_free{b}") for b in range(8)]
        raw_in = [sem(f"raw_in{r}") for r in range(RAW)]
        hi_done = sem("hi_done")
        lo_done = sem("lo_done")
        rows_used = sem("rows_used")
        wglr_in, wgu_in, const_in, small_in, x_in = map(sem, ("wglr_in", "wgu_in", "const_in", "small_in", "x_in"))
        ln_in = [sem(f"ln_in{n}") for n in range(3)]
        out_done = sem("out_done")
        dve_link, act_link, pool_link = sem("dve_link"), sem("act_link"), sem("pool_link")
        zabs_done, softplus_done, cum_done = map(sem, ("zabs_done", "softplus_done", "cum_done"))
        reset_done, att_zeroed, headsel_done, half_done = map(sem, ("reset_done", "att_zeroed", "headsel_done", "half_done"))
        bias_done, score_done, exp_done, prob_done = map(sem, ("bias_done", "score_done", "exp_done", "prob_done"))
        mix_hi = sem("mix_hi")
        expr_done, gate_done = sem("expr_done"), sem("gate_done")
        expo_done, decay_done, lev_done, qkdiag_done = map(sem, ("expo_done", "decay_done", "lev_done", "qkdiag_done"))
        ssq_done, meansq_done, rms_done, glao_done = map(sem, ("ssq_done", "meansq_done", "rms_done", "glao_done"))
        var_done, rstd_done, ln_done = map(sem, ("var_done", "rstd_done", "ln_done"))
        xT_hi = sem("xT_hi")
        cneg_done, cexp_done, cprob_done = map(sem, ("cneg_done", "cexp_done", "cprob_done"))
        cross_hi = sem("cross_hi")
        sq_done, hid_hi, hid_lo = map(sem, ("sq_done", "hid_hi", "hid_lo"))

        def wait_full(eng, name):
            b, before = FILL[name]
            eng.wait_ge(bank_full[b], before + 1)
            return bank[b]

        def freed(name):
            return bank_free[FILL[name][0]]

        def wait_out(eng, name):
            b, before = FILL[name]
            eng.wait_ge(bank_free[b], before + 1)

        def half_view(u):
            return raw[:, u % RAW, :]

        block = ctx.enter_context(nc.Block())

        @block.sync
        def _(sp):
            def chunk_source(c, half):
                name, kind, at = CHUNKS[c]
                w = weights[name]
                if kind == "cols":
                    return w[half * 512:(half + 1) * 512, at:at + 512].rearrange("(a p) n -> p a n", p=P)
                return w[at + half * 256:at + (half + 1) * 256, :].rearrange("(a p) n -> p a n", p=P)

            def load(u, src, tiles):
                if u >= RAW:
                    sp.wait_ge(lo_done, u - RAW + 1)
                if u == RAW:
                    sp.wait_ge(bank_full[FILL["glr"][0]], 1)
                sp.dma_start(half_view(u).rearrange("p (a n) -> p a n", a=tiles), src).then_inc(raw_in[u % RAW], 16)

            def load_chunk(c):
                for half in range(2):
                    load(unit(c, half), chunk_source(c, half), 4 if CHUNKS[c][1] == "cols" else 2)

            def load_ln(n):
                g, b = ln_rows[n]
                sp.dma_start(lng, g.partition_broadcast(P)).then_inc(ln_in[n], 16)
                sp.dma_start(lnb, b.partition_broadcast(P)).then_inc(ln_in[n], 16)

            load(0, xT.rearrange("(a p) s -> p a s", p=P), 8)
            sp.dma_start(wglr[:], w_in[:, GL:GL + RANK].rearrange("(a p) n -> p a n", p=P)).then_inc(wglr_in, 16)
            sp.dma_start(wgu[:], w_gate_up).then_inc(wgu_in, 16)
            sp.dma_start(bgate[:], b_gate).then_inc(small_in, 16)
            sp.dma_start(gnorm[:], gla_norm_g.partition_broadcast(P)).then_inc(small_in, 16)
            load_chunk(0)
            sp.dma_start(const[:], consts).then_inc(const_in, 16)
            for c in range(1, 6):
                load_chunk(c)
            load(MEM_UNIT, memT.rearrange("(a p) s -> p a s", p=P), 8)
            load_chunk(6)
            sp.dma_start(X[:], x.rearrange("(t p) n -> p t n", p=P)).then_inc(x_in, 16)
            load_chunk(7)
            load_chunk(8)
            load_chunk(9)
            load_chunk(10)
            sp.wait_ge(bank_full[FILL["pv1"][0]], FILL["pv1"][1] + 1)
            load_ln(0)
            for c in range(11, N_FRONT):
                load_chunk(c)
            ff1_src = [w_ff1[half * 512:(half + 1) * 512, :].rearrange("(a p) n -> p a n", p=P) for half in range(2)]

            def load_ff1(u, g):
                sp.dma_start(raw[:, u % RAW, :].rearrange("p (a n) -> p a n", a=4),
                             ff1_src[u % 2][:, :, bass.ds(g * 512, 512)]).then_inc(raw_in[u % RAW], 16)

            def load_ff2(u, g):
                sp.dma_start(raw[:, u % RAW, :].rearrange("p (a n) -> p a n", a=2),
                             w_ff2[bass.ds(g * 512 + (u % 2) * 256, 256), :].rearrange("(a p) n -> p a n", p=P))\
                    .then_inc(raw_in[u % RAW], 16)

            for c, source, g in ((C_FF1_0, load_ff1, 0), (C_FF1_1, load_ff1, 1), (C_FF2_0, load_ff2, 0)):
                for half in range(2):
                    u = unit(c, half)
                    sp.wait_ge(lo_done, u - RAW + 1)
                    source(u, g)
                if c == C_FF1_0:
                    sp.wait_ge(ln_done, 4)
                    load_ln(1)
            u0 = unit(C_LOOP, 0)
            with sp.Fori(0, G // 2 - 1) as i:
                for n in range(4):
                    for half in range(2):
                        k = 2 * n + half
                        sp.wait_ge(lo_done, i * 8 + (u0 + k - RAW + 1))
                        if n % 2 == 0:
                            load_ff1(u0 + k, i * 2 + 2 + n // 2)
                        else:
                            load_ff2(u0 + k, i * 2 + 1 + n // 2)
            for half in range(2):
                u = unit(C_LAST, half)
                sp.wait_ge(lo_done, u - RAW + 1)
                load_ff2(u, G - 1)
            sp.wait_ge(ln_done, 8)
            load_ln(2)
            for t in range(2):
                for n in range(2):
                    sp.wait_ge(ln_done, 8 + 2 * t + n + 1)
                    sp.dma_start(out[t * P:(t + 1) * P, n * 512:(n + 1) * 512],
                                 X[:, t, n * 512:(n + 1) * 512]).then_inc(out_done, 16)
            sp.wait_ge(out_done, 64)

        @block.gpsimd
        def _(pool):
            pool.memset(minus_half[:], -0.5).then_inc(half_done, 1)
            pool.memset(headsel[:], 0.0).then_inc(pool_link, 1)
            pool.memset(reset[:], 1.0).then_inc(pool_link, 1)
            pool.wait_ge(pool_link, 2)
            pool.memset(headsel[0:64, 0:1], 1.0).then_inc(headsel_done, 1)
            pool.wait_ge(headsel_done, 1)
            pool.memset(headsel[64:128, 1:2], 1.0).then_inc(headsel_done, 1)
            pool.wait_ge(headsel_done, 2)
            pool.memset(reset[:, :].rearrange("p (c s) -> p c s", s=CHUNK)[:, :, 0:1], 0.0).then_inc(reset_done, 1)
            pool.wait_ge(const_in, 16)
            for h in range(HA):
                pool.tensor_scalar(probsT[:, h * 384:(h + 1) * 384], const[:, C_DIST:C_DIST + 384],
                                   SLOPES[h] * DA ** 0.5, None, ALU.mult).then_inc(bias_done, 1)
            wait_out(pool, "qg")
            wait_out(pool, "kg")
            pool.tensor_tensor(qkdiag[:], qgT, kgT, ALU.mult).then_inc(qkdiag_done, 1)
            pool.wait_ge(cum_done, 1)
            pool.memset(att[:, 0:1024], 0.0).then_inc(att_zeroed, 1)
            pool.wait_ge(small_in, 32)
            for t in range(2):
                wait_out(pool, f"rg{t}")
                v = sg[:, t, :].rearrange("p (h n) -> p h n", h=HG)
                pool.tensor_tensor(v, v, gnorm[:, :].unsqueeze(1).to_broadcast([P, HG, DV]), ALU.mult)\
                    .then_inc(gate_done, 1)
            for n in range(len(LEVELS) + 1):
                w = LEVELS[n] if n < len(LEVELS) else P
                e = expo[n % 2].rearrange("p (b c w) -> p b c w", c=2, w=w)
                o = lev[n % 2].rearrange("p (b c w) -> p b c w", c=2, w=w)
                pool.wait_ge(decay_done, n + 1)
                if n >= 2:
                    b, before = FILL[f"lv{n - 2}r1"]
                    pool.wait_ge(bank_full[b], before + 1)
                if n < 2:
                    pool.wait_ge(bank_full[FILL["score7"][0]], FILL["score7"][1] + 1)
                for c, src in ((0, kgT), (1, qgT)):
                    pool.tensor_tensor(o[:, :, c, :], src.rearrange("p (b c w) -> p b c w", c=2, w=w)[:, :, c, :],
                                       e[:, :, c, :], ALU.mult).then_inc(lev_done, 1)
            pool.wait_ge(half_done, 1)
            for t in range(2):
                pool.wait_ge(meansq_done, t + 1)
                pool.tensor_tensor(rms[:, 4 * t:4 * t + 4], meansq[:, 4 * t:4 * t + 4], minus_half[:, 0:4], ALU.pow)\
                    .then_inc(rms_done, 1)
            for n in range(3):
                for t in range(2):
                    pool.wait_ge(var_done, 2 * n + t + 1)
                    pool.tensor_tensor(rstd[:, n, t, :], vareps[:, n, t, :], minus_half[:, 0:1], ALU.pow)\
                        .then_inc(rstd_done, 1)

        @block.scalar
        def _(act):
            def hi(u, dst, chunk=None):
                act.wait_ge(raw_in[u % RAW], 16 * (u // RAW + 1))
                if chunk is not None and chunk >= 2:
                    before = chunk - 2
                    if before in ROWS_END:
                        act.wait_ge(rows_used, ROWS_END[before])
                    elif before in CHUNK_END:
                        wait_full(act, CHUNK_END[before])
                    else:
                        b = 2 * (before - C_FF1_0) + 1
                        act.wait_ge(bank_full[b], FF_BASE[b] + 1)
                act.copy(dst, half_view(u)).then_inc(hi_done, 1)

            def hi_half(c, half):
                hi(unit(c, half), w_hi[:, c % 2, half, :], c)

            def evacuate(name, dst, scale=None):
                b = wait_full(act, name)
                if scale is None:
                    return act.copy(dst, b[:, :]).then_inc(freed(name), 1)
                return act.mul(dst, b[:, :], scale).then_inc(freed(name), 1)

            hi(0, actA_hi[:].rearrange("p a s -> p (a s)"))
            hi_half(0, 0)
            act.wait_ge(bank_full[FILL["glr"][0]], 1)
            act.copy(glrT[:], bank[4][0:RANK, 0:S]).then_inc(freed("glr"), 1)
            hi_half(0, 1)
            hi_half(1, 0)
            evacuate("qg", qgT, DK ** -0.5)
            hi_half(1, 1)
            act.wait_ge(zabs_done, 1)
            act.activation(zabs, zabs, ACT.Exp, scale=-1.0).then_inc(act_link, 1)
            act.wait_ge(act_link, 1)
            act.activation(zabs, zabs, ACT.Ln, bias=1.0).then_inc(softplus_done, 1)
            evacuate("kg", kgT)
            for n in range(2):
                hi_half(2, n)
                evacuate(f"qa{n}", qaT[:, 2 * n:2 * n + 2, :].rearrange("p m s -> p (m s)"))
            for n in range(2):
                hi_half(3, n)
                evacuate(f"ka{n}", kaT[:, 2 * n:2 * n + 2, :].rearrange("p m s -> p (m s)"))

            def exps(h):
                for t, (a, b) in enumerate(((0, P), (P, 3 * P))):
                    if t == 0:
                        act.wait_ge(score_done, h + 1)
                    else:
                        wait_out(act, f"score{h}")
                    v = probs[:, h * 384 + a:h * 384 + b]
                    act.activation(v, v, ACT.Exp, bias=negmax[:, 2 * h + t:2 * h + t + 1], scale=-1.0,
                                   accum_out=sums[:, 2 * h + t:2 * h + t + 1]).then_inc(exp_done, 1)

            def transposed(h):
                b = wait_full(act, f"pt{h}")
                act.copy(probsT[:, h * 384:(h + 1) * 384], b[:, 0:384]).then_inc(freed(f"pt{h}"), 1)

            hi_half(4, 0)
            evacuate("va0", va[:, 0, :])
            exps(0)
            exps(1)
            hi_half(4, 1)
            exps(2)
            exps(3)
            evacuate("va1", va[:, 1, :])
            hi_half(5, 0)
            evacuate("vg0", vg[:, 0, :])
            exps(4)
            exps(5)
            hi_half(5, 1)
            exps(6)
            exps(7)
            evacuate("vg1", vg[:, 1, :])
            for h in range(4):
                transposed(h)
            act.wait_ge(raw_in[MEM_UNIT % RAW], 16 * (MEM_UNIT // RAW + 1))
            hi(MEM_UNIT, actB_hi[:].rearrange("p a s -> p (a s)"))
            hi_half(6, 0)

            def exp_r(t):
                b = wait_full(act, f"rg{t}")
                act.activation(sg[:, t, :], b[:, :], ACT.Exp, scale=-1.0).then_inc(expr_done, 1)

            exp_r(0)
            for h in range(4, 8):
                transposed(h)
            hi_half(6, 1)
            exp_r(1)

            def mix(n, name):
                b = wait_full(act, name)
                if name.startswith("pv"):
                    dst = actA_hi[:, 2 * n:2 * n + 2, :]
                else:
                    dst = actA_hi[:, 4:8, (n - 2) * P:(n - 1) * P]
                act.copy(dst, b[:, :].rearrange("p (m s) -> p m s", m=dst.shape[1])).then_inc(mix_hi, 1)

            mix(0, "pv0")
            mix(1, "pv1")
            b = wait_full(act, "diag")
            act.copy(diag[:], b[:, 0:8]).then_inc(freed("diag"), 1)

            def decay(n):
                act.wait_ge(expo_done, n + 1)
                act.activation(expo[n % 2], expo[n % 2], ACT.Exp, scale=1.0 / GATE_TEMP).then_inc(decay_done, 1)

            def memk(n):
                evacuate(f"xk{n}", memkT[:, 2 * n:2 * n + 2, :].rearrange("p m s -> p (m s)"))

            decay(0)
            hi_half(7, 0)
            decay(1)
            memk(0)
            decay(2)
            hi_half(7, 1)
            memk(1)
            decay(3)
            hi_half(8, 0)
            decay(4)
            memk(2)
            decay(5)
            hi_half(8, 1)
            memk(3)
            decay(6)
            decay(7)
            hi_half(9, 0)
            evacuate("xv00", memv[:, 0, 0:512])
            for r in range(2):
                b = wait_full(act, f"off{r}")
                act.copy(attoff.rearrange("p (f r) s -> p f r s", r=2)[:, :, r, :],
                         b[:, 0:S].rearrange("p (f s) -> p f s", f=2)).then_inc(freed(f"off{r}"), 1)
            hi_half(9, 1)
            evacuate("xv01", memv[:, 1, 0:512])
            for t in range(2):
                wait_out(act, f"av{t}")
                for h in range(HG):
                    act.activation(qk[:, 128 * (4 * t + h):128 * (4 * t + h + 1)], vg[:, t, h * DV:(h + 1) * DV],
                                   ACT.Square, accum_out=ssq[:, 4 * t + h:4 * t + h + 1]).then_inc(ssq_done, 1)
                hi_half(10, t)
            hi_half(11, 0)
            mix(2, "gt0")
            mix(3, "gt1")
            hi_half(11, 1)
            evacuate("xv10", memv[:, 0, 512:1024])

            def xpose(n, name):
                t, c = divmod(n % 4, 2)
                b = wait_full(act, name)
                act.copy(actA_hi[:, 4 * c:4 * c + 4, t * P:(t + 1) * P],
                         b[:, :].rearrange("p (m s) -> p m s", m=4)).then_inc(xT_hi, 1)

            hi_half(12, 0)
            xpose(0, "xt00")
            xpose(1, "xt01")
            hi_half(12, 1)
            xpose(2, "xt10")
            xpose(3, "xt11")
            evacuate("xv11", memv[:, 1, 512:1024])

            def cq(h):
                evacuate(f"xq{h}", cqT[:, 2 * h:2 * h + 2, :].rearrange("p m s -> p (m s)"))

            def cexps(h):
                act.wait_ge(cneg_done, h + 1)
                b = wait_full(act, f"cs{h}")
                for t in range(2):
                    i = act.activation(cprobs[:, h, t, :], b[:, t * S:(t + 1) * S], ACT.Exp,
                                       bias=cneg[:, 2 * h + t:2 * h + t + 1], scale=DX ** -0.5,
                                       accum_out=csum[:, 2 * h + t:2 * h + t + 1])
                    i.then_inc(cexp_done if t == 0 else freed(f"cs{h}"), 1)

            def cT(h):
                evacuate(f"cpt{h}", cprobsT[:, h, :, :].rearrange("p m s -> p (m s)"))

            def cross(h):
                b = wait_full(act, f"cpv{h}")
                act.copy(actB_hi[:, 2 * h:2 * h + 2, :], b[:, :].rearrange("p (m s) -> p m s", m=2)).then_inc(cross_hi, 1)

            hi_half(13, 0)
            cq(0)
            hi_half(13, 1)
            cq(1)
            cexps(0)
            hi_half(14, 0)
            cq(2)
            cexps(1)
            hi_half(14, 1)
            cq(3)
            cexps(2)
            cT(0)
            cexps(3)
            cT(1)
            cross(0)
            cT(2)
            cross(1)
            hi_half(15, 0)
            cT(3)
            cross(2)
            hi_half(15, 1)
            cross(3)
            hi_half(C_FF1_0, 0)
            hi_half(C_FF1_0, 1)
            hi_half(C_FF1_1, 0)
            for n, name in enumerate(("yt00", "yt01", "yt10", "yt11")):
                xpose(4 + n, name)

            def relus(g2, f, use):
                b = 2 * g2 + f
                act.wait_ge(bank_full[b], use)
                act.activation(relu[:, f, :], bank[b][:, :], ACT.Relu).then_inc(bank_free[b], 1)

            def hid(g2, f, n):
                act.wait_ge(sq_done, n)
                act.copy(actB_hi[:, 4 * g2 + 2 * f:4 * g2 + 2 * f + 2, :],
                         relu[:, f, :].rearrange("p (m s) -> p m s", m=2)).then_inc(hid_hi, 1)

            def hi_loop(k, half, i):
                u = unit(C_LOOP + k, half)
                act.wait_ge(raw_in[u % RAW], i * 32 + 16 * (u // RAW + 1))
                if k % 2:
                    act.wait_ge(rows_used, i * 2 + (3 + k // 2))
                else:
                    act.wait_ge(bank_full[2 * (k // 2) - 1], i + (FF_BASE[2 * (k // 2) - 1] + 2))
                act.copy(w_hi[:, (C_LOOP + k) % 2, half, :], raw[:, u % RAW, :]).then_inc(hi_done, 1)

            for g in range(2):
                if g == 0:
                    hi_half(C_FF1_1, 1)
                if g == 1:
                    act.wait_ge(hid_lo, 1)
                relus(g, 0, FF_BASE[2 * g] + 1)
                if g == 1:
                    hi_half(C_FF2_0, 1)
                hid(g, 0, 2 * g + 1)
                if g == 1:
                    act.wait_ge(hid_lo, 2)
                relus(g, 1, FF_BASE[2 * g + 1] + 1)
                hi_half(C_FF2_0 + g, 0)
                hid(g, 1, 2 * g + 2)
            hi_half(C_LOOP, 1)
            with act.Fori(0, G // 2 - 1) as i:
                for g in range(2):
                    n = 4 + 2 * g
                    hi_loop(2 * g + 1, 0, i)
                    act.wait_ge(hid_lo, i * 4 + (n - 1))
                    relus(g, 0, i + (FF_BASE[2 * g] + 2))
                    hi_loop(2 * g + 1, 1, i)
                    hid(g, 0, i * 4 + (n + 1))
                    act.wait_ge(hid_lo, i * 4 + n)
                    relus(g, 1, i + (FF_BASE[2 * g + 1] + 2))
                    hi_loop(2 * g + 2, 0, i)
                    hid(g, 1, i * 4 + (n + 2))
                    hi_loop(2 * g + 2, 1, i)

        @block.vector
        def _(dve):
            chain = [0]

            def link(ins):
                chain[0] += 1
                ins.then_inc(dve_link, 1)
                dve.wait_ge(dve_link, chain[0])

            def lo(u, dst, hi_part):
                dve.wait_ge(hi_done, u + 1)
                dve.tensor_tensor(dst, half_view(u), hi_part.bitcast(f32), ALU.subtract).then_inc(lo_done, 1)

            def lo_half(c, half):
                lo(unit(c, half), w_lo[:, c % 2, half, :], w_hi[:, c % 2, half, :])

            flat = "p a s -> p (a s)"
            lo(0, actA_lo[:].rearrange(flat), actA_hi[:].rearrange(flat))
            lo_half(0, 0)
            lo_half(0, 1)
            dve.wait_ge(small_in, 32)
            b = wait_full(dve, "z")
            for f in range(2):
                i = dve.tensor_scalar(zlin[:, f * S:(f + 1) * S], b[:, f * S:(f + 1) * S], bgate[:, f:f + 1], None, ALU.add)
                i.then_inc(freed("z") if f == 1 else dve_link, 1)
            chain[0] += 1
            dve.wait_ge(dve_link, chain[0])
            wait_out(dve, "z")
            dve.scalar_tensor_tensor(zabs, zlin, -1.0, zlin, ALU.mult, ALU.max).then_inc(zabs_done, 1)
            lo_half(1, 0)
            dve.wait_ge(softplus_done, 1)
            link(dve.scalar_tensor_tensor(zlin, zlin, 0.0, zabs, ALU.min, ALU.subtract))
            dve.wait_ge(reset_done, 1)
            dve.tensor_tensor_scan(cum, reset[:], zlin, 0.0, ALU.mult, ALU.add).then_inc(cum_done, 1)
            lo_half(1, 1)
            lo_half(2, 0)
            lo_half(2, 1)
            lo_half(3, 0)
            lo_half(3, 1)

            def score(h):
                b = wait_full(dve, f"score{h}")
                dve.wait_ge(bias_done, h + 1)
                for t, (a, e) in enumerate(((0, P), (P, 3 * P))):
                    i = dve.tensor_tensor_reduce(
                        out=probs[:, h * 384 + a:h * 384 + e], in0=b[:, a:e],
                        in1=probsT[:, h * 384 + a:h * 384 + e], scale=-DA ** -0.5, scalar=3e38,
                        op0=ALU.add, op1=ALU.min, accum_out=negmax[:, 2 * h + t:2 * h + t + 1])
                    i.then_inc(score_done if t == 0 else freed(f"score{h}"), 1)

            def norm(h):
                dve.wait_ge(exp_done, 2 * h + 2)
                link(dve.reciprocal(rsums[:, 2 * h:2 * h + 2], sums[:, 2 * h:2 * h + 2]))
                for t, (a, e) in enumerate(((0, P), (P, 3 * P))):
                    v = probs[:, h * 384 + a:h * 384 + e]
                    dve.tensor_scalar(v, v, rsums[:, 2 * h + t:2 * h + t + 1], None, ALU.mult).then_inc(prob_done, 1)

            lo_half(4, 0)
            for h in range(4):
                score(h)
            norm(0)
            norm(1)
            lo_half(4, 1)
            norm(2)
            norm(3)
            lo_half(5, 0)
            for h in range(4, 8):
                score(h)
            norm(4)
            norm(5)
            lo_half(5, 1)
            norm(6)
            norm(7)

            def exponents(n):
                e, c4 = expo[n % 2], cum
                if n >= 2:
                    dve.wait_ge(lev_done, 2 * n - 2)
                else:
                    dve.wait_ge(bank_full[FILL["score7"][0]], FILL["score7"][1] + 1)
                if n < len(LEVELS) and LEVELS[n] < CHUNK:
                    w = LEVELS[n]
                    ev = e.rearrange("p (b c w) -> p b c w", c=2, w=w)
                    cv = c4.rearrange("p (b c w) -> p b c w", c=2, w=w)
                    mid = cv[:, :, 0, w - 1:w].to_broadcast([P, 512 // (2 * w), w])
                    link(dve.tensor_tensor(ev[:, :, 0, :], mid, cv[:, :, 0, :], ALU.subtract))
                    dve.tensor_tensor(ev[:, :, 1, :], cv[:, :, 1, :], mid, ALU.subtract).then_inc(expo_done, 1)
                    return
                ev = e.rearrange("p (f c w) -> p f c w", f=2, c=4)
                cv = c4.rearrange("p (f c w) -> p f c w", f=2, c=4)

                def last(c):
                    return cv[:, :, c, CHUNK - 1:CHUNK].to_broadcast([P, 2, CHUNK])

                if n < len(LEVELS):
                    for c in (0, 2):
                        link(dve.tensor_tensor(ev[:, :, c, :], last(c), cv[:, :, c, :], ALU.subtract))
                    link(dve.tensor_copy(ev[:, :, 1, :], cv[:, :, 1, :]))
                    dve.tensor_copy(ev[:, :, 3, :], cv[:, :, 3, :]).then_inc(expo_done, 1)
                else:
                    link(dve.tensor_tensor(ev[:, :, 0, :], last(0), cv[:, :, 0, :], ALU.subtract))
                    link(dve.tensor_tensor(ev[:, :, 0, :], ev[:, :, 0, :], last(1), ALU.add))
                    link(dve.tensor_tensor(ev[:, :, 1, :], last(1), cv[:, :, 1, :], ALU.subtract))
                    link(dve.tensor_copy(ev[:, :, 2, :], cv[:, :, 2, :]))
                    dve.tensor_tensor(ev[:, :, 3, :], cv[:, :, 3, :], last(2), ALU.add).then_inc(expo_done, 1)

            def masked(n):
                for r in range(2):
                    name = f"lv{n}r{r}"
                    b = wait_full(dve, name)
                    if n == 0:
                        dve.wait_ge(att_zeroed, 1)
                    else:
                        wait_out(dve, f"lv{n - 1}r{r}")
                    dve.copy_predicated(attT_r[:, :, r, :], level_mask(n).unsqueeze(1).to_broadcast([P, 4, P]),
                                        b[:, :].rearrange("p (a s) -> p a s", a=4))\
                        .then_inc(freed(name), 1)

            def silu(t):
                dve.wait_ge(expr_done, t + 1)
                v = sg[:, t, :]
                link(dve.tensor_scalar(v, v, 1.0, None, ALU.add))
                link(dve.reciprocal(v, v))
                b = wait_full(dve, f"rg{t}")
                dve.tensor_tensor(v, v, b[:, :], ALU.mult).then_inc(freed(f"rg{t}"), 1)

            def mix(n, name):
                b = wait_full(dve, name)
                dve.wait_ge(mix_hi, n + 1)
                sl = (slice(None), slice(2 * n, 2 * n + 2), slice(None)) if n < 2 else \
                    (slice(None), slice(4, 8), slice((n - 2) * P, (n - 1) * P))
                hi_part = actA_hi[sl]
                dve.tensor_tensor(actA_lo[sl], b[:, :].rearrange("p (m s) -> p m s", m=hi_part.shape[1]),
                                  hi_part.bitcast(f32), ALU.subtract).then_inc(freed(name), 1)

            lo(MEM_UNIT, actB_lo[:].rearrange(flat), actB_hi[:].rearrange(flat))
            exponents(0)
            lo_half(6, 0)
            silu(0)
            exponents(1)
            lo_half(6, 1)
            silu(1)
            mix(0, "pv0")
            mix(1, "pv1")
            lo_half(7, 0)
            exponents(2)
            masked(0)
            lo_half(7, 1)
            exponents(3)
            masked(1)
            exponents(4)
            masked(2)
            lo_half(8, 0)
            exponents(5)
            masked(3)
            exponents(6)
            masked(4)
            lo_half(8, 1)
            exponents(7)
            masked(5)
            masked(6)
            lo_half(9, 0)
            lo_half(9, 1)

            wait_out(dve, "diag")
            b1 = FILL["av1"]
            dve.wait_ge(bank_full[b1[0]], b1[1] + 1)
            for t in range(2):
                b = bank[FILL[f"av{t}"][0]]
                for h in range(HG):
                    v = vg[:, t, h * DV:(h + 1) * DV]
                    k = 4 * t + 2 * (h // 2) + h % 2
                    i = dve.scalar_tensor_tensor(v, v, diag[:, k:k + 1], b[:, h * DV:(h + 1) * DV], ALU.mult, ALU.add)
                    i.then_inc(dve_link if h < HG - 1 else freed(f"av{t}"), 1)
                chain[0] += HG - 1
            for t in range(2):
                dve.wait_ge(ssq_done, 4 * t + 4)
                dve.wait_ge(dve_link, chain[0])
                dve.tensor_scalar(meansq[:, 4 * t:4 * t + 4], ssq[:, 4 * t:4 * t + 4], 1.0 / DV, RMS_EPS,
                                  ALU.mult, ALU.add).then_inc(meansq_done, 1)
                lo_half(10, t)
            for t in range(2):
                dve.wait_ge(rms_done, t + 1)
                dve.wait_ge(gate_done, t + 1)
                for h in range(HG):
                    v = vg[:, t, h * DV:(h + 1) * DV]
                    dve.scalar_tensor_tensor(v, v, rms[:, 4 * t + h:4 * t + h + 1], sg[:, t, h * DV:(h + 1) * DV],
                                             ALU.mult, ALU.mult).then_inc(glao_done, 1)
            lo_half(11, 0)
            mix(2, "gt0")
            mix(3, "gt1")
            lo_half(11, 1)

            def layer_norm(n, t, banks):
                for c in range(2):
                    v = X[:, t, c * 512:(c + 1) * 512]
                    b, full, free = banks[c]
                    dve.wait_ge(full[0], full[1])
                    dve.scalar_tensor_tensor(v, v, ALPHA, b[:, :], ALU.mult, ALU.add).then_inc(free, 1)
                    dve.wait_ge(free, full[1])
                    link(dve.bn_stats(stats[:, n, t, c, :], v))
                link(dve.bn_aggr(mv[:, n, t, :], stats[:, n, t, :, :].rearrange("p c k -> p (c k)")))
                dve.tensor_scalar(vareps[:, n, t, :], mv[:, n, t, 1:2], LN_EPS, None, ALU.add).then_inc(var_done, 1)
                dve.wait_ge(ln_in[n], 32)
                for c in range(2):
                    v = X[:, t, c * 512:(c + 1) * 512]
                    link(dve.scalar_tensor_tensor(v, v, mv[:, n, t, 0:1], lng[:, c * 512:(c + 1) * 512],
                                                  ALU.subtract, ALU.mult))
                dve.wait_ge(rstd_done, 2 * n + t + 1)
                for c in range(2):
                    v = X[:, t, c * 512:(c + 1) * 512]
                    dve.scalar_tensor_tensor(v, v, rstd[:, n, t, :], lnb[:, c * 512:(c + 1) * 512],
                                             ALU.mult, ALU.add).then_inc(ln_done, 1)

            def front_banks(t, name):
                return [(bank[FILL[f"{name}{t}{c}"][0]],
                         (bank_full[FILL[f"{name}{t}{c}"][0]], FILL[f"{name}{t}{c}"][1] + 1),
                         freed(f"{name}{t}{c}")) for c in range(2)]

            def xpose(n, name):
                t, c = divmod(n % 4, 2)
                b = wait_full(dve, name)
                dve.wait_ge(xT_hi, n + 1)
                sl = (slice(None), slice(4 * c, 4 * c + 4), slice(t * P, (t + 1) * P))
                dve.tensor_tensor(actA_lo[sl], b[:, :].rearrange("p (m s) -> p m s", m=4),
                                  actA_hi[sl].bitcast(f32), ALU.subtract).then_inc(freed(name), 1)

            dve.wait_ge(x_in, 16)
            layer_norm(0, 0, front_banks(0, "mo"))
            layer_norm(0, 1, front_banks(1, "mo"))
            xpose(0, "xt00")
            xpose(1, "xt01")
            lo_half(12, 0)
            xpose(2, "xt10")
            xpose(3, "xt11")
            lo_half(12, 1)

            def cmaxes(h):
                b = wait_full(dve, f"cs{h}")
                link(dve.tensor_reduce(cmax[:, 2 * h:2 * h + 2], b[:, :].rearrange("p (t m) -> p t m", t=2),
                                       AX.X, ALU.max))
                dve.tensor_scalar(cneg[:, 2 * h:2 * h + 2], cmax[:, 2 * h:2 * h + 2], -DX ** -0.5, None, ALU.mult)\
                    .then_inc(cneg_done, 1)

            def cnorm(h):
                dve.wait_ge(cexp_done, h + 1)
                wait_out(dve, f"cs{h}")
                link(dve.reciprocal(crec[:, 2 * h:2 * h + 2], csum[:, 2 * h:2 * h + 2]))
                for t in range(2):
                    v = cprobs[:, h, t, :]
                    dve.tensor_scalar(v, v, crec[:, 2 * h + t:2 * h + t + 1], None, ALU.mult).then_inc(cprob_done, 1)

            def cross(h):
                b = wait_full(dve, f"cpv{h}")
                dve.wait_ge(cross_hi, h + 1)
                dve.tensor_tensor(actB_lo[:, 2 * h:2 * h + 2, :], b[:, :].rearrange("p (m s) -> p m s", m=2),
                                  actB_hi[:, 2 * h:2 * h + 2, :].bitcast(f32), ALU.subtract)\
                    .then_inc(freed(f"cpv{h}"), 1)

            lo_half(13, 0)
            lo_half(13, 1)
            cmaxes(0)
            cnorm(0)
            lo_half(14, 0)
            cmaxes(1)
            cnorm(1)
            lo_half(14, 1)
            cmaxes(2)
            cnorm(2)
            cmaxes(3)
            cnorm(3)
            cross(0)
            cross(1)
            lo_half(15, 0)
            cross(2)
            lo_half(15, 1)
            cross(3)
            lo_half(C_FF1_0, 0)
            lo_half(C_FF1_0, 1)
            layer_norm(1, 0, front_banks(0, "xo"))
            layer_norm(1, 1, front_banks(1, "xo"))
            xpose(4, "yt00")
            xpose(5, "yt01")
            xpose(6, "yt10")
            xpose(7, "yt11")
            lo_half(C_FF1_1, 0)

            def square(g2, f, n):
                dve.wait_ge(bank_free[2 * g2 + f], n)
                dve.tensor_tensor(relu[:, f, :], relu[:, f, :], relu[:, f, :], ALU.mult).then_inc(sq_done, 1)

            def hid(g2, f, n):
                dve.wait_ge(hid_hi, n)
                sl = (slice(None), slice(4 * g2 + 2 * f, 4 * g2 + 2 * f + 2), slice(None))
                dve.tensor_tensor(actB_lo[sl], relu[:, f, :].rearrange("p (m s) -> p m s", m=2),
                                  actB_hi[sl].bitcast(f32), ALU.subtract).then_inc(hid_lo, 1)

            def lo_loop(k, half, i):
                c = C_LOOP + k
                u = unit(c, half)
                dve.wait_ge(hi_done, i * 8 + (u + 1))
                dve.tensor_tensor(w_lo[:, c % 2, half, :], raw[:, u % RAW, :], w_hi[:, c % 2, half, :].bitcast(f32),
                                  ALU.subtract).then_inc(lo_done, 1)

            for g in range(2):
                if g == 0:
                    lo_half(C_FF1_1, 1)
                square(g, 0, FF_BASE[2 * g] + 1)
                if g == 1:
                    lo_half(C_FF2_0, 1)
                hid(g, 0, 2 * g + 1)
                square(g, 1, FF_BASE[2 * g + 1] + 1)
                lo_half(C_FF2_0 + g, 0)
                hid(g, 1, 2 * g + 2)
            lo_half(C_LOOP, 1)
            with dve.Fori(0, G // 2 - 1) as i:
                for g in range(2):
                    n = 4 + 2 * g
                    lo_loop(2 * g + 1, 0, i)
                    square(g, 0, i + (FF_BASE[2 * g] + 2))
                    lo_loop(2 * g + 1, 1, i)
                    hid(g, 0, i * 4 + (n + 1))
                    square(g, 1, i + (FF_BASE[2 * g + 1] + 2))
                    lo_loop(2 * g + 2, 0, i)
                    hid(g, 1, i * 4 + (n + 2))
                    lo_loop(2 * g + 2, 1, i)
            for t in range(2):
                layer_norm(2, t, [(bank[4 + 2 * t + c], (bank_full[4 + 2 * t + c], FF_BASE[4 + 2 * t + c] + 1), bank_free[4 + 2 * t + c])
                                  for c in range(2)])

        @block.tensor
        def _(pe):
            def begin(name):
                b, before = FILL[name]
                if before:
                    pe.wait_ge(bank_free[b], before)
                return bank[b]

            def full(name):
                return bank_full[FILL[name][0]]

            def three(dst, stat, mov, start, stop):
                pe.matmul(dst, stat[0], mov[0], start=start, stop=False)
                pe.matmul(dst, stat[0], mov[1], start=False, stop=False)
                return pe.matmul(dst, stat[1], mov[0], start=False, stop=stop)

            def weight(c, k, a, b):
                return [w[:, c % 2, k // 4, (k % 4) * 512 + a:(k % 4) * 512 + b] for w in (w_hi, w_lo)]

            def weight_rows(c, k, a, b):
                return [w[:, c % 2, k // 2, (k % 2) * 1024 + a:(k % 2) * 1024 + b] for w in (w_hi, w_lo)]

            A, B = (actA_hi, actA_lo), (actB_hi, actB_lo)

            def features(c, step, src, name):
                b = begin(name)
                for m in range(2):
                    for k in range(8):
                        if step == 0 and m == 0 and k % 4 == 0:
                            pe.wait_ge(lo_done, unit(c, k // 4) + 1)
                        i = three(b[:, m * S:(m + 1) * S], weight(c, k, (2 * step + m) * P, (2 * step + m + 1) * P),
                                  [a[:, k, :] for a in src], k == 0, k == 7)
                i.then_inc(full(name), 1)

            def tokens(c, t, src, name, midway=None):
                b = begin(name)
                for k in range(8):
                    if t == 0 and k % 4 == 0:
                        pe.wait_ge(lo_done, unit(c, k // 4) + 1)
                    if k == 4 and midway is not None:
                        midway()
                    i = three(b[:, :], [a[:, k, t * P:(t + 1) * P] for a in src], weight(c, k, 0, 512), k == 0, k == 7)
                i.then_inc(full(name), 1)

            def rows(c, part, src, names, base, after=None):
                for t in range(2):
                    for n in range(2):
                        b = begin(names[2 * t + n]) if part == 0 else bank[FILL[names[2 * t + n]][0]]
                        for k in range(4):
                            if t == 0 and n == 0 and k % 2 == 0:
                                pe.wait_ge(lo_done, unit(c, k // 2) + 1)
                            i = three(b[:, :], [a[:, base + k, t * P:(t + 1) * P] for a in src],
                                      weight_rows(c, k, n * 512, (n + 1) * 512), part == 0 and k == 0,
                                      part == 1 and k == 3)
                        if part == 1:
                            i.then_inc(full(names[2 * t + n]), 1)
                        elif t == 1 and n == 1:
                            i.then_inc(rows_used, 1)
                        if after is not None:
                            after(2 * t + n)

            b = begin("glr")
            pe.wait_ge(raw_in[0], 16)
            pe.wait_ge(wglr_in, 16)
            for k in range(8):
                i = pe.matmul(b[0:RANK, 0:S], wglr[:, k, :], raw[:, 0, k * S:(k + 1) * S], start=k == 0, stop=k == 7)
            i.then_inc(full("glr"), 1)
            pe.wait_ge(lo_done, 1)
            features(0, 0, A, "qg")
            b = begin("z")
            wait_out(pe, "glr")
            pe.wait_ge(wgu_in, 16)
            for f in range(2):
                i = pe.matmul(b[:, f * S:(f + 1) * S], wgu[:, f * P:(f + 1) * P], glrT[:], start=True, stop=True)
            i.then_inc(full("z"), 1)
            features(0, 1, A, "kg")
            features(1, 0, A, "qa0")
            features(1, 1, A, "qa1")
            features(2, 0, A, "ka0")
            features(2, 1, A, "ka1")

            def score(h):
                b = begin(f"score{h}")
                r = slice(64 * (h % 2), 64 * (h % 2) + 64)
                pe.matmul(b[:, 0:P], qaT[r, h // 2, 0:P], kaT[r, h // 2, 0:P], start=True, stop=True)
                pe.matmul(b[:, P:3 * P], qaT[r, h // 2, P:S], kaT[r, h // 2, :], start=True, stop=True)\
                    .then_inc(full(f"score{h}"), 1)

            def transpose_probs(h):
                b = begin(f"pt{h}")
                pe.wait_ge(prob_done, 2 * h + 2)
                for a in range(3):
                    i = pe.transpose(b[:, a * P:(a + 1) * P], probs[:, h * 384 + a * P:h * 384 + (a + 1) * P], ident)
                i.then_inc(full(f"pt{h}"), 1)

            tokens(3, 0, A, "va0")
            for name in ("qa0", "qa1", "ka0", "ka1"):
                wait_out(pe, name)
            for h in range(4):
                score(h)
            tokens(3, 1, A, "va1")
            tokens(4, 0, A, "vg0")
            for h in range(4, 8):
                score(h)
            tokens(4, 1, A, "vg1")
            for h in range(4):
                transpose_probs(h)
            tokens(5, 0, A, "rg0")
            for h in range(4, 8):
                transpose_probs(h)
            tokens(5, 1, A, "rg1")
            for name in ["va0", "va1"] + [f"pt{h}" for h in range(HA)]:
                wait_out(pe, name)
            for n in range(2):
                b = begin(f"pv{n}")
                for h in range(4 * n, 4 * n + 4):
                    r = slice(64 * (h % 2), 64 * (h % 2) + 64)
                    c = (h // 2 - 2 * n) * S
                    pe.matmul(b[r, c:c + S], va[:, 0, h * DA:(h + 1) * DA], probsT[:, h * 384:h * 384 + S],
                              start=True, stop=False)
                    i = pe.matmul(b[r, c + P:c + S], va[:, 1, h * DA:(h + 1) * DA],
                                  probsT[:, h * 384 + S:h * 384 + 384], start=False, stop=True)
                i.then_inc(full(f"pv{n}"), 1)
            b = begin("diag")
            pe.wait_ge(qkdiag_done, 1)
            pe.wait_ge(headsel_done, 2)
            for t in range(2):
                for f in range(2):
                    k = 4 * t + 2 * f
                    i = pe.matmul(b[:, k:k + 2], qkdiag[:, f * S + t * P:f * S + (t + 1) * P], headsel[:],
                                  start=True, stop=True)
            i.then_inc(full("diag"), 1)

            def level(n):
                pe.wait_ge(lev_done, 2 * n + 2)
                banks = [begin(f"lv{n}r{r}") for r in range(2)]
                for a in range(4):
                    for r in range(2):
                        v = lev[n % 2][64 * r:64 * r + 64, (a % 2) * S + (a // 2) * P:(a % 2) * S + (a // 2 + 1) * P]
                        i = pe.matmul(banks[r][:, a * P:(a + 1) * P], v, v, start=True, stop=True)
                        if a == 3:
                            i.then_inc(full(f"lv{n}r{r}"), 1)

            pe.wait_ge(lo_done, MEM_UNIT + 1)
            features(6, 0, B, "xk0")
            level(0)
            features(6, 1, B, "xk1")
            level(1)
            level(2)
            features(7, 0, B, "xk2")
            level(3)
            level(4)
            features(7, 1, B, "xk3")
            level(5)
            level(6)
            tokens(8, 0, B, "xv00")
            pe.wait_ge(lev_done, 16)
            banks = [begin("off0"), begin("off1")]
            for f in range(2):
                for r in range(2):
                    v = lev[1][64 * r:64 * r + 64, f * S:(f + 1) * S]
                    i = pe.matmul(banks[r][:, f * P:(f + 1) * P], v[:, 0:P], v[:, P:S], start=True, stop=True)
                    if f == 1:
                        i.then_inc(full(f"off{r}"), 1)
            tokens(8, 1, B, "xv01")
            for name in ("vg0", "vg1", "off0", "off1", "lv6r0", "lv6r1"):
                wait_out(pe, name)
            for t in range(2):
                b = begin(f"av{t}")
                for h in range(HG):
                    c = slice(h * DV, (h + 1) * DV)
                    if t == 1:
                        pe.matmul(b[:, c], attoff[:, h, :], vg[:, 0, c], start=True, stop=False)
                    i = pe.matmul(b[:, c], attT[:, t, h, :], vg[:, t, c], start=t == 0, stop=True)
                i.then_inc(full(f"av{t}"), 1)
            mo = ["mo00", "mo01", "mo10", "mo11"]
            wait_out(pe, "pv0")
            wait_out(pe, "pv1")
            rows(9, 0, A, mo, 0)
            for t in range(2):
                b = begin(f"gt{t}")
                pe.wait_ge(glao_done, 4 * t + 4)
                for h in range(HG):
                    i = pe.transpose(b[:, h * P:(h + 1) * P], vg[:, t, h * DV:(h + 1) * DV], ident)
                i.then_inc(full(f"gt{t}"), 1)
            wait_out(pe, "gt0")
            wait_out(pe, "gt1")
            rows(10, 1, A, mo, 4)

            def transpose_x(n, t, name):
                for c in range(2):
                    b = begin(f"{name}{t}{c}")
                    pe.wait_ge(ln_done, 4 * n + 2 * t + c + 1)
                    for m in range(4):
                        i = pe.transpose(b[:, m * P:(m + 1) * P], X[:, t, (4 * c + m) * P:(4 * c + m + 1) * P], ident)
                    i.then_inc(full(f"{name}{t}{c}"), 1)

            tokens(11, 0, B, "xv10")
            transpose_x(0, 0, "xt")
            tokens(11, 1, B, "xv11", midway=lambda: transpose_x(0, 1, "xt"))

            def cscore(h):
                b = begin(f"cs{h}")
                wait_out(pe, f"xq{h}")
                for t in range(2):
                    for d in range(2):
                        i = pe.matmul(b[:, t * S:(t + 1) * S], cqT[:, 2 * h + d, t * P:(t + 1) * P],
                                      memkT[:, 2 * h + d, :], start=d == 0, stop=d == 1)
                i.then_inc(full(f"cs{h}"), 1)

            def ctranspose(h):
                b = begin(f"cpt{h}")
                pe.wait_ge(cprob_done, 2 * h + 2)
                for m in range(2):
                    for t in range(2):
                        i = pe.transpose(b[:, m * S + t * P:m * S + (t + 1) * P], cprobs[:, h, t, m * P:(m + 1) * P], ident)
                i.then_inc(full(f"cpt{h}"), 1)

            def cvalues(h):
                b = begin(f"cpv{h}")
                wait_out(pe, f"cpt{h}")
                for d in range(2):
                    for m in range(2):
                        i = pe.matmul(b[:, d * S:(d + 1) * S], memv[:, m, h * DX + d * P:h * DX + (d + 1) * P],
                                      cprobsT[:, h, m, :], start=m == 0, stop=m == 1)
                i.then_inc(full(f"cpv{h}"), 1)

            for name in ("xt00", "xt01", "xt10", "xt11"):
                wait_out(pe, name)
            features(12, 0, A, "xq0")
            features(12, 1, A, "xq1")
            for n in range(4):
                wait_out(pe, f"xk{n}")
            cscore(0)
            features(13, 0, A, "xq2")
            cscore(1)
            features(13, 1, A, "xq3")
            cscore(2)
            ctranspose(0)
            cscore(3)
            for name in ("xv00", "xv01", "xv10", "xv11"):
                wait_out(pe, name)
            cvalues(0)
            ctranspose(1)
            cvalues(1)
            ctranspose(2)
            cvalues(2)
            ctranspose(3)
            xo = ["xo00", "xo01", "xo10", "xo11"]
            wait_out(pe, "cpv0")
            wait_out(pe, "cpv1")
            rows(14, 0, B, xo, 0, after=lambda n: cvalues(3) if n == 1 else None)
            wait_out(pe, "cpv2")
            wait_out(pe, "cpv3")
            rows(15, 1, B, xo, 4)
            transpose_x(1, 0, "yt")
            transpose_x(1, 1, "yt")
            for name in ("yt00", "yt01", "yt10", "yt11"):
                wait_out(pe, name)

            def ff1(g2, par, lo_need, free_need):
                for f in range(2):
                    b = bank[2 * g2 + f]
                    pe.wait_ge(bank_free[2 * g2 + f], free_need[f])
                    for m in range(2):
                        for k in range(8):
                            if f == 0 and m == 0 and k % 4 == 0:
                                pe.wait_ge(lo_done, lo_need[k // 4])
                            i = three(b[:, m * S:(m + 1) * S],
                                      [w[:, par, k // 4, (k % 4) * 512 + (2 * f + m) * P:(k % 4) * 512 + (2 * f + m + 1) * P]
                                       for w in (w_hi, w_lo)], [a[:, k, :] for a in A], k == 0, k == 7)
                    i.then_inc(bank_full[2 * g2 + f], 1)

            def ff2(g2, par, lo_need, hid_need, first=False, last=False):
                pe.wait_ge(hid_lo, hid_need)
                for t in range(2):
                    for n in range(2):
                        b = bank[4 + 2 * t + n]
                        if first:
                            pe.wait_ge(bank_free[4 + 2 * t + n], FF_BASE[4 + 2 * t + n])
                        for k in range(4):
                            if t == 0 and n == 0 and k % 2 == 0:
                                pe.wait_ge(lo_done, lo_need[k // 2])
                            i = three(b[:, :], [a[:, 4 * g2 + k, t * P:(t + 1) * P] for a in B],
                                      [w[:, par, k // 2, (k % 2) * 1024 + n * 512:(k % 2) * 1024 + (n + 1) * 512]
                                       for w in (w_hi, w_lo)], first and k == 0, last and k == 3)
                        if last:
                            i.then_inc(bank_full[4 + 2 * t + n], 1)
                if not last:
                    i.then_inc(rows_used, 1)

            def need(c):
                return [unit(c, half) + 1 for half in range(2)]

            for g in range(2):
                ff1(g, (C_FF1_0 + g) % 2, need(C_FF1_0 + g), [FF_BASE[2 * g + f] for f in range(2)])
            ff2(0, C_FF2_0 % 2, need(C_FF2_0), 2, first=True)
            with pe.Fori(0, G // 2 - 1) as i:
                for g in range(2):
                    c = C_LOOP + 2 * g
                    ff1(g, c % 2, [i * 8 + n for n in need(c)],
                        [i + (FF_BASE[2 * g + f] + 1) for f in range(2)])
                    ff2(1 - g, (c + 1) % 2, [i * 8 + n for n in need(c + 1)], i * 4 + (4 + 2 * g))
            ff2(1, C_LAST % 2, need(C_LAST), 2 * G, last=True)


def kernel(**inputs):
    import concourse.bacc as bacc
    from concourse.bass_utils import run_bass_kernel_spmd

    names = ["x", "xT", "memT", "w_in", "w_gate_up", "b_gate", "gla_norm_g", "w_mix_o", "ln1_g", "ln1_b",
             "w_xq", "w_xkv", "w_xo", "ln2_g", "ln2_b", "w_ff1", "w_ff2", "ln3_g", "ln3_b"]
    laid = {n: np.asarray(a)[0] for n, a in inputs.items()}
    laid["b_gate"] = laid["b_gate"].reshape(2, P).T
    laid["xT"], laid["memT"] = laid["x"].T, laid["mem"].T
    arrays = {f"in_{n}": np.ascontiguousarray(laid[n]) for n in names}
    arrays["in_consts"] = shape_constants()
    nc = bacc.Bacc("TRN2", target_bir_lowering=False, num_devices=1)
    args = {n: nc.dram_tensor(f"in_{n}", arrays[f"in_{n}"].shape, mybir.dt.float32, kind="ExternalInput").ap()
            for n in names + ["consts"]}
    out = nc.dram_tensor("out", (S, D), mybir.dt.float32, kind="ExternalOutput").ap()
    build(nc, out=out, **args)
    result = run_bass_kernel_spmd(nc, [arrays], core_ids=[0]).results[0]["out"]
    return result.reshape(1, S, D)
```

```python
from contextlib import ExitStack

import numpy as np
import concourse.bass as bass
from concourse import mybir

D = 1024
S = 256
P = 128
HA, DA = 8, 64
HG, DK, DV = 4, 64, 128
CHUNK = 64
RANK = 16
HX, DX = 4, 256
F = 4 * D
GATE_TEMP = 16.0
LN_EPS, RMS_EPS = 1e-5, 1e-6
ALPHA = 2.0 ** 0.25
QA, KA, VA, QG, KG, VG, RG, GL = 0, 512, 1024, 1536, 1792, 2048, 2560, 3072
LEVELS = [64, 32, 16, 8, 4, 2, 1]
SLOPES = [2.0 ** (-8.0 * (h + 1) / HA) for h in range(HA)]
MASKED = -1e36
C_ID, C_DIST, C_MASK = 0, P, P + 3 * P
N_CONST = C_MASK + len(LEVELS) * P
G = 8


def shape_constants():
    c = np.zeros((P, N_CONST), np.float32)
    c[:, C_ID:C_ID + P] = np.eye(P)
    q, k = np.arange(P)[:, None], np.arange(S)[None, :]
    c[:, C_DIST:C_DIST + P] = np.where(k[:, :P] <= q, k[:, :P] - q, MASKED)
    c[:, C_DIST + P:C_DIST + 3 * P] = np.where(k <= q + P, k - q - P, MASKED)
    s, t = np.arange(P)[:, None], np.arange(P)[None, :]
    for n, w in enumerate(LEVELS):
        own = (s // (2 * w) == t // (2 * w)) & (s % (2 * w) < w) & (t % (2 * w) >= w)
        c[:, C_MASK + n * P:C_MASK + (n + 1) * P] = own
    return c


CHUNKS = [
    ("w_in", "cols", QG), ("w_in", "cols", QA), ("w_in", "cols", KA), ("w_in", "cols", VA),
    ("w_in", "cols", VG), ("w_in", "cols", RG),
    ("w_xkv", "cols", 0), ("w_xkv", "cols", 512), ("w_xkv", "cols", 1024),
    ("w_mix_o", "rows", 0), ("w_mix_o", "rows", 512),
    ("w_xkv", "cols", 1536),
    ("w_xq", "cols", 0), ("w_xq", "cols", 512),
    ("w_xo", "rows", 0), ("w_xo", "rows", 512),
]
N_FRONT = len(CHUNKS)
C_FF1_0, C_FF1_1, C_FF2_0, C_LOOP = N_FRONT, N_FRONT + 1, N_FRONT + 2, N_FRONT + 3
C_LAST = C_LOOP + 2 * (G - 2)
MEM_CHUNK = 6


def unit(chunk, half):
    return 1 + 2 * chunk + half + (chunk >= MEM_CHUNK)


MEM_UNIT = unit(MEM_CHUNK, 0) - 1
RAW = 4
POOL_UNITS = [unit(12, 1)]


EARLY = 3


def hi_count(u):
    return u + 1 - EARLY


def lo_count(u):
    return u + 1 - EARLY - sum(v <= u for v in POOL_UNITS)


def raw_count(u):
    return 16 * (u // RAW + (u % RAW >= EARLY))

FRONT_FILLS = (
    [("glr", 4), ("qg", 0), ("kg", 1), ("z", 5), ("qa0", 2), ("qa1", 3), ("ka0", 0), ("ka1", 1), ("va0", 2)]
    + [(f"score{h}", 4 + h) for h in range(4)] + [("va1", 3), ("vg0", 0)]
    + [(f"score{h}", h) for h in range(4, 8)] + [("vg1", 1)]
    + [(f"pt{h}", 4 + h) for h in range(4)] + [("rg0", 2)] + [(f"pt{h}", h) for h in range(4, 8)]
    + [("rg1", 3), ("pv0", 4), ("pv1", 5), ("diag", 6), ("xk0", 0), ("xk1", 1)]
    + [("lv0r0", 4), ("lv0r1", 5), ("lv1r0", 6), ("lv1r1", 7), ("xk2", 2), ("lv2r0", 4), ("lv2r1", 5),
       ("lv3r0", 6), ("lv3r1", 7), ("xk3", 3), ("lv4r0", 4), ("lv4r1", 5), ("lv5r0", 6), ("lv5r1", 7),
       ("xv00", 0), ("lv6r0", 4), ("lv6r1", 5), ("off0", 6), ("off1", 7), ("xv01", 1), ("av0", 4), ("av1", 5)]
    + [("mo00", 2), ("mo01", 3), ("mo10", 0), ("gt0", 6), ("gt1", 7), ("mo11", 1)]
    + [("xv10", 2), ("xt00", 4), ("xt01", 5), ("xv11", 3), ("xt10", 6), ("xt11", 7)]
    + [("xq0", 0), ("xq1", 1), ("cs0", 4), ("xq2", 2), ("cs1", 5), ("xq3", 3), ("cs2", 6), ("cpt0", 4), ("cpt1", 5)]
    + [("cs3", 7), ("cpv0", 4), ("cpv1", 5), ("cpt2", 6), ("cpv2", 6)]
    + [("xo00", 0), ("cpt3", 7), ("xo01", 1), ("cpv3", 7), ("xo10", 2), ("xo11", 3)]
    + [("yt00", 4), ("yt01", 5), ("hid0", 0), ("yt10", 6), ("yt11", 7), ("hid1", 1), ("ht0", 4), ("ht1", 5)]
)
FILL = {}
for _name, _bank in FRONT_FILLS:
    FILL[_name] = (_bank, sum(b == _bank for b, _ in FILL.values()))
CHUNK_END = {0: "kg", 1: "qa1", 2: "ka1", 3: "va1", 4: "vg1", 5: "rg1", 6: "xk1", 7: "xk3", 8: "xv01",
             10: "mo11", 11: "xv11", 12: "xq1", 13: "xq3", 15: "xo11", C_FF1_0: "hid1"}
ROWS_END = {9: 1, 14: 2, C_FF2_0: 3}
FF_BASE = [sum(b == bank for b, _ in FILL.values()) for bank in range(8)]


def build(nc, x, xT, memT, w_in, w_gate_up, b_gate, gla_norm_g, w_mix_o, ln1_g, ln1_b, w_xq, w_xkv,
          w_xo, ln2_g, ln2_b, w_ff1, w_ff2, ln3_g, ln3_b, consts, out):
    f32, f32r, i32 = mybir.dt.float32, mybir.dt.float32r, mybir.dt.int32
    ALU, ACT, AX = mybir.AluOpType, mybir.ActivationFunctionType, mybir.AxisListType
    weights = {"w_in": w_in, "w_xkv": w_xkv, "w_mix_o": w_mix_o, "w_xq": w_xq, "w_xo": w_xo}
    ln_rows = [(ln1_g, ln1_b), (ln2_g, ln2_b), (ln3_g, ln3_b)]

    ctx = ExitStack()
    with ctx:
        def sb(name, shape, dt=f32):
            return ctx.enter_context(nc.sbuf_tensor(name, shape, dt))

        def sem(name):
            return ctx.enter_context(nc.semaphore(name))

        raw = sb("raw", [P, RAW, 2048])
        w_hi = sb("w_hi", [P, 2, 2, 2048], f32r)
        w_lo = sb("w_lo", [P, 2, 2, 2048], f32r)
        actA_hi = sb("actA_hi", [P, 8, S], f32r)
        actA_lo = sb("actA_lo", [P, 8, S], f32r)
        actB_hi = sb("actB_hi", [P, 8, S], f32r)
        actB_lo = sb("actB_lo", [P, 8, S], f32r)
        X = sb("X", [P, 2, D])
        const = sb("const", [P, N_CONST])
        probs = sb("probs", [P, HA * 384])
        probsT = sb("probsT", [P, HA * 384])
        qk = sb("qk", [P, 2048])
        values = sb("values", [P, 2048])
        gla = sb("gla", [P, 2560])
        att = sb("att", [P, 1536])
        reset = sb("reset", [P, 512])
        qkdiag = sb("qkdiag", [P, 512])
        wglr = sb("wglr", [P, 8, RANK])
        wgu = sb("wgu", [RANK, 256])
        glrT = sb("glrT", [RANK, S])
        bgate = sb("bgate", [P, 2])
        headsel = sb("headsel", [P, 2])
        gnorm = sb("gnorm", [P, DV])
        negmax = sb("negmax", [P, 2 * HA])
        sums = sb("sums", [P, 2 * HA])
        rsums = sb("rsums", [P, 2 * HA])
        diag = sb("diag", [P, 8])
        ssq = sb("ssq", [P, 8])
        meansq = sb("meansq", [P, 8])
        rms = sb("rms", [P, 8])
        minus_half = sb("minus_half", [P, 8])
        stats = sb("stats", [P, 3, 2, 2, 6])
        mv = sb("mv", [P, 3, 2, 2])
        vareps = sb("vareps", [P, 3, 2, 1])
        rstd = sb("rstd", [P, 3, 2, 1])
        cmax = sb("cmax", [P, 2 * HX])
        cneg = sb("cneg", [P, 2 * HX])
        csum = sb("csum", [P, 2 * HX])
        crec = sb("crec", [P, 2 * HX])

        ident = const[:, C_ID:C_ID + P]
        qaT = qk[:, 0:1024].rearrange("p (m s) -> p m s", m=4)
        kaT = qk[:, 1024:2048].rearrange("p (m s) -> p m s", m=4)
        expo = [qk[:, 512 * b:512 * b + 512] for b in range(2)]
        lev = [qk[:, 1024 + 512 * b:1536 + 512 * b] for b in range(2)]
        va = values[:, 0:1024].rearrange("p (t n) -> p t n", t=2)
        vg = values[:, 1024:2048].rearrange("p (t n) -> p t n", t=2)
        sg = gla[:, 0:1024].rearrange("p (t n) -> p t n", t=2)
        qgT, kgT, cum = gla[:, 1024:1536], gla[:, 1536:2048], gla[:, 2048:2560]
        attT = att[:, 0:1024].rearrange("p (t h s) -> p t h s", t=2, h=HG)
        attT_r = att[:, 0:1024].rearrange("p (a r s) -> p a r s", a=4, r=2)
        attoff = att[:, 1024:1536].rearrange("p (h s) -> p h s", h=HG)
        zlin, zabs = att[:, 0:512], att[:, 512:1024]
        memkT = probs[:, 0:2048].rearrange("p (m s) -> p m s", m=8)
        lng = probs[:, 2048:3072]
        memv = probsT[:, 0:2048].rearrange("p (t n) -> p t n", t=2)
        lnb = probsT[:, 2048:3072]
        cqT = values[:, :].rearrange("p (m s) -> p m s", m=8)
        cprobs = qk[:, :].rearrange("p (h t m) -> p h t m", h=HX, t=2)
        cprobsT = gla[:, 0:2048].rearrange("p (h m s) -> p h m s", h=HX, m=2)
        relu = att[:, 0:1024].rearrange("p (b n) -> p b n", b=2)

        def level_mask(n):
            return const[:, C_MASK + n * P:C_MASK + (n + 1) * P].bitcast(i32)

        bank = [ctx.enter_context(nc.psum_tensor(f"bank{b}", [P, 512], f32)) for b in range(8)]

        bank_full = [sem(f"bank_full{b}") for b in range(8)]
        bank_free = [sem(f"bank_free{b}") for b in range(8)]
        raw_in = [sem(f"raw_in{r}") for r in range(RAW)]
        hi_done = sem("hi_done")
        lo_done = sem("lo_done")
        early_in = [sem(f"early_in{n}") for n in range(2 * EARLY)]
        early_hi, early_lo = sem("early_hi"), sem("early_lo")
        pool_lo = sem("pool_lo")
        rows_used = sem("rows_used")
        wglr_in, wgu_in, const_in, small_in, x_in = map(sem, ("wglr_in", "wgu_in", "const_in", "small_in", "x_in"))
        ln_in = [sem(f"ln_in{n}") for n in range(3)]
        out_done = sem("out_done")
        dve_link, act_link, pool_link = sem("dve_link"), sem("act_link"), sem("pool_link")
        zabs_done, softplus_done, cum_done = map(sem, ("zabs_done", "softplus_done", "cum_done"))
        reset_done, att_zeroed, headsel_done, half_done = map(sem, ("reset_done", "att_zeroed", "headsel_done", "half_done"))
        bias_done, score_done, exp_done, prob_done = map(sem, ("bias_done", "score_done", "exp_done", "prob_done"))
        mix_hi = sem("mix_hi")
        expr_done, gate_done = sem("expr_done"), sem("gate_done")
        expo_done, decay_done, lev_done, qkdiag_done = map(sem, ("expo_done", "decay_done", "lev_done", "qkdiag_done"))
        ssq_done, meansq_done, rms_done, glao_done = map(sem, ("ssq_done", "meansq_done", "rms_done", "glao_done"))
        var_done, rstd_done, ln_done = map(sem, ("var_done", "rstd_done", "ln_done"))
        xT_hi = sem("xT_hi")
        cneg_done, cexp_done, cprob_done = map(sem, ("cneg_done", "cexp_done", "cprob_done"))
        cross_hi = sem("cross_hi")
        sq_done, hid_hi, hid_lo = map(sem, ("sq_done", "hid_hi", "hid_lo"))

        def wait_full(eng, name):
            b, before = FILL[name]
            eng.wait_ge(bank_full[b], before + 1)
            return bank[b]

        def freed(name):
            return bank_free[FILL[name][0]]

        def wait_out(eng, name):
            b, before = FILL[name]
            eng.wait_ge(bank_free[b], before + 1)

        def wait_lo(eng, u, piece=1):
            if u < EARLY:
                eng.wait_ge(early_lo, 2 * u + piece + 1)
            elif u in POOL_UNITS:
                eng.wait_ge(pool_lo, POOL_UNITS.index(u) + 1)
            else:
                eng.wait_ge(lo_done, lo_count(u))

        def early(act_part, w_part):
            return [act_part[:].rearrange("p a s -> p (a s)"), w_part[:, 0, 0, :], w_part[:, 0, 1, :]]

        def half_view(u):
            return raw[:, u % RAW, :]

        block = ctx.enter_context(nc.Block())

        @block.sync
        def _(sp):
            def chunk_source(c, half):
                name, kind, at = CHUNKS[c]
                w = weights[name]
                if kind == "cols":
                    return w[half * 512:(half + 1) * 512, at:at + 512].rearrange("(a p) n -> p a n", p=P)
                return w[at + half * 256:at + (half + 1) * 256, :].rearrange("(a p) n -> p a n", p=P)

            def load(u, src, tiles):
                if u >= RAW:
                    wait_lo(sp, u - RAW)
                if u == RAW:
                    sp.wait_ge(bank_full[FILL["glr"][0]], 1)
                sp.dma_start(half_view(u).rearrange("p (a n) -> p a n", a=tiles), src).then_inc(raw_in[u % RAW], 16)

            def load_chunk(c):
                for half in range(2):
                    load(unit(c, half), chunk_source(c, half), 4 if CHUNKS[c][1] == "cols" else 2)

            def load_ln(n):
                g, b = ln_rows[n]
                sp.dma_start(lng, g.partition_broadcast(P)).then_inc(ln_in[n], 16)
                sp.dma_start(lnb, b.partition_broadcast(P)).then_inc(ln_in[n], 16)

            for u in range(EARLY):
                src = xT.rearrange("(a p) s -> p a s", p=P) if u == 0 else chunk_source(0, u - 1)
                tiles = src.shape[1] // 2
                for piece in range(2):
                    sp.dma_start(raw[:, u, piece * 1024:(piece + 1) * 1024].rearrange("p (a n) -> p a n", a=tiles),
                                 src[:, piece * tiles:(piece + 1) * tiles, :]).then_inc(early_in[2 * u + piece], 16)
            load_chunk(1)
            sp.dma_start(const[:], consts).then_inc(const_in, 16)
            for c in range(2, 6):
                load_chunk(c)
            load(MEM_UNIT, memT.rearrange("(a p) s -> p a s", p=P), 8)
            load_chunk(6)
            sp.dma_start(X[:], x.rearrange("(t p) n -> p t n", p=P)).then_inc(x_in, 16)
            load_chunk(7)
            load_chunk(8)
            load_chunk(9)
            load_chunk(10)
            sp.wait_ge(bank_full[FILL["pv1"][0]], FILL["pv1"][1] + 1)
            load_ln(0)
            for c in range(11, N_FRONT):
                load_chunk(c)
            ff1_src = [w_ff1[half * 512:(half + 1) * 512, :].rearrange("(a p) n -> p a n", p=P) for half in range(2)]

            def load_ff1(u, g):
                sp.dma_start(raw[:, u % RAW, :].rearrange("p (a n) -> p a n", a=4),
                             ff1_src[u % 2][:, :, bass.ds(g * 512, 512)]).then_inc(raw_in[u % RAW], 16)

            def load_ff2(u, g):
                sp.dma_start(raw[:, u % RAW, :].rearrange("p (a n) -> p a n", a=2),
                             w_ff2[bass.ds(g * 512 + (u % 2) * 256, 256), :].rearrange("(a p) n -> p a n", p=P))\
                    .then_inc(raw_in[u % RAW], 16)

            for c, source, g in ((C_FF1_0, load_ff1, 0), (C_FF1_1, load_ff1, 1), (C_FF2_0, load_ff2, 0)):
                for half in range(2):
                    u = unit(c, half)
                    wait_lo(sp, u - RAW)
                    source(u, g)
                if c == C_FF1_0:
                    sp.wait_ge(ln_done, 4)
                    load_ln(1)
            u0 = unit(C_LOOP, 0)
            with sp.Fori(0, G // 2 - 1) as i:
                for n in range(4):
                    for half in range(2):
                        k = 2 * n + half
                        sp.wait_ge(lo_done, i * 8 + lo_count(u0 + k - RAW))
                        if n % 2 == 0:
                            load_ff1(u0 + k, i * 2 + 2 + n // 2)
                        else:
                            load_ff2(u0 + k, i * 2 + 1 + n // 2)
            for half in range(2):
                u = unit(C_LAST, half)
                wait_lo(sp, u - RAW)
                load_ff2(u, G - 1)
            sp.wait_ge(ln_done, 8)
            load_ln(2)
            for t in range(2):
                for n in range(2):
                    sp.wait_ge(ln_done, 8 + 2 * t + n + 1)
                    sp.dma_start(out[t * P:(t + 1) * P, n * 512:(n + 1) * 512],
                                 X[:, t, n * 512:(n + 1) * 512]).then_inc(out_done, 16)
            sp.wait_ge(out_done, 64)

        @block.gpsimd
        def _(pool):
            pool.memset(minus_half[:], -0.5).then_inc(half_done, 1)
            pool.memset(headsel[:], 0.0).then_inc(pool_link, 1)
            pool.memset(reset[:], 1.0).then_inc(pool_link, 1)
            pool.wait_ge(pool_link, 2)
            pool.memset(headsel[0:64, 0:1], 1.0).then_inc(headsel_done, 1)
            pool.wait_ge(headsel_done, 1)
            pool.memset(headsel[64:128, 1:2], 1.0).then_inc(headsel_done, 1)
            pool.wait_ge(headsel_done, 2)
            pool.memset(reset[:, :].rearrange("p (c s) -> p c s", s=CHUNK)[:, :, 0:1], 0.0).then_inc(reset_done, 1)
            pool.wait_ge(const_in, 16)
            for h in range(HA):
                pool.tensor_scalar(probsT[:, h * 384:(h + 1) * 384], const[:, C_DIST:C_DIST + 384],
                                   SLOPES[h] * DA ** 0.5, None, ALU.mult).then_inc(bias_done, 1)
            wait_out(pool, "qg")
            wait_out(pool, "kg")
            pool.tensor_tensor(qkdiag[:], qgT, kgT, ALU.mult).then_inc(qkdiag_done, 1)
            pool.wait_ge(cum_done, 1)
            pool.memset(att[:, 0:1024], 0.0).then_inc(att_zeroed, 1)
            pool.wait_ge(small_in, 32)
            for t in range(2):
                wait_out(pool, f"rg{t}")
                v = sg[:, t, :].rearrange("p (h n) -> p h n", h=HG)
                pool.tensor_tensor(v, v, gnorm[:, :].unsqueeze(1).to_broadcast([P, HG, DV]), ALU.mult)\
                    .then_inc(gate_done, 1)
            for n in range(len(LEVELS) + 1):
                w = LEVELS[n] if n < len(LEVELS) else P
                e = expo[n % 2].rearrange("p (b c w) -> p b c w", c=2, w=w)
                o = lev[n % 2].rearrange("p (b c w) -> p b c w", c=2, w=w)
                pool.wait_ge(decay_done, n + 1)
                if n >= 2:
                    b, before = FILL[f"lv{n - 2}r1"]
                    pool.wait_ge(bank_full[b], before + 1)
                if n < 2:
                    pool.wait_ge(bank_full[FILL["score7"][0]], FILL["score7"][1] + 1)
                for c, src in ((0, kgT), (1, qgT)):
                    pool.tensor_tensor(o[:, :, c, :], src.rearrange("p (b c w) -> p b c w", c=2, w=w)[:, :, c, :],
                                       e[:, :, c, :], ALU.mult).then_inc(lev_done, 1)
            pool.wait_ge(half_done, 1)
            for t in range(2):
                pool.wait_ge(meansq_done, t + 1)
                pool.tensor_tensor(rms[:, 4 * t:4 * t + 4], meansq[:, 4 * t:4 * t + 4], minus_half[:, 0:4], ALU.pow)\
                    .then_inc(rms_done, 1)
            for n in range(3):
                if n == 1:
                    for k, u in enumerate(POOL_UNITS):
                        pool.wait_ge(hi_done, hi_count(u))
                        pool.tensor_tensor(w_lo[:, 0, 1, :], half_view(u), w_hi[:, 0, 1, :].bitcast(f32), ALU.subtract)\
                            .then_inc(pool_lo, 1)
                for t in range(2):
                    pool.wait_ge(var_done, 2 * n + t + 1)
                    pool.tensor_tensor(rstd[:, n, t, :], vareps[:, n, t, :], minus_half[:, 0:1], ALU.pow)\
                        .then_inc(rstd_done, 1)

        @block.scalar
        def _(act):
            def hi(u, dst, chunk=None):
                act.wait_ge(raw_in[u % RAW], raw_count(u))
                if chunk is not None and chunk >= 2:
                    before = chunk - 2
                    if before in ROWS_END:
                        act.wait_ge(rows_used, ROWS_END[before])
                    elif before in CHUNK_END:
                        wait_full(act, CHUNK_END[before])
                    else:
                        act.wait_ge(bank_full[3], FF_BASE[3] + 1)
                act.copy(dst, half_view(u)).then_inc(hi_done, 1)

            def hi_half(c, half):
                hi(unit(c, half), w_hi[:, c % 2, half, :], c)

            def evacuate(name, dst, scale=None):
                b = wait_full(act, name)
                if scale is None:
                    return act.copy(dst, b[:, :]).then_inc(freed(name), 1)
                return act.mul(dst, b[:, :], scale).then_inc(freed(name), 1)

            act.dma_start(wglr[:], w_in[:, GL:GL + RANK].rearrange("(a p) n -> p a n", p=P)).then_inc(wglr_in, 16)
            act.dma_start(wgu[:], w_gate_up).then_inc(wgu_in, 16)
            act.dma_start(bgate[:], b_gate).then_inc(small_in, 16)
            act.dma_start(gnorm[:], gla_norm_g.partition_broadcast(P)).then_inc(small_in, 16)
            for u, whole in enumerate(early(actA_hi, w_hi)):
                for piece in range(2):
                    act.wait_ge(early_in[2 * u + piece], 16)
                    act.copy(whole[:, piece * 1024:(piece + 1) * 1024], raw[:, u, piece * 1024:(piece + 1) * 1024])\
                        .then_inc(early_hi, 1)
            hi_half(1, 0)
            wait_full(act, "glr")
            act.copy(glrT[:], bank[4][0:RANK, 0:S]).then_inc(freed("glr"), 1)
            hi_half(1, 1)
            evacuate("qg", qgT, DK ** -0.5)
            evacuate("kg", kgT)
            act.wait_ge(zabs_done, 1)
            act.activation(zabs, zabs, ACT.Exp, scale=-1.0).then_inc(act_link, 1)
            act.wait_ge(act_link, 1)
            act.activation(zabs, zabs, ACT.Ln, bias=1.0).then_inc(softplus_done, 1)
            for n in range(2):
                hi_half(2, n)
                evacuate(f"qa{n}", qaT[:, 2 * n:2 * n + 2, :].rearrange("p m s -> p (m s)"))
            for n in range(2):
                hi_half(3, n)
                evacuate(f"ka{n}", kaT[:, 2 * n:2 * n + 2, :].rearrange("p m s -> p (m s)"))

            def exps(h):
                for t, (a, b) in enumerate(((0, P), (P, 3 * P))):
                    if t == 0:
                        act.wait_ge(score_done, h + 1)
                    else:
                        wait_out(act, f"score{h}")
                    v = probs[:, h * 384 + a:h * 384 + b]
                    act.activation(v, v, ACT.Exp, bias=negmax[:, 2 * h + t:2 * h + t + 1], scale=-1.0,
                                   accum_out=sums[:, 2 * h + t:2 * h + t + 1]).then_inc(exp_done, 1)

            def transposed(h):
                b = wait_full(act, f"pt{h}")
                act.copy(probsT[:, h * 384:(h + 1) * 384], b[:, 0:384]).then_inc(freed(f"pt{h}"), 1)

            hi_half(4, 0)
            evacuate("va0", va[:, 0, :])
            exps(0)
            exps(1)
            hi_half(4, 1)
            exps(2)
            exps(3)
            evacuate("va1", va[:, 1, :])
            hi_half(5, 0)
            evacuate("vg0", vg[:, 0, :])
            exps(4)
            exps(5)
            hi_half(5, 1)
            exps(6)
            exps(7)
            evacuate("vg1", vg[:, 1, :])
            for h in range(4):
                transposed(h)
            hi(MEM_UNIT, actB_hi[:].rearrange("p a s -> p (a s)"))
            hi_half(6, 0)

            def exp_r(t):
                b = wait_full(act, f"rg{t}")
                act.activation(sg[:, t, :], b[:, :], ACT.Exp, scale=-1.0).then_inc(expr_done, 1)

            exp_r(0)
            for h in range(4, 8):
                transposed(h)
            hi_half(6, 1)
            exp_r(1)

            def mix(n, name):
                b = wait_full(act, name)
                if name.startswith("pv"):
                    dst = actA_hi[:, 2 * n:2 * n + 2, :]
                else:
                    dst = actA_hi[:, 4:8, (n - 2) * P:(n - 1) * P]
                act.copy(dst, b[:, :].rearrange("p (m s) -> p m s", m=dst.shape[1])).then_inc(mix_hi, 1)

            mix(0, "pv0")
            mix(1, "pv1")
            b = wait_full(act, "diag")
            act.copy(diag[:], b[:, 0:8]).then_inc(freed("diag"), 1)

            def decay(n):
                act.wait_ge(expo_done, n + 1)
                act.activation(expo[n % 2], expo[n % 2], ACT.Exp, scale=1.0 / GATE_TEMP).then_inc(decay_done, 1)

            def memk(n):
                evacuate(f"xk{n}", memkT[:, 2 * n:2 * n + 2, :].rearrange("p m s -> p (m s)"))

            decay(0)
            hi_half(7, 0)
            decay(1)
            memk(0)
            decay(2)
            hi_half(7, 1)
            memk(1)
            decay(3)
            hi_half(8, 0)
            decay(4)
            memk(2)
            decay(5)
            hi_half(8, 1)
            memk(3)
            decay(6)
            decay(7)
            hi_half(9, 0)
            evacuate("xv00", memv[:, 0, 0:512])
            for r in range(2):
                b = wait_full(act, f"off{r}")
                act.copy(attoff.rearrange("p (f r) s -> p f r s", r=2)[:, :, r, :],
                         b[:, 0:S].rearrange("p (f s) -> p f s", f=2)).then_inc(freed(f"off{r}"), 1)
            hi_half(9, 1)
            evacuate("xv01", memv[:, 1, 0:512])
            for t in range(2):
                wait_out(act, f"av{t}")
                for h in range(HG):
                    act.activation(qk[:, 128 * (4 * t + h):128 * (4 * t + h + 1)], vg[:, t, h * DV:(h + 1) * DV],
                                   ACT.Square, accum_out=ssq[:, 4 * t + h:4 * t + h + 1]).then_inc(ssq_done, 1)
            hi_half(10, 0)
            hi_half(10, 1)
            mix(2, "gt0")
            mix(3, "gt1")
            hi_half(11, 0)
            hi_half(11, 1)

            def xpose(n, name):
                t, c = divmod(n % 4, 2)
                b = wait_full(act, name)
                act.copy(actA_hi[:, 4 * c:4 * c + 4, t * P:(t + 1) * P],
                         b[:, :].rearrange("p (m s) -> p m s", m=4)).then_inc(xT_hi, 1)

            hi_half(12, 0)
            hi_half(12, 1)
            evacuate("xv10", memv[:, 0, 512:1024])
            xpose(0, "xt00")
            xpose(1, "xt01")
            xpose(2, "xt10")
            xpose(3, "xt11")
            evacuate("xv11", memv[:, 1, 512:1024])

            def cq(h):
                evacuate(f"xq{h}", cqT[:, 2 * h:2 * h + 2, :].rearrange("p m s -> p (m s)"))

            def cexps(h):
                act.wait_ge(cneg_done, h + 1)
                b = wait_full(act, f"cs{h}")
                for t in range(2):
                    i = act.activation(cprobs[:, h, t, :], b[:, t * S:(t + 1) * S], ACT.Exp,
                                       bias=cneg[:, 2 * h + t:2 * h + t + 1], scale=DX ** -0.5,
                                       accum_out=csum[:, 2 * h + t:2 * h + t + 1])
                    i.then_inc(cexp_done if t == 0 else freed(f"cs{h}"), 1)

            def cT(h):
                evacuate(f"cpt{h}", cprobsT[:, h, :, :].rearrange("p m s -> p (m s)"))

            def cross(h):
                b = wait_full(act, f"cpv{h}")
                act.copy(actB_hi[:, 2 * h:2 * h + 2, :], b[:, :].rearrange("p (m s) -> p m s", m=2)).then_inc(cross_hi, 1)

            hi_half(13, 0)
            cq(0)
            hi_half(13, 1)
            cq(1)
            cexps(0)
            hi_half(14, 0)
            cq(2)
            cexps(1)
            hi_half(14, 1)
            cq(3)
            cexps(2)
            cT(0)
            cT(1)
            cexps(3)
            cross(0)
            cross(1)
            cT(2)
            cross(2)
            cT(3)
            hi_half(15, 0)
            cross(3)
            hi_half(15, 1)
            hi_half(C_FF1_0, 0)
            hi_half(C_FF1_0, 1)
            hi_half(C_FF1_1, 0)
            def relus(g2, f, use):
                b = 2 * g2 + f
                act.wait_ge(bank_full[b], use)
                act.activation(relu[:, f, :], bank[b][:, :], ACT.Relu).then_inc(bank_free[b], 1)

            def hid(g2, f, n):
                act.wait_ge(sq_done, n)
                act.copy(actB_hi[:, 4 * g2 + 2 * f:4 * g2 + 2 * f + 2, :],
                         relu[:, f, :].rearrange("p (m s) -> p m s", m=2)).then_inc(hid_hi, 1)

            def hi_loop(k, half, i):
                u = unit(C_LOOP + k, half)
                act.wait_ge(raw_in[u % RAW], i * 32 + raw_count(u))
                if k % 2:
                    act.wait_ge(rows_used, i * 2 + (3 + k // 2))
                else:
                    act.wait_ge(bank_full[k - 1], i + (FF_BASE[k - 1] + k // 2))
                act.copy(w_hi[:, (C_LOOP + k) % 2, half, :], raw[:, u % RAW, :]).then_inc(hi_done, 1)

            def first_relu(t):
                wait_full(act, f"hid{t}")
                act.activation(relu[:, t, :], bank[FILL[f"hid{t}"][0]][:, :], ACT.Relu).then_inc(freed(f"hid{t}"), 1)

            def first_hid(t):
                b = wait_full(act, f"ht{t}")
                act.copy(actB_hi[:, 0:4, t * P:(t + 1) * P], b[:, :].rearrange("p (m s) -> p m s", m=4))\
                    .then_inc(hid_hi, 1)

            xpose(4, "yt00")
            xpose(5, "yt01")
            hi_half(C_FF1_1, 1)
            xpose(6, "yt10")
            xpose(7, "yt11")
            first_relu(0)
            first_relu(1)
            hi_half(C_FF2_0, 0)
            first_hid(0)
            first_hid(1)
            relus(1, 0, FF_BASE[2] + 1)
            hi_half(C_FF2_0, 1)
            hid(1, 0, 3)
            relus(1, 1, FF_BASE[3] + 1)
            hi_half(C_LOOP, 0)
            hid(1, 1, 4)
            hi_half(C_LOOP, 1)
            with act.Fori(0, G // 2 - 1) as i:
                for g in range(2):
                    n = 4 + 2 * g
                    hi_loop(2 * g + 1, 0, i)
                    act.wait_ge(hid_lo, i * 4 + (n - 3))
                    relus(g, 0, i + (FF_BASE[2 * g] + 1 + g))
                    hi_loop(2 * g + 1, 1, i)
                    hid(g, 0, i * 4 + (n + 1))
                    act.wait_ge(hid_lo, i * 4 + (n - 2))
                    relus(g, 1, i + (FF_BASE[2 * g + 1] + 1 + g))
                    hi_loop(2 * g + 2, 0, i)
                    hid(g, 1, i * 4 + (n + 2))
                    hi_loop(2 * g + 2, 1, i)

        @block.vector
        def _(dve):
            chain = [0]

            def link(ins):
                chain[0] += 1
                ins.then_inc(dve_link, 1)
                dve.wait_ge(dve_link, chain[0])

            def lo(u, dst, hi_part):
                dve.wait_ge(hi_done, hi_count(u))
                dve.tensor_tensor(dst, half_view(u), hi_part.bitcast(f32), ALU.subtract).then_inc(lo_done, 1)

            def lo_half(c, half):
                lo(unit(c, half), w_lo[:, c % 2, half, :], w_hi[:, c % 2, half, :])

            flat = "p a s -> p (a s)"
            for u, (whole, hi_part) in enumerate(zip(early(actA_lo, w_lo), early(actA_hi, w_hi))):
                for piece in range(2):
                    cut = slice(piece * 1024, (piece + 1) * 1024)
                    dve.wait_ge(early_hi, 2 * u + piece + 1)
                    dve.tensor_tensor(whole[:, cut], raw[:, u, cut], hi_part[:, cut].bitcast(f32), ALU.subtract)\
                        .then_inc(early_lo, 1)
            lo_half(1, 0)
            lo_half(1, 1)
            dve.wait_ge(small_in, 32)
            b = wait_full(dve, "z")
            for f in range(2):
                i = dve.tensor_scalar(zlin[:, f * S:(f + 1) * S], b[:, f * S:(f + 1) * S], bgate[:, f:f + 1], None, ALU.add)
                i.then_inc(freed("z") if f == 1 else dve_link, 1)
            chain[0] += 1
            dve.wait_ge(dve_link, chain[0])
            wait_out(dve, "z")
            dve.scalar_tensor_tensor(zabs, zlin, -1.0, zlin, ALU.mult, ALU.max).then_inc(zabs_done, 1)
            lo_half(2, 0)
            dve.wait_ge(softplus_done, 1)
            link(dve.scalar_tensor_tensor(zlin, zlin, 0.0, zabs, ALU.min, ALU.subtract))
            dve.wait_ge(reset_done, 1)
            dve.tensor_tensor_scan(cum, reset[:], zlin, 0.0, ALU.mult, ALU.add).then_inc(cum_done, 1)
            lo_half(2, 1)
            lo_half(3, 0)
            lo_half(3, 1)

            def score(h):
                b = wait_full(dve, f"score{h}")
                dve.wait_ge(bias_done, h + 1)
                for t, (a, e) in enumerate(((0, P), (P, 3 * P))):
                    i = dve.tensor_tensor_reduce(
                        out=probs[:, h * 384 + a:h * 384 + e], in0=b[:, a:e],
                        in1=probsT[:, h * 384 + a:h * 384 + e], scale=-DA ** -0.5, scalar=3e38,
                        op0=ALU.add, op1=ALU.min, accum_out=negmax[:, 2 * h + t:2 * h + t + 1])
                    i.then_inc(score_done if t == 0 else freed(f"score{h}"), 1)

            def norm(h):
                dve.wait_ge(exp_done, 2 * h + 2)
                link(dve.reciprocal(rsums[:, 2 * h:2 * h + 2], sums[:, 2 * h:2 * h + 2]))
                for t, (a, e) in enumerate(((0, P), (P, 3 * P))):
                    v = probs[:, h * 384 + a:h * 384 + e]
                    dve.tensor_scalar(v, v, rsums[:, 2 * h + t:2 * h + t + 1], None, ALU.mult).then_inc(prob_done, 1)

            lo_half(4, 0)
            for h in range(4):
                score(h)
            norm(0)
            norm(1)
            lo_half(4, 1)
            norm(2)
            norm(3)
            lo_half(5, 0)
            for h in range(4, 8):
                score(h)
            norm(4)
            norm(5)
            lo_half(5, 1)
            norm(6)
            norm(7)

            def exponents(n):
                e, c4 = expo[n % 2], cum
                if n >= 2:
                    dve.wait_ge(lev_done, 2 * n - 2)
                else:
                    dve.wait_ge(bank_full[FILL["score7"][0]], FILL["score7"][1] + 1)
                if n < len(LEVELS) and LEVELS[n] < CHUNK:
                    w = LEVELS[n]
                    ev = e.rearrange("p (b c w) -> p b c w", c=2, w=w)
                    cv = c4.rearrange("p (b c w) -> p b c w", c=2, w=w)
                    mid = cv[:, :, 0, w - 1:w].to_broadcast([P, 512 // (2 * w), w])
                    link(dve.tensor_tensor(ev[:, :, 0, :], mid, cv[:, :, 0, :], ALU.subtract))
                    dve.tensor_tensor(ev[:, :, 1, :], cv[:, :, 1, :], mid, ALU.subtract).then_inc(expo_done, 1)
                    return
                ev = e.rearrange("p (f c w) -> p f c w", f=2, c=4)
                cv = c4.rearrange("p (f c w) -> p f c w", f=2, c=4)

                def last(c):
                    return cv[:, :, c, CHUNK - 1:CHUNK].to_broadcast([P, 2, CHUNK])

                if n < len(LEVELS):
                    for c in (0, 2):
                        link(dve.tensor_tensor(ev[:, :, c, :], last(c), cv[:, :, c, :], ALU.subtract))
                    link(dve.tensor_copy(ev[:, :, 1, :], cv[:, :, 1, :]))
                    dve.tensor_copy(ev[:, :, 3, :], cv[:, :, 3, :]).then_inc(expo_done, 1)
                else:
                    link(dve.tensor_tensor(ev[:, :, 0, :], last(0), cv[:, :, 0, :], ALU.subtract))
                    link(dve.tensor_tensor(ev[:, :, 0, :], ev[:, :, 0, :], last(1), ALU.add))
                    link(dve.tensor_tensor(ev[:, :, 1, :], last(1), cv[:, :, 1, :], ALU.subtract))
                    link(dve.tensor_copy(ev[:, :, 2, :], cv[:, :, 2, :]))
                    dve.tensor_tensor(ev[:, :, 3, :], cv[:, :, 3, :], last(2), ALU.add).then_inc(expo_done, 1)

            def masked(n):
                for r in range(2):
                    name = f"lv{n}r{r}"
                    b = wait_full(dve, name)
                    if n == 0:
                        dve.wait_ge(att_zeroed, 1)
                    else:
                        wait_out(dve, f"lv{n - 1}r{r}")
                    dve.copy_predicated(attT_r[:, :, r, :], level_mask(n).unsqueeze(1).to_broadcast([P, 4, P]),
                                        b[:, :].rearrange("p (a s) -> p a s", a=4))\
                        .then_inc(freed(name), 1)

            def silu(t):
                dve.wait_ge(expr_done, t + 1)
                v = sg[:, t, :]
                link(dve.tensor_scalar(v, v, 1.0, None, ALU.add))
                link(dve.reciprocal(v, v))
                b = wait_full(dve, f"rg{t}")
                dve.tensor_tensor(v, v, b[:, :], ALU.mult).then_inc(freed(f"rg{t}"), 1)

            def mix(n, name):
                b = wait_full(dve, name)
                dve.wait_ge(mix_hi, n + 1)
                sl = (slice(None), slice(2 * n, 2 * n + 2), slice(None)) if n < 2 else \
                    (slice(None), slice(4, 8), slice((n - 2) * P, (n - 1) * P))
                hi_part = actA_hi[sl]
                dve.tensor_tensor(actA_lo[sl], b[:, :].rearrange("p (m s) -> p m s", m=hi_part.shape[1]),
                                  hi_part.bitcast(f32), ALU.subtract).then_inc(freed(name), 1)

            lo(MEM_UNIT, actB_lo[:].rearrange(flat), actB_hi[:].rearrange(flat))
            exponents(0)
            lo_half(6, 0)
            silu(0)
            exponents(1)
            lo_half(6, 1)
            silu(1)
            mix(0, "pv0")
            mix(1, "pv1")
            lo_half(7, 0)
            exponents(2)
            masked(0)
            lo_half(7, 1)
            exponents(3)
            masked(1)
            exponents(4)
            masked(2)
            lo_half(8, 0)
            exponents(5)
            masked(3)
            exponents(6)
            masked(4)
            lo_half(8, 1)
            exponents(7)
            masked(5)
            masked(6)
            lo_half(9, 0)
            lo_half(9, 1)

            wait_out(dve, "diag")
            b1 = FILL["av1"]
            dve.wait_ge(bank_full[b1[0]], b1[1] + 1)
            for t in range(2):
                b = bank[FILL[f"av{t}"][0]]
                for h in range(HG):
                    v = vg[:, t, h * DV:(h + 1) * DV]
                    k = 4 * t + 2 * (h // 2) + h % 2
                    i = dve.scalar_tensor_tensor(v, v, diag[:, k:k + 1], b[:, h * DV:(h + 1) * DV], ALU.mult, ALU.add)
                    i.then_inc(dve_link if h < HG - 1 else freed(f"av{t}"), 1)
                chain[0] += HG - 1
            for t in range(2):
                dve.wait_ge(ssq_done, 4 * t + 4)
                dve.wait_ge(dve_link, chain[0])
                dve.tensor_scalar(meansq[:, 4 * t:4 * t + 4], ssq[:, 4 * t:4 * t + 4], 1.0 / DV, RMS_EPS,
                                  ALU.mult, ALU.add).then_inc(meansq_done, 1)
            for t in range(2):
                dve.wait_ge(rms_done, t + 1)
                dve.wait_ge(gate_done, t + 1)
                for h in range(HG):
                    v = vg[:, t, h * DV:(h + 1) * DV]
                    dve.scalar_tensor_tensor(v, v, rms[:, 4 * t + h:4 * t + h + 1], sg[:, t, h * DV:(h + 1) * DV],
                                             ALU.mult, ALU.mult).then_inc(glao_done, 1)
            lo_half(10, 0)
            mix(2, "gt0")
            mix(3, "gt1")
            lo_half(10, 1)
            lo_half(11, 0)
            lo_half(11, 1)

            def layer_norm(n, t, banks):
                halves = [X[:, t, c * 512:(c + 1) * 512] for c in range(2)]
                for v, (b, full, free) in zip(halves, banks):
                    dve.wait_ge(full[0], full[1])
                    dve.scalar_tensor_tensor(v, v, ALPHA, b[:, :], ALU.mult, ALU.add).then_inc(free, 1)
                for c, (v, (b, full, free)) in enumerate(zip(halves, banks)):
                    dve.wait_ge(free, full[1])
                    dve.bn_stats(stats[:, n, t, c, :], v).then_inc(dve_link, 1)
                chain[0] += 2
                dve.wait_ge(dve_link, chain[0])
                link(dve.bn_aggr(mv[:, n, t, :], stats[:, n, t, :, :].rearrange("p c k -> p (c k)")))
                dve.tensor_scalar(vareps[:, n, t, :], mv[:, n, t, 1:2], LN_EPS, None, ALU.add).then_inc(var_done, 1)
                dve.wait_ge(ln_in[n], 32)
                for c, v in enumerate(halves):
                    dve.scalar_tensor_tensor(v, v, mv[:, n, t, 0:1], lng[:, c * 512:(c + 1) * 512],
                                             ALU.subtract, ALU.mult).then_inc(dve_link, 1)
                chain[0] += 2
                dve.wait_ge(rstd_done, 2 * n + t + 1)
                for c, v in enumerate(halves):
                    dve.wait_ge(dve_link, chain[0] - 1 + c)
                    dve.scalar_tensor_tensor(v, v, rstd[:, n, t, :], lnb[:, c * 512:(c + 1) * 512],
                                             ALU.mult, ALU.add).then_inc(ln_done, 1)

            def front_banks(t, name):
                return [(bank[FILL[f"{name}{t}{c}"][0]],
                         (bank_full[FILL[f"{name}{t}{c}"][0]], FILL[f"{name}{t}{c}"][1] + 1),
                         freed(f"{name}{t}{c}")) for c in range(2)]

            def xpose(n, name):
                t, c = divmod(n % 4, 2)
                b = wait_full(dve, name)
                dve.wait_ge(xT_hi, n + 1)
                sl = (slice(None), slice(4 * c, 4 * c + 4), slice(t * P, (t + 1) * P))
                dve.tensor_tensor(actA_lo[sl], b[:, :].rearrange("p (m s) -> p m s", m=4),
                                  actA_hi[sl].bitcast(f32), ALU.subtract).then_inc(freed(name), 1)

            dve.wait_ge(x_in, 16)
            layer_norm(0, 0, front_banks(0, "mo"))
            layer_norm(0, 1, front_banks(1, "mo"))
            xpose(0, "xt00")
            xpose(1, "xt01")
            lo_half(12, 0)
            xpose(2, "xt10")
            xpose(3, "xt11")

            def cmaxes(h):
                b = wait_full(dve, f"cs{h}")
                link(dve.tensor_reduce(cmax[:, 2 * h:2 * h + 2], b[:, :].rearrange("p (t m) -> p t m", t=2),
                                       AX.X, ALU.max))
                dve.tensor_scalar(cneg[:, 2 * h:2 * h + 2], cmax[:, 2 * h:2 * h + 2], -DX ** -0.5, None, ALU.mult)\
                    .then_inc(cneg_done, 1)

            def cnorm(h):
                dve.wait_ge(cexp_done, h + 1)
                wait_out(dve, f"cs{h}")
                link(dve.reciprocal(crec[:, 2 * h:2 * h + 2], csum[:, 2 * h:2 * h + 2]))
                for t in range(2):
                    v = cprobs[:, h, t, :]
                    dve.tensor_scalar(v, v, crec[:, 2 * h + t:2 * h + t + 1], None, ALU.mult).then_inc(cprob_done, 1)

            def cross(h):
                b = wait_full(dve, f"cpv{h}")
                dve.wait_ge(cross_hi, h + 1)
                dve.tensor_tensor(actB_lo[:, 2 * h:2 * h + 2, :], b[:, :].rearrange("p (m s) -> p m s", m=2),
                                  actB_hi[:, 2 * h:2 * h + 2, :].bitcast(f32), ALU.subtract)\
                    .then_inc(freed(f"cpv{h}"), 1)

            lo_half(13, 0)
            lo_half(13, 1)
            cmaxes(0)
            cnorm(0)
            lo_half(14, 0)
            cmaxes(1)
            cnorm(1)
            lo_half(14, 1)
            cmaxes(2)
            cnorm(2)
            cmaxes(3)
            cnorm(3)
            cross(0)
            cross(1)
            lo_half(15, 0)
            cross(2)
            lo_half(15, 1)
            cross(3)
            lo_half(C_FF1_0, 0)
            lo_half(C_FF1_0, 1)
            def square(g2, f, n):
                dve.wait_ge(bank_free[2 * g2 + f], n)
                dve.tensor_tensor(relu[:, f, :], relu[:, f, :], relu[:, f, :], ALU.mult).then_inc(sq_done, 1)

            def hid(g2, f, n):
                dve.wait_ge(hid_hi, n)
                sl = (slice(None), slice(4 * g2 + 2 * f, 4 * g2 + 2 * f + 2), slice(None))
                dve.tensor_tensor(actB_lo[sl], relu[:, f, :].rearrange("p (m s) -> p m s", m=2),
                                  actB_hi[sl].bitcast(f32), ALU.subtract).then_inc(hid_lo, 1)

            def lo_loop(k, half, i):
                c = C_LOOP + k
                u = unit(c, half)
                dve.wait_ge(hi_done, i * 8 + hi_count(u))
                dve.tensor_tensor(w_lo[:, c % 2, half, :], raw[:, u % RAW, :], w_hi[:, c % 2, half, :].bitcast(f32),
                                  ALU.subtract).then_inc(lo_done, 1)

            def first_square(t):
                wait_out(dve, f"hid{t}")
                dve.tensor_tensor(relu[:, t, :], relu[:, t, :], relu[:, t, :], ALU.mult).then_inc(sq_done, 1)

            def first_hid(t):
                b = wait_full(dve, f"ht{t}")
                dve.wait_ge(hid_hi, t + 1)
                dve.tensor_tensor(actB_lo[:, 0:4, t * P:(t + 1) * P], b[:, :].rearrange("p (m s) -> p m s", m=4),
                                  actB_hi[:, 0:4, t * P:(t + 1) * P].bitcast(f32), ALU.subtract)\
                    .then_inc(freed(f"ht{t}"), 1)

            layer_norm(1, 0, front_banks(0, "xo"))
            xpose(4, "yt00")
            xpose(5, "yt01")
            layer_norm(1, 1, front_banks(1, "xo"))
            xpose(6, "yt10")
            xpose(7, "yt11")
            lo_half(C_FF1_1, 0)
            first_square(0)
            lo_half(C_FF1_1, 1)
            first_square(1)
            lo_half(C_FF2_0, 0)
            first_hid(0)
            first_hid(1)
            square(1, 0, FF_BASE[2] + 1)
            lo_half(C_FF2_0, 1)
            hid(1, 0, 3)
            square(1, 1, FF_BASE[3] + 1)
            lo_half(C_LOOP, 0)
            hid(1, 1, 4)
            lo_half(C_LOOP, 1)
            with dve.Fori(0, G // 2 - 1) as i:
                for g in range(2):
                    n = 4 + 2 * g
                    lo_loop(2 * g + 1, 0, i)
                    square(g, 0, i + (FF_BASE[2 * g] + 1 + g))
                    lo_loop(2 * g + 1, 1, i)
                    hid(g, 0, i * 4 + (n + 1))
                    square(g, 1, i + (FF_BASE[2 * g + 1] + 1 + g))
                    lo_loop(2 * g + 2, 0, i)
                    hid(g, 1, i * 4 + (n + 2))
                    lo_loop(2 * g + 2, 1, i)
            for t in range(2):
                layer_norm(2, t, [(bank[4 + 2 * t + c], (bank_full[4 + 2 * t + c], FF_BASE[4 + 2 * t + c] + 1), bank_free[4 + 2 * t + c])
                                  for c in range(2)])

        @block.tensor
        def _(pe):
            def begin(name):
                b, before = FILL[name]
                if before:
                    pe.wait_ge(bank_free[b], before)
                return bank[b]

            def full(name):
                return bank_full[FILL[name][0]]

            def three(dst, stat, mov, start, stop):
                pe.matmul(dst, stat[0], mov[0], start=start, stop=False)
                pe.matmul(dst, stat[0], mov[1], start=False, stop=False)
                return pe.matmul(dst, stat[1], mov[0], start=False, stop=stop)

            def weight(c, k, a, b):
                return [w[:, c % 2, k // 4, (k % 4) * 512 + a:(k % 4) * 512 + b] for w in (w_hi, w_lo)]

            def weight_rows(c, k, a, b):
                return [w[:, c % 2, k // 2, (k % 2) * 1024 + a:(k % 2) * 1024 + b] for w in (w_hi, w_lo)]

            A, B = (actA_hi, actA_lo), (actB_hi, actB_lo)

            def features(c, step, src, name, ready=None):
                b = begin(name)
                for m in range(2):
                    for k in range(8):
                        if step == 0 and m == 0 and k % 4 == 0:
                            wait_lo(pe, unit(c, k // 4))
                            if ready is not None:
                                ready(k // 4)
                        i = three(b[:, m * S:(m + 1) * S], weight(c, k, (2 * step + m) * P, (2 * step + m + 1) * P),
                                  [a[:, k, :] for a in src], k == 0, k == 7)
                i.then_inc(full(name), 1)

            def tokens(c, t, src, name, midway=None):
                b = begin(name)
                for k in range(8):
                    if t == 0 and k % 4 == 0:
                        wait_lo(pe, unit(c, k // 4))
                    if k == 4 and midway is not None:
                        midway()
                    i = three(b[:, :], [a[:, k, t * P:(t + 1) * P] for a in src], weight(c, k, 0, 512), k == 0, k == 7)
                i.then_inc(full(name), 1)

            def rows(c, part, src, names, base, after=None):
                for t in range(2):
                    for n in range(2):
                        b = begin(names[2 * t + n]) if part == 0 else bank[FILL[names[2 * t + n]][0]]
                        for k in range(4):
                            if t == 0 and n == 0 and k % 2 == 0:
                                wait_lo(pe, unit(c, k // 2))
                            i = three(b[:, :], [a[:, base + k, t * P:(t + 1) * P] for a in src],
                                      weight_rows(c, k, n * 512, (n + 1) * 512), part == 0 and k == 0,
                                      part == 1 and k == 3)
                        if part == 1:
                            i.then_inc(full(names[2 * t + n]), 1)
                        elif t == 1 and n == 1:
                            i.then_inc(rows_used, 1)
                        if after is not None:
                            after(2 * t + n)

            b = begin("glr")
            pe.wait_ge(wglr_in, 16)
            for k in range(8):
                if k % 4 == 0:
                    pe.wait_ge(early_in[k // 4], 16)
                i = pe.matmul(b[0:RANK, 0:S], wglr[:, k, :], raw[:, 0, k * S:(k + 1) * S], start=k == 0, stop=k == 7)
            i.then_inc(full("glr"), 1)
            banks = [begin("qg"), begin("kg")]
            for piece in range(4):
                if piece % 2 == 0:
                    wait_lo(pe, 0, piece // 2)
                wait_lo(pe, 1 + piece // 2, piece % 2)
                for m in range(4):
                    dst = banks[m // 2][:, (m % 2) * S:(m % 2 + 1) * S]
                    for k in range(2 * piece, 2 * piece + 2):
                        stat, mov = weight(0, k, m * P, (m + 1) * P), (actA_hi[:, k, :], actA_lo[:, k, :])
                        pe.matmul(dst, stat[0], mov[0], start=k == 0 and m % 2 == 0, stop=False, skip_group_check=True)
                        pe.matmul(dst, stat[0], mov[1], start=False, stop=False, skip_group_check=True)
                        i = pe.matmul(dst, stat[1], mov[0], start=False, stop=k == 7, skip_group_check=True)
                    if piece == 3 and m % 2 == 1:
                        i.then_inc(full(("qg", "kg")[m // 2]), 1)
            b = begin("z")
            wait_out(pe, "glr")
            pe.wait_ge(wgu_in, 16)
            for f in range(2):
                i = pe.matmul(b[:, f * S:(f + 1) * S], wgu[:, f * P:(f + 1) * P], glrT[:], start=True, stop=True)
            i.then_inc(full("z"), 1)
            features(1, 0, A, "qa0")
            features(1, 1, A, "qa1")
            features(2, 0, A, "ka0")
            features(2, 1, A, "ka1")

            def score(h):
                b = begin(f"score{h}")
                r = slice(64 * (h % 2), 64 * (h % 2) + 64)
                pe.matmul(b[:, 0:P], qaT[r, h // 2, 0:P], kaT[r, h // 2, 0:P], start=True, stop=True)
                pe.matmul(b[:, P:3 * P], qaT[r, h // 2, P:S], kaT[r, h // 2, :], start=True, stop=True)\
                    .then_inc(full(f"score{h}"), 1)

            def transpose_probs(h):
                b = begin(f"pt{h}")
                pe.wait_ge(prob_done, 2 * h + 2)
                for a in range(3):
                    i = pe.transpose(b[:, a * P:(a + 1) * P], probs[:, h * 384 + a * P:h * 384 + (a + 1) * P], ident)
                i.then_inc(full(f"pt{h}"), 1)

            tokens(3, 0, A, "va0")
            for name in ("qa0", "qa1", "ka0", "ka1"):
                wait_out(pe, name)
            for h in range(4):
                score(h)
            tokens(3, 1, A, "va1")
            tokens(4, 0, A, "vg0")
            for h in range(4, 8):
                score(h)
            tokens(4, 1, A, "vg1")
            for h in range(4):
                transpose_probs(h)
            tokens(5, 0, A, "rg0")
            for h in range(4, 8):
                transpose_probs(h)
            tokens(5, 1, A, "rg1")
            for name in ["va0", "va1"] + [f"pt{h}" for h in range(HA)]:
                wait_out(pe, name)
            for n in range(2):
                b = begin(f"pv{n}")
                for h in range(4 * n, 4 * n + 4):
                    r = slice(64 * (h % 2), 64 * (h % 2) + 64)
                    c = (h // 2 - 2 * n) * S
                    pe.matmul(b[r, c:c + S], va[:, 0, h * DA:(h + 1) * DA], probsT[:, h * 384:h * 384 + S],
                              start=True, stop=False)
                    i = pe.matmul(b[r, c + P:c + S], va[:, 1, h * DA:(h + 1) * DA],
                                  probsT[:, h * 384 + S:h * 384 + 384], start=False, stop=True)
                i.then_inc(full(f"pv{n}"), 1)
            b = begin("diag")
            pe.wait_ge(qkdiag_done, 1)
            pe.wait_ge(headsel_done, 2)
            for t in range(2):
                for f in range(2):
                    k = 4 * t + 2 * f
                    i = pe.matmul(b[:, k:k + 2], qkdiag[:, f * S + t * P:f * S + (t + 1) * P], headsel[:],
                                  start=True, stop=True)
            i.then_inc(full("diag"), 1)

            def level(n):
                pe.wait_ge(lev_done, 2 * n + 2)
                banks = [begin(f"lv{n}r{r}") for r in range(2)]
                for a in range(4):
                    for r in range(2):
                        v = lev[n % 2][64 * r:64 * r + 64, (a % 2) * S + (a // 2) * P:(a % 2) * S + (a // 2 + 1) * P]
                        i = pe.matmul(banks[r][:, a * P:(a + 1) * P], v, v, start=True, stop=True)
                        if a == 3:
                            i.then_inc(full(f"lv{n}r{r}"), 1)

            wait_lo(pe, MEM_UNIT)
            features(6, 0, B, "xk0")
            features(6, 1, B, "xk1")
            level(0)
            level(1)
            features(7, 0, B, "xk2")
            level(2)
            level(3)
            features(7, 1, B, "xk3")
            level(4)
            level(5)
            tokens(8, 0, B, "xv00")
            level(6)
            pe.wait_ge(lev_done, 16)
            banks = [begin("off0"), begin("off1")]
            for f in range(2):
                for r in range(2):
                    v = lev[1][64 * r:64 * r + 64, f * S:(f + 1) * S]
                    i = pe.matmul(banks[r][:, f * P:(f + 1) * P], v[:, 0:P], v[:, P:S], start=True, stop=True)
                    if f == 1:
                        i.then_inc(full(f"off{r}"), 1)
            tokens(8, 1, B, "xv01")
            for name in ("vg0", "vg1", "off0", "off1", "lv6r0", "lv6r1"):
                wait_out(pe, name)
            for t in range(2):
                b = begin(f"av{t}")
                for h in range(HG):
                    c = slice(h * DV, (h + 1) * DV)
                    if t == 1:
                        pe.matmul(b[:, c], attoff[:, h, :], vg[:, 0, c], start=True, stop=False)
                    i = pe.matmul(b[:, c], attT[:, t, h, :], vg[:, t, c], start=t == 0, stop=True)
                i.then_inc(full(f"av{t}"), 1)
            mo = ["mo00", "mo01", "mo10", "mo11"]
            wait_out(pe, "pv0")
            wait_out(pe, "pv1")

            def transpose_gla(n):
                if n == 2:
                    for t in range(2):
                        b = begin(f"gt{t}")
                        pe.wait_ge(glao_done, 4 * t + 4)
                        for h in range(HG):
                            i = pe.transpose(b[:, h * P:(h + 1) * P], vg[:, t, h * DV:(h + 1) * DV], ident)
                        i.then_inc(full(f"gt{t}"), 1)

            rows(9, 0, A, mo, 0, after=transpose_gla)
            wait_out(pe, "gt0")
            wait_out(pe, "gt1")
            rows(10, 1, A, mo, 4)

            def transpose_x(n, t, name):
                for c in range(2):
                    b = begin(f"{name}{t}{c}")
                    pe.wait_ge(ln_done, 4 * n + 2 * t + c + 1)
                    for m in range(4):
                        i = pe.transpose(b[:, m * P:(m + 1) * P], X[:, t, (4 * c + m) * P:(4 * c + m + 1) * P], ident)
                    i.then_inc(full(f"{name}{t}{c}"), 1)

            tokens(11, 0, B, "xv10")
            transpose_x(0, 0, "xt")
            tokens(11, 1, B, "xv11", midway=lambda: transpose_x(0, 1, "xt"))

            def cscore(h):
                b = begin(f"cs{h}")
                wait_out(pe, f"xq{h}")
                for t in range(2):
                    for d in range(2):
                        i = pe.matmul(b[:, t * S:(t + 1) * S], cqT[:, 2 * h + d, t * P:(t + 1) * P],
                                      memkT[:, 2 * h + d, :], start=d == 0, stop=d == 1)
                i.then_inc(full(f"cs{h}"), 1)

            def ctranspose(h):
                b = begin(f"cpt{h}")
                pe.wait_ge(cprob_done, 2 * h + 2)
                for m in range(2):
                    for t in range(2):
                        i = pe.transpose(b[:, m * S + t * P:m * S + (t + 1) * P], cprobs[:, h, t, m * P:(m + 1) * P], ident)
                i.then_inc(full(f"cpt{h}"), 1)

            def cvalues(h):
                b = begin(f"cpv{h}")
                wait_out(pe, f"cpt{h}")
                for d in range(2):
                    for m in range(2):
                        i = pe.matmul(b[:, d * S:(d + 1) * S], memv[:, m, h * DX + d * P:h * DX + (d + 1) * P],
                                      cprobsT[:, h, m, :], start=m == 0, stop=m == 1)
                i.then_inc(full(f"cpv{h}"), 1)


            def normed(name):
                return lambda c: [wait_out(pe, f"{name}{t}{c}") for t in range(2)]

            features(12, 0, A, "xq0", ready=normed("xt"))
            features(12, 1, A, "xq1")
            for n in range(4):
                wait_out(pe, f"xk{n}")
            cscore(0)
            features(13, 0, A, "xq2")
            cscore(1)
            features(13, 1, A, "xq3")
            cscore(2)
            ctranspose(0)
            ctranspose(1)
            cscore(3)
            for name in ("xv00", "xv01", "xv10", "xv11"):
                wait_out(pe, name)
            cvalues(0)
            cvalues(1)
            ctranspose(2)
            cvalues(2)
            xo = ["xo00", "xo01", "xo10", "xo11"]
            wait_out(pe, "cpv0")
            wait_out(pe, "cpv1")
            rows(14, 0, B, xo, 0, after=lambda n: (ctranspose, cvalues)[n](3) if n < 2 else None)
            wait_out(pe, "cpv2")
            wait_out(pe, "cpv3")
            rows(15, 1, B, xo, 4)
            transpose_x(1, 0, "yt")
            wait_out(pe, "yt00")
            wait_out(pe, "yt01")
            tokens(C_FF1_0, 0, A, "hid0", midway=lambda: transpose_x(1, 1, "yt"))
            wait_out(pe, "yt10")
            wait_out(pe, "yt11")
            tokens(C_FF1_0, 1, A, "hid1")

            def transpose_hidden():
                for t in range(2):
                    b = begin(f"ht{t}")
                    pe.wait_ge(sq_done, t + 1)
                    for m in range(4):
                        i = pe.transpose(b[:, m * P:(m + 1) * P], relu[:, t, m * P:(m + 1) * P], ident)
                    i.then_inc(full(f"ht{t}"), 1)

            def ff1(g2, par, lo_need, free_need, between=None):
                for f in range(2):
                    b = bank[2 * g2 + f]
                    pe.wait_ge(bank_free[2 * g2 + f], free_need[f])
                    for m in range(2):
                        for k in range(8):
                            if f == 0 and m == 0 and k % 4 == 0:
                                pe.wait_ge(lo_done, lo_need[k // 4])
                            i = three(b[:, m * S:(m + 1) * S],
                                      [w[:, par, k // 4, (k % 4) * 512 + (2 * f + m) * P:(k % 4) * 512 + (2 * f + m + 1) * P]
                                       for w in (w_hi, w_lo)], [a[:, k, :] for a in A], k == 0, k == 7)
                    i.then_inc(bank_full[2 * g2 + f], 1)
                    if f == 0 and between is not None:
                        between()

            def ff2(g2, par, lo_need, hid_need=None, first=False, last=False):
                if not first:
                    pe.wait_ge(hid_lo, hid_need)
                for t in range(2):
                    for n in range(2):
                        b = bank[4 + 2 * t + n]
                        if first:
                            pe.wait_ge(bank_free[4 + 2 * t + n], FF_BASE[4 + 2 * t + n])
                        for k in range(4):
                            if t == 0 and n == 0 and k % 2 == 0:
                                pe.wait_ge(lo_done, lo_need[k // 2])
                            i = three(b[:, :], [a[:, 4 * g2 + k, t * P:(t + 1) * P] for a in B],
                                      [w[:, par, k // 2, (k % 2) * 1024 + n * 512:(k % 2) * 1024 + (n + 1) * 512]
                                       for w in (w_hi, w_lo)], first and k == 0, last and k == 3)
                        if last:
                            i.then_inc(bank_full[4 + 2 * t + n], 1)
                if not last:
                    i.then_inc(rows_used, 1)

            def need(c):
                return [lo_count(unit(c, half)) for half in range(2)]

            ff1(1, C_FF1_1 % 2, need(C_FF1_1), [FF_BASE[2], FF_BASE[3]], between=transpose_hidden)
            ff2(0, C_FF2_0 % 2, need(C_FF2_0), first=True)
            with pe.Fori(0, G // 2 - 1) as i:
                for g in range(2):
                    c = C_LOOP + 2 * g
                    ff1(g, c % 2, [i * 8 + n for n in need(c)],
                        [i + (FF_BASE[2 * g + f] + g) for f in range(2)])
                    ff2(1 - g, (c + 1) % 2, [i * 8 + n for n in need(c + 1)], i * 4 + (2 + 2 * g))
            ff2(1, C_LAST % 2, need(C_LAST), 2 * G - 2, last=True)


def kernel(**inputs):
    import concourse.bacc as bacc
    from concourse.bass_utils import run_bass_kernel_spmd

    names = ["x", "xT", "memT", "w_in", "w_gate_up", "b_gate", "gla_norm_g", "w_mix_o", "ln1_g", "ln1_b",
             "w_xq", "w_xkv", "w_xo", "ln2_g", "ln2_b", "w_ff1", "w_ff2", "ln3_g", "ln3_b"]
    laid = {n: np.asarray(a)[0] for n, a in inputs.items()}
    laid["b_gate"] = laid["b_gate"].reshape(2, P).T
    laid["xT"], laid["memT"] = laid["x"].T, laid["mem"].T
    arrays = {f"in_{n}": np.ascontiguousarray(laid[n]) for n in names}
    arrays["in_consts"] = shape_constants()
    nc = bacc.Bacc("TRN2", target_bir_lowering=False, num_devices=1)
    args = {n: nc.dram_tensor(f"in_{n}", arrays[f"in_{n}"].shape, mybir.dt.float32, kind="ExternalInput").ap()
            for n in names + ["consts"]}
    out = nc.dram_tensor("out", (S, D), mybir.dt.float32, kind="ExternalOutput").ap()
    build(nc, out=out, **args)
    result = run_bass_kernel_spmd(nc, [arrays], core_ids=[0]).results[0]["out"]
    return result.reshape(1, S, D)
```

```python
from contextlib import ExitStack

import numpy as np
import concourse.bass as bass
from concourse import mybir

D = 1024
S = 256
P = 128
HA, DA = 8, 64
HG, DK, DV = 4, 64, 128
CHUNK = 64
RANK = 16
HX, DX = 4, 256
F = 4 * D
GATE_TEMP = 16.0
LN_EPS, RMS_EPS = 1e-5, 1e-6
ALPHA = 2.0 ** 0.25
QA, KA, VA, QG, KG, VG, RG, GL = 0, 512, 1024, 1536, 1792, 2048, 2560, 3072
LEVELS = [64, 32, 16, 8, 4, 2, 1]
SLOPES = [2.0 ** (-8.0 * (h + 1) / HA) for h in range(HA)]
LN3_COLS = 704
MASKED = -1e36
C_ID, C_DIST, C_MASK = 0, P, P + 3 * P
N_CONST = C_MASK + len(LEVELS) * P
WARM_UP = 2
G = 8


def shape_constants():
    c = np.zeros((P, N_CONST), np.float32)
    c[:, C_ID:C_ID + P] = np.eye(P)
    q, k = np.arange(P)[:, None], np.arange(S)[None, :]
    c[:, C_DIST:C_DIST + P] = np.where(k[:, :P] <= q, k[:, :P] - q, MASKED)
    c[:, C_DIST + P:C_DIST + 3 * P] = np.where(k <= q + P, k - q - P, MASKED)
    s, t = np.arange(P)[:, None], np.arange(P)[None, :]
    for n, w in enumerate(LEVELS):
        own = (s // (2 * w) == t // (2 * w)) & (s % (2 * w) < w) & (t % (2 * w) >= w)
        c[:, C_MASK + n * P:C_MASK + (n + 1) * P] = own
    return c


CHUNKS = [
    ("w_in", "cols", QG), ("w_in", "cols", QA), ("w_in", "cols", KA), ("w_in", "cols", VA),
    ("w_in", "cols", VG), ("w_in", "cols", RG),
    ("w_xkv", "cols", 0), ("w_xkv", "cols", 512), ("w_xkv", "cols", 1024),
    ("w_mix_o", "rows", 0), ("w_mix_o", "rows", 512),
    ("w_xkv", "cols", 1536),
    ("w_xq", "cols", 0), ("w_xq", "cols", 512),
    ("w_xo", "rows", 0), ("w_xo", "rows", 512),
]
N_FRONT = len(CHUNKS)
C_FF1_0, C_FF1_1, C_FF2_0, C_LOOP = N_FRONT, N_FRONT + 1, N_FRONT + 2, N_FRONT + 3
C_LAST = C_LOOP + 2 * (G - 2)
MEM_CHUNK = 6


def unit(chunk, half):
    return 1 + 2 * chunk + half + (chunk >= MEM_CHUNK)


MEM_UNIT = unit(MEM_CHUNK, 0) - 1
RAW = 4
POOL_UNITS = [unit(12, 1), unit(C_FF1_0, 1)]
EARLY = 3


def hi_count(u):
    return u + 1 - EARLY


def lo_count(u):
    return u + 1 - EARLY - sum(v <= u for v in POOL_UNITS)


def raw_count(u):
    return 16 * (u // RAW + (u % RAW >= EARLY))


FRONT_FILLS = (
    [("glr", 4), ("qg", 0), ("kg", 1), ("z", 5), ("qa0", 2), ("qa1", 3), ("ka0", 0), ("ka1", 1), ("va0", 2)]
    + [(f"score{h}", 4 + h) for h in range(4)] + [("va1", 3), ("vg0", 0)]
    + [(f"score{h}", h) for h in range(4, 8)] + [("vg1", 1)]
    + [(f"pt{h}", 4 + h) for h in range(4)] + [("rg0", 2)] + [(f"pt{h}", h) for h in range(4, 8)]
    + [("rg1", 3), ("pv0", 4), ("pv1", 5), ("diag", 6), ("xk0", 0), ("xk1", 1)]
    + [("lv0", 4), ("lv1", 5), ("xk2", 2), ("lv2", 6), ("lv3", 7), ("xk3", 3), ("lv4", 4), ("lv5", 5),
       ("xv00", 0), ("lv6", 6), ("off0", 7), ("off1", 4), ("xv01", 1), ("av0", 5), ("av1", 6)]
    + [("mo00", 2), ("mo01", 3), ("mo10", 0), ("gt0", 7), ("gt1", 4), ("mo11", 1)]
    + [("xv10", 2), ("xt00", 4), ("xt01", 5), ("xv11", 3), ("xt10", 6), ("xt11", 7)]
    + [("xq0", 0), ("xq1", 1), ("cs0", 4), ("xq2", 2), ("cs1", 5), ("cpt0", 4), ("xq3", 3), ("cs2", 6)]
    + [("cpt1", 5), ("cpv0", 4), ("cs3", 7), ("cpv1", 5), ("cpt2", 6)]
    + [("xo00", 0), ("cpv2", 6), ("cpt3", 7), ("xo01", 1), ("cpv3", 7), ("xo10", 2), ("xo11", 3)]
    + [("yt00", 4), ("yt01", 5), ("hid0", 0), ("yt10", 6), ("yt11", 7), ("hid1", 1), ("ht0", 4), ("ht1", 5)]
)
FILL = {}
for _name, _bank in FRONT_FILLS:
    FILL[_name] = (_bank, sum(b == _bank for b, _ in FILL.values()))
CHUNK_END = {0: "kg", 1: "qa1", 2: "ka1", 3: "va1", 4: "vg1", 5: "rg1", 6: "xk1", 7: "xk3", 8: "xv01",
             10: "mo11", 11: "xv11", 12: "xq1", 13: "xq3", 15: "xo11", C_FF1_0: "hid1"}
ROWS_END = {9: 1, 14: 2, C_FF2_0: 3}
FF_BASE = [sum(b == bank for b, _ in FILL.values()) for bank in range(8)]


def build(nc, x, xT, memT, w_in, w_gate_up, b_gate, gla_norm_g, w_mix_o, ln1_g, ln1_b, w_xq, w_xkv,
          w_xo, ln2_g, ln2_b, w_ff1, w_ff2, ln3_g, ln3_b, consts, out):
    f32, f32r, i32 = mybir.dt.float32, mybir.dt.float32r, mybir.dt.int32
    ALU, ACT, AX = mybir.AluOpType, mybir.ActivationFunctionType, mybir.AxisListType
    weights = {"w_in": w_in, "w_xkv": w_xkv, "w_mix_o": w_mix_o, "w_xq": w_xq, "w_xo": w_xo}
    ln_rows = [(ln1_g, ln1_b), (ln2_g, ln2_b), (ln3_g, ln3_b)]

    ctx = ExitStack()
    with ctx:
        def sb(name, shape, dt=f32):
            return ctx.enter_context(nc.sbuf_tensor(name, shape, dt))

        def sem(name):
            return ctx.enter_context(nc.semaphore(name))

        raw = sb("raw", [P, RAW, 2048])
        w_hi = sb("w_hi", [P, 2, 2, 2048], f32r)
        w_lo = sb("w_lo", [P, 2, 2, 2048], f32r)
        actA_hi = sb("actA_hi", [P, 8, S], f32r)
        actA_lo = sb("actA_lo", [P, 8, S], f32r)
        actB_hi = sb("actB_hi", [P, 8, S], f32r)
        actB_lo = sb("actB_lo", [P, 8, S], f32r)
        X = sb("X", [P, 2, D])
        wglr = sb("wglr", [P, 8, RANK])
        wgu = sb("wgu", [RANK, 256])
        glrT = sb("glrT", [RANK, S])
        bgate = sb("bgate", [P, 2])
        headsel = sb("headsel", [P, 2])
        gnorm = sb("gnorm", [P, DV])
        negmax = sb("negmax", [P, 2 * HA])
        sums = sb("sums", [P, 2 * HA])
        rsums = sb("rsums", [P, 2 * HA])
        diag = sb("diag", [P, 8])
        ssq = sb("ssq", [P, 8])
        meansq = sb("meansq", [P, 8])
        rms = sb("rms", [P, 8])
        minus_half = sb("minus_half", [P, 8])
        stats = sb("stats", [P, 3, 2, 2, 6])
        mv = sb("mv", [P, 3, 2, 2])
        vareps = sb("vareps", [P, 3, 2, 1])
        rstd = sb("rstd", [P, 3, 2, 1])
        cmax = sb("cmax", [P, 2 * HX])
        cneg = sb("cneg", [P, 2 * HX])
        csum = sb("csum", [P, 2 * HX])
        crec = sb("crec", [P, 2 * HX])

        columns = {"const": N_CONST,
                   "probs": HA * 384,
                   "probsT": HA * 384,
                   "qk": 2048,
                   "values": 2048,
                   "gla": 2560,
                   "att": 1536,
                   "reset": 512,
                   "qkdiag": 512}
        with ExitStack() as first:
            const, probs, probsT, qk, values, gla, att, reset, qkdiag = (
                first.enter_context(nc.sbuf_tensor(name, [P, n], f32)) for name, n in columns.items())
        again = sb("again", [P, sum(columns.values())], f32r)
        begins = dict(zip(columns, np.cumsum([0] + list(columns.values())).tolist()))

        def shared(name, a, b):
            return again[:, begins[name] + a:begins[name] + b]

        ident = const[:, C_ID:C_ID + P]
        qaT = qk[:, 0:1024].rearrange("p (m s) -> p m s", m=4)
        kaT = qk[:, 1024:2048].rearrange("p (m s) -> p m s", m=4)
        expo = [qk[:, 512 * b:512 * b + 512] for b in range(2)]
        lev = [qk[:, 1024 + 512 * b:1536 + 512 * b] for b in range(2)]
        va = values[:, 0:1024].rearrange("p (t n) -> p t n", t=2)
        vg = values[:, 1024:2048].rearrange("p (t n) -> p t n", t=2)
        sg = gla[:, 0:1024].rearrange("p (t n) -> p t n", t=2)
        qgT, kgT, cum = gla[:, 1024:1536], gla[:, 1536:2048], gla[:, 2048:2560]
        attT = att[:, 0:1024].rearrange("p (t h s) -> p t h s", t=2, h=HG)
        attoff = att[:, 1024:1536].rearrange("p (h s) -> p h s", h=HG)
        zlin, zabs = att[:, 0:512], att[:, 512:1024]
        memkT = probs[:, 0:2048].rearrange("p (m s) -> p m s", m=8)
        lng = probs[:, 2048:3072]
        memv = probsT[:, 0:2048].rearrange("p (t n) -> p t n", t=2)
        lnb = probsT[:, 2048:3072]
        cprobs = qk[:, :].rearrange("p (h t m) -> p h t m", h=HX, t=2)
        mem_hi_pieces = [shared("att", 0, 512), shared("att", 512, 1024), shared("att", 1024, 1536),
                         shared("reset", 0, 512), shared("qkdiag", 0, 512), shared("gla", 2048, 2560),
                         shared("const", C_DIST, C_DIST + 512), shared("const", C_DIST + 512, C_DIST + 1024)]
        mem_pieces = [memkT[:, 2 * h:2 * h + 2, :].rearrange("p m s -> p (m s)") for h in range(HX)] \
            + [memv[:, m, c * 512:(c + 1) * 512] for c in range(2) for m in range(2)]
        mem_lo_pieces = [shared("probs", 512 * h, 512 * h + 512) for h in range(HX)] \
            + [shared("probsT", m * D + c * 512, m * D + (c + 1) * 512) for c in range(2) for m in range(2)]
        cq_hi, cq_lo = shared("values", 0, 2048).rearrange("p (m s) -> p m s", m=8), actB_lo
        cprobsT_hi = shared("gla", 0, 2048).rearrange("p (h m s) -> p h m s", h=HX, m=2)
        cprobsT_lo = actB_hi[:].rearrange("p (h m) s -> p h m s", h=HX)

        yT_half = [qk[:, t * 512:(t + 1) * 512].rearrange("p (m s) -> p m s", m=4) for t in range(2)]
        relu = att[:, 0:1024].rearrange("p (b n) -> p b n", b=2)

        lev_q = [v[:, :].rearrange("p (a r s) -> p a r s", a=4, r=2) for v in (reset, qkdiag)]

        def level_mask(n):
            return const[:, C_MASK + n * P:C_MASK + (n + 1) * P].bitcast(i32)

        bank = [ctx.enter_context(nc.psum_tensor(f"bank{b}", [P, 512], f32)) for b in range(8)]

        bank_full = [sem(f"bank_full{b}") for b in range(8)]
        bank_free = [sem(f"bank_free{b}") for b in range(8)]
        raw_in = [sem(f"raw_in{r}") for r in range(RAW)]
        hi_done = sem("hi_done")
        lo_done = sem("lo_done")
        early_in = [sem(f"early_in{n}") for n in range(2 * EARLY)]
        early_hi, early_lo = sem("early_hi"), sem("early_lo")
        pool_lo = sem("pool_lo")
        rows_used = sem("rows_used")
        wglr_in, wgu_in, const_in, small_in, x_in = map(sem, ("wglr_in", "wgu_in", "const_in", "small_in", "x_in"))
        ln_in = [sem(f"ln_in{n}") for n in range(3)]
        out_done = sem("out_done")
        dve_link, act_link, pool_link = sem("dve_link"), sem("act_link"), sem("pool_link")
        zabs_done, softplus_done, cum_done = map(sem, ("zabs_done", "softplus_done", "cum_done"))
        reset_done, att_zeroed, headsel_done, half_done = map(sem, ("reset_done", "att_zeroed", "headsel_done", "half_done"))
        lev_q_zeroed = sem("lev_q_zeroed")
        bias_done, score_done, exp_done, prob_done = map(sem, ("bias_done", "score_done", "exp_done", "prob_done"))
        mix_hi = sem("mix_hi")
        expr_done, gate_done = sem("expr_done"), sem("gate_done")
        expo_done, decay_done, lev_done, qkdiag_done = map(sem, ("expo_done", "decay_done", "lev_done", "qkdiag_done"))
        ssq_done, meansq_done, rms_done, glao_done = map(sem, ("ssq_done", "meansq_done", "rms_done", "glao_done"))
        var_done, rstd_done, ln_done = map(sem, ("var_done", "rstd_done", "ln_done"))
        centred, rest_done = sem("centred"), sem("rest_done")
        yT_lo = sem("yT_lo")
        xT_hi = sem("xT_hi")
        cneg_done, cexp_done, cprob_done = map(sem, ("cneg_done", "cexp_done", "cprob_done"))
        mem_hi, mem_lo = sem("mem_hi"), sem("mem_lo")
        cq_hi_done, cT_hi_done = sem("cq_hi_done"), sem("cT_hi_done")
        cross_hi = sem("cross_hi")
        sq_done, hid_hi, hid_lo = map(sem, ("sq_done", "hid_hi", "hid_lo"))

        def wait_full(eng, name):
            b, before = FILL[name]
            eng.wait_ge(bank_full[b], before + 1)
            return bank[b]

        def freed(name):
            return bank_free[FILL[name][0]]

        def wait_out(eng, name):
            b, before = FILL[name]
            eng.wait_ge(bank_free[b], before + 1)

        def wait_lo(eng, u, piece=1):
            if u < EARLY:
                eng.wait_ge(early_lo, 2 * u + piece + 1)
            elif u in POOL_UNITS:
                eng.wait_ge(pool_lo, POOL_UNITS.index(u) + 1)
            else:
                eng.wait_ge(lo_done, lo_count(u))

        def early(act_part, w_part):
            return [act_part[:].rearrange("p a s -> p (a s)"), w_part[:, 0, 0, :], w_part[:, 0, 1, :]]

        def half_view(u):
            return raw[:, u % RAW, :]

        block = ctx.enter_context(nc.Block())

        @block.sync
        def _(sp):
            def chunk_source(c, half):
                name, kind, at = CHUNKS[c]
                w = weights[name]
                if kind == "cols":
                    return w[half * 512:(half + 1) * 512, at:at + 512].rearrange("(a p) n -> p a n", p=P)
                return w[at + half * 256:at + (half + 1) * 256, :].rearrange("(a p) n -> p a n", p=P)

            def load(u, src, tiles):
                if u >= RAW:
                    wait_lo(sp, u - RAW)
                if u == RAW:
                    sp.wait_ge(bank_full[FILL["glr"][0]], 1)
                sp.dma_start(half_view(u).rearrange("p (a n) -> p a n", a=tiles), src).then_inc(raw_in[u % RAW], 16)

            def load_chunk(c):
                for half in range(2):
                    load(unit(c, half), chunk_source(c, half), 4 if CHUNKS[c][1] == "cols" else 2)

            def load_ln(n):
                g, b = ln_rows[n]
                sp.dma_start(lng, g.partition_broadcast(P)).then_inc(ln_in[n], 16)
                sp.dma_start(lnb, b.partition_broadcast(P)).then_inc(ln_in[n], 16)

            for u in range(EARLY):
                src = xT.rearrange("(a p) s -> p a s", p=P) if u == 0 else chunk_source(0, u - 1)
                tiles = src.shape[1] // 2
                for piece in range(2):
                    sp.dma_start(raw[:, u, piece * 1024:(piece + 1) * 1024].rearrange("p (a n) -> p a n", a=tiles),
                                 src[:, piece * tiles:(piece + 1) * tiles, :]).then_inc(early_in[2 * u + piece], 16)
            load_chunk(1)
            sp.dma_start(const[:], consts).then_inc(const_in, 16)
            for c in range(2, 6):
                load_chunk(c)
            load(MEM_UNIT, memT.rearrange("(a p) s -> p a s", p=P), 8)
            load_chunk(6)
            sp.dma_start(X[:], x.rearrange("(t p) n -> p t n", p=P)).then_inc(x_in, 16)
            load_chunk(7)
            load_chunk(8)
            load_chunk(9)
            load_chunk(10)
            sp.wait_ge(bank_full[FILL["pv1"][0]], FILL["pv1"][1] + 1)
            load_ln(0)
            for c in range(11, N_FRONT):
                load_chunk(c)
            ff1_src = [w_ff1[half * 512:(half + 1) * 512, :].rearrange("(a p) n -> p a n", p=P) for half in range(2)]

            def load_ff1(u, g):
                sp.dma_start(raw[:, u % RAW, :].rearrange("p (a n) -> p a n", a=4),
                             ff1_src[u % 2][:, :, bass.ds(g * 512, 512)]).then_inc(raw_in[u % RAW], 16)

            def load_ff2(u, g):
                sp.dma_start(raw[:, u % RAW, :].rearrange("p (a n) -> p a n", a=2),
                             w_ff2[bass.ds(g * 512 + (u % 2) * 256, 256), :].rearrange("(a p) n -> p a n", p=P))\
                    .then_inc(raw_in[u % RAW], 16)

            for c, source, g in ((C_FF1_0, load_ff1, 0), (C_FF1_1, load_ff1, 1), (C_FF2_0, load_ff2, 0)):
                for half in range(2):
                    u = unit(c, half)
                    wait_lo(sp, u - RAW)
                    source(u, g)
                if c == C_FF1_0:
                    sp.wait_ge(ln_done, 4)
                    load_ln(1)
            u0 = unit(C_LOOP, 0)
            with sp.Fori(0, G // 2 - 1) as i:
                for n in range(4):
                    for half in range(2):
                        k = 2 * n + half
                        sp.wait_ge(lo_done, i * 8 + lo_count(u0 + k - RAW))
                        if n % 2 == 0:
                            load_ff1(u0 + k, i * 2 + 2 + n // 2)
                        else:
                            load_ff2(u0 + k, i * 2 + 1 + n // 2)
            for half in range(2):
                u = unit(C_LAST, half)
                wait_lo(sp, u - RAW)
                load_ff2(u, G - 1)
            sp.wait_ge(ln_done, 8)
            load_ln(2)
            for t in range(2):
                half = (LN3_COLS, D)[t] // 2
                for n in range(2):
                    sp.wait_ge(ln_done, 8 + 2 * t + n + 1)
                    cols = slice(n * half, (n + 1) * half)
                    sp.dma_start(out[t * P:(t + 1) * P, cols], X[:, t, cols]).then_inc(out_done, 16)
                if t == 0:
                    sp.wait_ge(rest_done, 1)
                    sp.dma_start(out[0:P, LN3_COLS:], X[:, 0, LN3_COLS:]).then_inc(out_done, 16)
            sp.wait_ge(out_done, 80)

        @block.gpsimd
        def _(pool):
            pool.memset(reset[:], 1.0).then_inc(pool_link, 1)
            pool.memset(minus_half[:], -0.5).then_inc(half_done, 1)
            pool.wait_ge(pool_link, 1)
            pool.memset(reset[:, :].rearrange("p (c s) -> p c s", s=CHUNK)[:, :, 0:1], 0.0).then_inc(reset_done, 1)
            pool.memset(headsel[:], 0.0).then_inc(pool_link, 1)
            pool.wait_ge(pool_link, 2)
            pool.memset(headsel[0:64, 0:1], 1.0).then_inc(headsel_done, 1)
            pool.wait_ge(headsel_done, 1)
            pool.memset(headsel[64:128, 1:2], 1.0).then_inc(headsel_done, 1)
            pool.wait_ge(headsel_done, 2)
            pool.wait_ge(const_in, 16)
            for h in range(HA):
                pool.tensor_scalar(probsT[:, h * 384:(h + 1) * 384], const[:, C_DIST:C_DIST + 384],
                                   SLOPES[h] * DA ** 0.5, None, ALU.mult).then_inc(bias_done, 1)
            wait_out(pool, "qg")
            wait_out(pool, "kg")
            pool.tensor_tensor(qkdiag[:], qgT, kgT, ALU.mult).then_inc(qkdiag_done, 1)
            pool.wait_ge(cum_done, 1)
            pool.memset(att[:, 0:1024], 0.0).then_inc(att_zeroed, 1)
            pool.memset(lev_q[0], 0.0).then_inc(lev_q_zeroed, 1)
            wait_full(pool, "diag")
            pool.memset(lev_q[1], 0.0).then_inc(lev_q_zeroed, 1)
            pool.wait_ge(lev_q_zeroed, 2)
            pool.wait_ge(small_in, 32)
            for t in range(2):
                wait_out(pool, f"rg{t}")
                v = sg[:, t, :].rearrange("p (h n) -> p h n", h=HG)
                pool.tensor_tensor(v, v, gnorm[:, :].unsqueeze(1).to_broadcast([P, HG, DV]), ALU.mult)\
                    .then_inc(gate_done, 1)
            for n in range(len(LEVELS) + 1):
                w = LEVELS[n] if n < len(LEVELS) else P

                def part(v, c):
                    return v.rearrange("p (b c w) -> p b c w", c=2, w=w)[:, :, c, :]

                pool.wait_ge(decay_done, n + 1)
                if n >= 1:
                    pool.wait_ge(lev_done, 3 * n)
                if n >= 2:
                    b, before = FILL[f"lv{n - 2}"]
                    pool.wait_ge(bank_full[b], before + 1)
                if n < 2:
                    pool.wait_ge(bank_full[FILL["score7"][0]], FILL["score7"][1] + 1)
                pool.tensor_tensor(part(lev[n % 2], 0), part(kgT, 0), part(expo[n % 2], 0), ALU.mult).then_inc(lev_done, 1)
                if n == len(LEVELS):
                    pool.tensor_tensor(part(lev[n % 2], 1), part(qgT, 1), part(expo[n % 2], 1), ALU.mult)\
                        .then_inc(lev_done, 1)
                else:
                    for r in range(2):
                        own = slice(64 * r, 64 * r + 64)
                        pool.wait_ge(lev_done, 3 * n + 1 + r)
                        q, e = (v[own, :].rearrange("p (a b c w) -> p a b c w", a=4, c=2, w=w)[:, :, :, 1, :]
                                for v in (qgT, expo[n % 2]))
                        pool.tensor_tensor(lev_q[n % 2][own, :, r, :].rearrange("p a (b w) -> p a b w", w=w), q, e,
                                           ALU.mult).then_inc(lev_done, 1)
            pool.wait_ge(half_done, 1)
            for t in range(2):
                pool.wait_ge(meansq_done, t + 1)
                pool.tensor_tensor(rms[:, 4 * t:4 * t + 4], meansq[:, 4 * t:4 * t + 4], minus_half[:, 0:4], ALU.pow)\
                    .then_inc(rms_done, 1)
            for n in range(3):
                if n == 1:
                    for k, u in enumerate(POOL_UNITS):
                        pool.wait_ge(hi_done, hi_count(u))
                        pool.tensor_tensor(w_lo[:, 0, 1, :], half_view(u), w_hi[:, 0, 1, :].bitcast(f32), ALU.subtract)\
                            .then_inc(pool_lo, 1)
                for t in range(2):
                    pool.wait_ge(var_done, 2 * n + t + 1)
                    pool.tensor_tensor(rstd[:, n, t, :], vareps[:, n, t, :], minus_half[:, 0:1], ALU.pow)\
                        .then_inc(rstd_done, 1)
                    if n == 1:
                        wait_out(pool, f"yt{t}1")
                        pool.wait_ge(xT_hi, 2 * t + 6)
                        sl = (slice(None), slice(4, 8), slice(t * P, (t + 1) * P))
                        pool.tensor_tensor(actA_lo[sl], yT_half[t], actA_hi[sl].bitcast(f32), ALU.subtract)\
                            .then_inc(yT_lo, 1)
                    if n == 2 and t == 0:
                        v, rest = X[:, t, LN3_COLS:], slice(LN3_COLS, D)
                        pool.wait_ge(ln_in[2], 32)
                        pool.wait_ge(rstd_done, 5)
                        pool.tensor_scalar(v, v, mv[:, n, t, 0:1], rstd[:, n, t, :], ALU.subtract, ALU.mult)\
                            .then_inc(centred, 1)
                        pool.wait_ge(centred, 1)
                        pool.tensor_tensor(v, v, lng[:, rest], ALU.mult).then_inc(centred, 1)
                        pool.wait_ge(centred, 2)
                        pool.tensor_tensor(v, v, lnb[:, rest], ALU.add).then_inc(rest_done, 1)

        @block.scalar
        def _(act):
            def hi(u, dst, chunk=None):
                act.wait_ge(raw_in[u % RAW], raw_count(u))
                if chunk is not None and chunk >= 2:
                    before = chunk - 2
                    if before in ROWS_END:
                        act.wait_ge(rows_used, ROWS_END[before])
                    elif before in CHUNK_END:
                        wait_full(act, CHUNK_END[before])
                    else:
                        act.wait_ge(bank_full[3], FF_BASE[3] + 1)
                act.copy(dst, half_view(u)).then_inc(hi_done, 1)

            def hi_half(c, half):
                hi(unit(c, half), w_hi[:, c % 2, half, :], c)

            def evacuate(name, dst, scale=None):
                b = wait_full(act, name)
                if scale is None:
                    return act.copy(dst, b[:, :]).then_inc(freed(name), 1)
                return act.mul(dst, b[:, :], scale).then_inc(freed(name), 1)

            act.dma_start(wglr[:], w_in[:, GL:GL + RANK].rearrange("(a p) n -> p a n", p=P)).then_inc(wglr_in, 16)
            act.wait_ge(half_done, 1)
            act.copy(diag[:], minus_half[:])
            act.dma_start(wgu[:], w_gate_up).then_inc(wgu_in, 16)
            act.dma_start(bgate[:], b_gate).then_inc(small_in, 16)
            act.dma_start(gnorm[:], gla_norm_g.partition_broadcast(P)).then_inc(small_in, 16)
            for u, whole in enumerate(early(actA_hi, w_hi)):
                for piece in range(2):
                    act.wait_ge(early_in[2 * u + piece], 16)
                    act.copy(whole[:, piece * 1024:(piece + 1) * 1024], raw[:, u, piece * 1024:(piece + 1) * 1024])\
                        .then_inc(early_hi, 1)
            hi_half(1, 0)
            wait_full(act, "glr")
            act.copy(glrT[:], bank[4][0:RANK, 0:S]).then_inc(freed("glr"), 1)
            hi_half(1, 1)
            evacuate("qg", qgT, DK ** -0.5)
            evacuate("kg", kgT)
            act.wait_ge(zabs_done, 1)
            act.activation(zabs, zabs, ACT.Exp, scale=-1.0).then_inc(act_link, 1)
            act.wait_ge(act_link, 1)
            act.activation(zabs, zabs, ACT.Ln, bias=1.0).then_inc(softplus_done, 1)
            for n in range(2):
                hi_half(2, n)
                evacuate(f"qa{n}", qaT[:, 2 * n:2 * n + 2, :].rearrange("p m s -> p (m s)"))
            for n in range(2):
                hi_half(3, n)
                evacuate(f"ka{n}", kaT[:, 2 * n:2 * n + 2, :].rearrange("p m s -> p (m s)"))

            def exps(h):
                for t, (a, b) in enumerate(((0, P), (P, 3 * P))):
                    if t == 0:
                        act.wait_ge(score_done, h + 1)
                    else:
                        wait_out(act, f"score{h}")
                    v = probs[:, h * 384 + a:h * 384 + b]
                    act.activation(v, v, ACT.Exp, bias=negmax[:, 2 * h + t:2 * h + t + 1], scale=-1.0,
                                   accum_out=sums[:, 2 * h + t:2 * h + t + 1]).then_inc(exp_done, 1)

            def transposed(h):
                b = wait_full(act, f"pt{h}")
                act.copy(probsT[:, h * 384:(h + 1) * 384], b[:, 0:384]).then_inc(freed(f"pt{h}"), 1)

            hi_half(4, 0)
            evacuate("va0", va[:, 0, :])
            exps(0)
            exps(1)
            hi_half(4, 1)
            exps(2)
            exps(3)
            evacuate("va1", va[:, 1, :])
            hi_half(5, 0)
            evacuate("vg0", vg[:, 0, :])
            exps(4)
            exps(5)
            hi_half(5, 1)
            exps(6)
            exps(7)
            evacuate("vg1", vg[:, 1, :])
            for h in range(4):
                transposed(h)
            hi(MEM_UNIT, actB_hi[:].rearrange("p a s -> p (a s)"))
            hi_half(6, 0)

            def exp_r(t):
                b = wait_full(act, f"rg{t}")
                act.activation(sg[:, t, :], b[:, :], ACT.Exp, scale=-1.0).then_inc(expr_done, 1)

            exp_r(0)
            for h in range(4, 8):
                transposed(h)
            hi_half(6, 1)
            exp_r(1)

            def mix(n, name):
                b = wait_full(act, name)
                if name.startswith("pv"):
                    dst = actA_hi[:, 2 * n:2 * n + 2, :]
                else:
                    dst = actA_hi[:, 4:8, (n - 2) * P:(n - 1) * P]
                act.copy(dst, b[:, :].rearrange("p (m s) -> p m s", m=dst.shape[1])).then_inc(mix_hi, 1)

            mix(0, "pv0")
            mix(1, "pv1")
            b = wait_full(act, "diag")
            act.copy(diag[:], b[:, 0:8]).then_inc(freed("diag"), 1)

            def decay(n):
                act.wait_ge(expo_done, n + 1)
                act.activation(expo[n % 2], expo[n % 2], ACT.Exp, scale=1.0 / GATE_TEMP).then_inc(decay_done, 1)

            def memk(n):
                evacuate(f"xk{n}", memkT[:, 2 * n:2 * n + 2, :].rearrange("p m s -> p (m s)"))

            decay(0)
            hi_half(7, 0)
            decay(1)
            memk(0)
            hi_half(7, 1)
            decay(2)
            memk(1)
            decay(3)
            hi_half(8, 0)
            decay(4)
            memk(2)
            decay(5)
            hi_half(8, 1)
            memk(3)
            decay(6)
            decay(7)
            hi_half(9, 0)
            evacuate("xv00", memv[:, 0, 0:512])
            for r in range(2):
                b = wait_full(act, f"off{r}")
                act.copy(attoff.rearrange("p (f r) s -> p f r s", r=2)[:, :, r, :],
                         b[:, 0:S].rearrange("p (f s) -> p f s", f=2)).then_inc(freed(f"off{r}"), 1)
            hi_half(9, 1)
            evacuate("xv01", memv[:, 1, 0:512])
            for t in range(2):
                wait_out(act, f"av{t}")
                for h in range(HG):
                    act.activation(qk[:, 128 * (4 * t + h):128 * (4 * t + h + 1)], vg[:, t, h * DV:(h + 1) * DV],
                                   ACT.Square, accum_out=ssq[:, 4 * t + h:4 * t + h + 1]).then_inc(ssq_done, 1)
            hi_half(10, 0)
            hi_half(10, 1)
            mix(2, "gt0")
            mix(3, "gt1")
            hi_half(11, 0)
            hi_half(11, 1)

            def piece(k, name=None):
                if name is None:
                    wait_full(act, "av1")
                    wait_out(act, "lv6")
                    src = mem_pieces[k]
                else:
                    src = wait_full(act, name)[:, :]
                act.copy(mem_hi_pieces[k], src).then_inc(mem_hi, 1)

            def xpose(n, name):
                t, c = divmod(n % 4, 2)
                b = wait_full(act, name)
                act.copy(actA_hi[:, 4 * c:4 * c + 4, t * P:(t + 1) * P],
                         b[:, :].rearrange("p (m s) -> p m s", m=4)).then_inc(xT_hi, 1)

            hi_half(12, 0)
            hi_half(12, 1)
            for k in range(6):
                piece(k)
            piece(6, "xv10")
            xpose(0, "xt00")
            xpose(1, "xt01")
            xpose(2, "xt10")
            xpose(3, "xt11")
            piece(7, "xv11")

            def cq(h):
                b = wait_full(act, f"xq{h}")
                act.copy(cq_hi[:, 2 * h:2 * h + 2, :].rearrange("p m s -> p (m s)"), b[:, :]).then_inc(cq_hi_done, 1)

            def cexps(h):
                act.wait_ge(cneg_done, h + 1)
                b = wait_full(act, f"cs{h}")
                for t in range(2):
                    i = act.activation(cprobs[:, h, t, :], b[:, t * S:(t + 1) * S], ACT.Exp,
                                       bias=cneg[:, 2 * h + t:2 * h + t + 1], scale=DX ** -0.5,
                                       accum_out=csum[:, 2 * h + t:2 * h + t + 1])
                    i.then_inc(cexp_done if t == 0 else freed(f"cs{h}"), 1)

            def cT(h):
                b = wait_full(act, f"cpt{h}")
                act.copy(cprobsT_hi[:, h, :, :].rearrange("p m s -> p (m s)"), b[:, :]).then_inc(cT_hi_done, 1)

            def cross(h):
                b = wait_full(act, f"cpv{h}")
                act.copy(actB_hi[:, 2 * h:2 * h + 2, :], b[:, :].rearrange("p (m s) -> p m s", m=2)).then_inc(cross_hi, 1)

            hi_half(13, 0)
            cq(0)
            hi_half(13, 1)
            cq(1)
            cexps(0)
            hi_half(14, 0)
            cq(2)
            cexps(1)
            cT(0)
            hi_half(14, 1)
            cq(3)
            cT(1)
            cexps(2)
            cross(0)
            cross(1)
            cexps(3)
            cT(2)
            hi_half(15, 0)
            cross(2)
            cT(3)
            hi_half(15, 1)
            cross(3)
            hi_half(C_FF1_0, 0)
            hi_half(C_FF1_0, 1)

            def relus(g2, f, use):
                b = 2 * g2 + f
                act.wait_ge(bank_full[b], use)
                act.activation(relu[:, f, :], bank[b][:, :], ACT.Relu).then_inc(bank_free[b], 1)

            def hid(g2, f, n):
                act.wait_ge(sq_done, n)
                act.copy(actB_hi[:, 4 * g2 + 2 * f:4 * g2 + 2 * f + 2, :],
                         relu[:, f, :].rearrange("p (m s) -> p m s", m=2)).then_inc(hid_hi, 1)

            def hi_loop(k, half, i):
                u = unit(C_LOOP + k, half)
                act.wait_ge(raw_in[u % RAW], i * 32 + raw_count(u))
                if k % 2:
                    act.wait_ge(rows_used, i * 2 + (3 + k // 2))
                else:
                    act.wait_ge(bank_full[k - 1], i + (FF_BASE[k - 1] + k // 2))
                act.copy(w_hi[:, (C_LOOP + k) % 2, half, :], raw[:, u % RAW, :]).then_inc(hi_done, 1)

            def first_relu(t):
                wait_full(act, f"hid{t}")
                act.activation(relu[:, t, :], bank[FILL[f"hid{t}"][0]][:, :], ACT.Relu).then_inc(freed(f"hid{t}"), 1)

            def first_hid(t):
                b = wait_full(act, f"ht{t}")
                act.copy(actB_hi[:, 0:4, t * P:(t + 1) * P], b[:, :].rearrange("p (m s) -> p m s", m=4))\
                    .then_inc(hid_hi, 1)

            xpose(4, "yt00")
            xpose(5, "yt01")
            evacuate("yt01", yT_half[0].rearrange("p m s -> p (m s)"))
            hi_half(C_FF1_1, 0)
            hi_half(C_FF1_1, 1)
            xpose(6, "yt10")
            xpose(7, "yt11")
            evacuate("yt11", yT_half[1].rearrange("p m s -> p (m s)"))
            first_relu(0)
            first_relu(1)
            hi_half(C_FF2_0, 0)
            first_hid(0)
            first_hid(1)
            relus(1, 0, FF_BASE[2] + 1)
            hi_half(C_FF2_0, 1)
            hid(1, 0, 3)
            relus(1, 1, FF_BASE[3] + 1)
            hi_half(C_LOOP, 0)
            hid(1, 1, 4)
            hi_half(C_LOOP, 1)
            with act.Fori(0, G // 2 - 1) as i:
                for g in range(2):
                    n = 4 + 2 * g
                    hi_loop(2 * g + 1, 0, i)
                    act.wait_ge(hid_lo, i * 4 + (n - 3))
                    relus(g, 0, i + (FF_BASE[2 * g] + 1 + g))
                    hi_loop(2 * g + 1, 1, i)
                    hid(g, 0, i * 4 + (n + 1))
                    act.wait_ge(hid_lo, i * 4 + (n - 2))
                    relus(g, 1, i + (FF_BASE[2 * g + 1] + 1 + g))
                    hi_loop(2 * g + 2, 0, i)
                    hid(g, 1, i * 4 + (n + 2))
                    hi_loop(2 * g + 2, 1, i)

        @block.vector
        def _(dve):
            chain = [0]

            def link(ins):
                chain[0] += 1
                ins.then_inc(dve_link, 1)
                dve.wait_ge(dve_link, chain[0])

            def lo(u, dst, hi_part):
                dve.wait_ge(hi_done, hi_count(u))
                dve.tensor_tensor(dst, half_view(u), hi_part.bitcast(f32), ALU.subtract).then_inc(lo_done, 1)

            def lo_half(c, half):
                lo(unit(c, half), w_lo[:, c % 2, half, :], w_hi[:, c % 2, half, :])

            flat = "p a s -> p (a s)"
            for u, (whole, hi_part) in enumerate(zip(early(actA_lo, w_lo), early(actA_hi, w_hi))):
                for piece in range(2):
                    cut = slice(piece * 1024, (piece + 1) * 1024)
                    dve.wait_ge(early_hi, 2 * u + piece + 1)
                    dve.tensor_tensor(whole[:, cut], raw[:, u, cut], hi_part[:, cut].bitcast(f32), ALU.subtract)\
                        .then_inc(early_lo, 1)
            lo_half(1, 0)
            lo_half(1, 1)
            dve.wait_ge(small_in, 32)
            b = wait_full(dve, "z")
            for f in range(2):
                i = dve.tensor_scalar(zlin[:, f * S:(f + 1) * S], b[:, f * S:(f + 1) * S], bgate[:, f:f + 1], None, ALU.add)
                i.then_inc(freed("z") if f == 1 else dve_link, 1)
            chain[0] += 1
            dve.wait_ge(dve_link, chain[0])
            wait_out(dve, "z")
            dve.scalar_tensor_tensor(zabs, zlin, -1.0, zlin, ALU.mult, ALU.max).then_inc(zabs_done, 1)
            lo_half(2, 0)
            lo_half(2, 1)
            dve.wait_ge(softplus_done, 1)
            link(dve.scalar_tensor_tensor(zlin, zlin, 0.0, zabs, ALU.min, ALU.subtract))
            dve.wait_ge(reset_done, 1)
            dve.tensor_tensor_scan(cum, reset[:], zlin, 0.0, ALU.mult, ALU.add).then_inc(cum_done, 1)
            lo_half(3, 0)
            lo_half(3, 1)

            def score(h):
                b = wait_full(dve, f"score{h}")
                dve.wait_ge(bias_done, h + 1)
                for t, (a, e) in enumerate(((0, P), (P, 3 * P))):
                    i = dve.tensor_tensor_reduce(
                        out=probs[:, h * 384 + a:h * 384 + e], in0=b[:, a:e],
                        in1=probsT[:, h * 384 + a:h * 384 + e], scale=-DA ** -0.5, scalar=3e38,
                        op0=ALU.add, op1=ALU.min, accum_out=negmax[:, 2 * h + t:2 * h + t + 1])
                    i.then_inc(score_done if t == 0 else freed(f"score{h}"), 1)

            def norm(h):
                dve.wait_ge(exp_done, 2 * h + 2)
                link(dve.reciprocal(rsums[:, 2 * h:2 * h + 2], sums[:, 2 * h:2 * h + 2]))
                for t, (a, e) in enumerate(((0, P), (P, 3 * P))):
                    v = probs[:, h * 384 + a:h * 384 + e]
                    dve.tensor_scalar(v, v, rsums[:, 2 * h + t:2 * h + t + 1], None, ALU.mult).then_inc(prob_done, 1)

            lo_half(4, 0)
            for h in range(4):
                score(h)
            norm(0)
            norm(1)
            lo_half(4, 1)
            norm(2)
            norm(3)
            lo_half(5, 0)
            for h in range(4, 8):
                score(h)
            norm(4)
            norm(5)
            lo_half(5, 1)
            norm(6)
            norm(7)

            def exponents(n):
                e, c4 = expo[n % 2], cum
                if n >= 2:
                    dve.wait_ge(lev_done, 3 * (n - 1))
                else:
                    dve.wait_ge(bank_full[FILL["score7"][0]], FILL["score7"][1] + 1)
                if n < len(LEVELS) and LEVELS[n] < CHUNK:
                    w = LEVELS[n]
                    ev = e.rearrange("p (b c w) -> p b c w", c=2, w=w)
                    cv = c4.rearrange("p (b c w) -> p b c w", c=2, w=w)
                    mid = cv[:, :, 0, w - 1:w].to_broadcast([P, 512 // (2 * w), w])
                    link(dve.tensor_tensor(ev[:, :, 0, :], mid, cv[:, :, 0, :], ALU.subtract))
                    dve.tensor_tensor(ev[:, :, 1, :], cv[:, :, 1, :], mid, ALU.subtract).then_inc(expo_done, 1)
                    return
                ev = e.rearrange("p (f c w) -> p f c w", f=2, c=4)
                cv = c4.rearrange("p (f c w) -> p f c w", f=2, c=4)

                def last(c):
                    return cv[:, :, c, CHUNK - 1:CHUNK].to_broadcast([P, 2, CHUNK])

                if n < len(LEVELS):
                    for c in (0, 2):
                        link(dve.tensor_tensor(ev[:, :, c, :], last(c), cv[:, :, c, :], ALU.subtract))
                    link(dve.tensor_copy(ev[:, :, 1, :], cv[:, :, 1, :]))
                    dve.tensor_copy(ev[:, :, 3, :], cv[:, :, 3, :]).then_inc(expo_done, 1)
                else:
                    link(dve.tensor_tensor(ev[:, :, 0, :], last(0), cv[:, :, 0, :], ALU.subtract))
                    link(dve.tensor_tensor(ev[:, :, 0, :], ev[:, :, 0, :], last(1), ALU.add))
                    link(dve.tensor_tensor(ev[:, :, 1, :], last(1), cv[:, :, 1, :], ALU.subtract))
                    link(dve.tensor_copy(ev[:, :, 2, :], cv[:, :, 2, :]))
                    dve.tensor_tensor(ev[:, :, 3, :], cv[:, :, 3, :], last(2), ALU.add).then_inc(expo_done, 1)

            def masked(n):
                name, w = f"lv{n}", LEVELS[n]
                b = wait_full(dve, name)
                if n == 0:
                    dve.wait_ge(att_zeroed, 1)
                else:
                    wait_out(dve, f"lv{n - 1}")
                dve.copy_predicated(
                    att[:, 0:1024].rearrange("p (a b c w) -> p a b c w", a=8, c=2, w=w)[:, :, :, 1, :],
                    level_mask(n).rearrange("p (b c w) -> p b c w", c=2, w=w)[:, :, 1, :]
                    .unsqueeze(1).to_broadcast([P, 8, 64 // w, w]),
                    b[:, :].rearrange("p (a b w) -> p a b w", a=8, w=w)).then_inc(freed(name), 1)

            def silu(t):
                dve.wait_ge(expr_done, t + 1)
                v = sg[:, t, :]
                link(dve.tensor_scalar(v, v, 1.0, None, ALU.add))
                link(dve.reciprocal(v, v))
                b = wait_full(dve, f"rg{t}")
                dve.tensor_tensor(v, v, b[:, :], ALU.mult).then_inc(freed(f"rg{t}"), 1)

            def mix(n, name):
                b = wait_full(dve, name)
                dve.wait_ge(mix_hi, n + 1)
                sl = (slice(None), slice(2 * n, 2 * n + 2), slice(None)) if n < 2 else \
                    (slice(None), slice(4, 8), slice((n - 2) * P, (n - 1) * P))
                hi_part = actA_hi[sl]
                dve.tensor_tensor(actA_lo[sl], b[:, :].rearrange("p (m s) -> p m s", m=hi_part.shape[1]),
                                  hi_part.bitcast(f32), ALU.subtract).then_inc(freed(name), 1)

            lo(MEM_UNIT, actB_lo[:].rearrange(flat), actB_hi[:].rearrange(flat))
            exponents(0)
            lo_half(6, 0)
            silu(0)
            exponents(1)
            lo_half(6, 1)
            silu(1)
            mix(0, "pv0")
            mix(1, "pv1")
            lo_half(7, 0)
            lo_half(7, 1)
            exponents(2)
            masked(0)
            exponents(3)
            masked(1)
            exponents(4)
            masked(2)
            lo_half(8, 0)
            exponents(5)
            masked(3)
            exponents(6)
            masked(4)
            lo_half(8, 1)
            exponents(7)
            masked(5)
            masked(6)
            lo_half(9, 0)
            lo_half(9, 1)

            wait_out(dve, "diag")
            b1 = FILL["av1"]
            dve.wait_ge(bank_full[b1[0]], b1[1] + 1)
            for t in range(2):
                b = bank[FILL[f"av{t}"][0]]
                for h in range(HG):
                    v = vg[:, t, h * DV:(h + 1) * DV]
                    k = 4 * t + 2 * (h // 2) + h % 2
                    i = dve.scalar_tensor_tensor(v, v, diag[:, k:k + 1], b[:, h * DV:(h + 1) * DV], ALU.mult, ALU.add)
                    i.then_inc(dve_link if h < HG - 1 else freed(f"av{t}"), 1)
                chain[0] += HG - 1
            for t in range(2):
                dve.wait_ge(ssq_done, 4 * t + 4)
                dve.wait_ge(dve_link, chain[0])
                dve.tensor_scalar(meansq[:, 4 * t:4 * t + 4], ssq[:, 4 * t:4 * t + 4], 1.0 / DV, RMS_EPS,
                                  ALU.mult, ALU.add).then_inc(meansq_done, 1)
            for t in range(2):
                dve.wait_ge(rms_done, t + 1)
                dve.wait_ge(gate_done, t + 1)
                for h in range(HG):
                    v = vg[:, t, h * DV:(h + 1) * DV]
                    dve.scalar_tensor_tensor(v, v, rms[:, 4 * t + h:4 * t + h + 1], sg[:, t, h * DV:(h + 1) * DV],
                                             ALU.mult, ALU.mult).then_inc(glao_done, 1)
            lo_half(10, 0)
            mix(2, "gt0")
            mix(3, "gt1")
            lo_half(10, 1)
            lo_half(11, 0)
            lo_half(11, 1)

            def add_half(n, t, c, banks):
                b, full, free = banks[c]
                v = X[:, t, c * 512:(c + 1) * 512]
                dve.wait_ge(full[0], full[1])
                dve.scalar_tensor_tensor(v, v, ALPHA, b[:, :], ALU.mult, ALU.add).then_inc(free, 1)

            def half_stats(n, t, c, banks):
                b, full, free = banks[c]
                dve.wait_ge(free, full[1])
                dve.bn_stats(stats[:, n, t, c, :], X[:, t, c * 512:(c + 1) * 512]).then_inc(dve_link, 1)
                chain[0] += 1

            def normalize(n, t):
                dve.wait_ge(dve_link, chain[0])
                link(dve.bn_aggr(mv[:, n, t, :], stats[:, n, t, :, :].rearrange("p c k -> p (c k)")))
                dve.tensor_scalar(vareps[:, n, t, :], mv[:, n, t, 1:2], LN_EPS, None, ALU.add).then_inc(var_done, 1)
                dve.wait_ge(ln_in[n], 32)
                half = (LN3_COLS if (n, t) == (2, 0) else D) // 2
                cols = [slice(c * half, (c + 1) * half) for c in range(2)]
                for c in cols:
                    dve.scalar_tensor_tensor(X[:, t, c], X[:, t, c], mv[:, n, t, 0:1], lng[:, c],
                                             ALU.subtract, ALU.mult).then_inc(dve_link, 1)
                chain[0] += 2
                dve.wait_ge(rstd_done, 2 * n + t + 1)
                for k, c in enumerate(cols):
                    dve.wait_ge(dve_link, chain[0] - 1 + k)
                    dve.scalar_tensor_tensor(X[:, t, c], X[:, t, c], rstd[:, n, t, :], lnb[:, c],
                                             ALU.mult, ALU.add).then_inc(ln_done, 1)

            def layer_norm(n, t, banks):
                for c in range(2):
                    add_half(n, t, c, banks)
                    half_stats(n, t, c, banks)
                normalize(n, t)

            def front_banks(t, name):
                return [(bank[FILL[f"{name}{t}{c}"][0]],
                         (bank_full[FILL[f"{name}{t}{c}"][0]], FILL[f"{name}{t}{c}"][1] + 1),
                         freed(f"{name}{t}{c}")) for c in range(2)]

            def xpose(n, name):
                t, c = divmod(n % 4, 2)
                b = wait_full(dve, name)
                dve.wait_ge(xT_hi, n + 1)
                sl = (slice(None), slice(4 * c, 4 * c + 4), slice(t * P, (t + 1) * P))
                dve.tensor_tensor(actA_lo[sl], b[:, :].rearrange("p (m s) -> p m s", m=4),
                                  actA_hi[sl].bitcast(f32), ALU.subtract).then_inc(freed(name), 1)

            dve.wait_ge(x_in, 16)
            layer_norm(0, 0, front_banks(0, "mo"))
            layer_norm(0, 1, front_banks(1, "mo"))
            xpose(0, "xt00")
            xpose(1, "xt01")
            lo_half(12, 0)
            xpose(2, "xt10")
            xpose(3, "xt11")

            def piece(k, name=None):
                src = mem_pieces[k] if name is None else wait_full(dve, name)[:, :]
                dve.wait_ge(mem_hi, k + 1)
                dve.tensor_tensor(mem_lo_pieces[k], src, mem_hi_pieces[k].bitcast(f32), ALU.subtract)\
                    .then_inc(mem_lo if name is None else freed(name), 1)

            def cq(h):
                b = wait_full(dve, f"xq{h}")
                dve.wait_ge(cq_hi_done, h + 1)
                sl = (slice(None), slice(2 * h, 2 * h + 2), slice(None))
                dve.tensor_tensor(cq_lo[sl], b[:, :].rearrange("p (m s) -> p m s", m=2),
                                  cq_hi[sl].bitcast(f32), ALU.subtract).then_inc(freed(f"xq{h}"), 1)

            def cT(h):
                b = wait_full(dve, f"cpt{h}")
                dve.wait_ge(cT_hi_done, h + 1)
                dve.tensor_tensor(cprobsT_lo[:, h], b[:, :].rearrange("p (m s) -> p m s", m=2),
                                  cprobsT_hi[:, h].bitcast(f32), ALU.subtract).then_inc(freed(f"cpt{h}"), 1)

            for k in range(4):
                piece(k)
            piece(6, "xv10")

            def cmaxes(h):
                b = wait_full(dve, f"cs{h}")
                link(dve.tensor_reduce(cmax[:, 2 * h:2 * h + 2], b[:, :].rearrange("p (t m) -> p t m", t=2),
                                       AX.X, ALU.max))
                dve.tensor_scalar(cneg[:, 2 * h:2 * h + 2], cmax[:, 2 * h:2 * h + 2], -DX ** -0.5, None, ALU.mult)\
                    .then_inc(cneg_done, 1)

            def cnorm(h):
                dve.wait_ge(cexp_done, h + 1)
                wait_out(dve, f"cs{h}")
                link(dve.reciprocal(crec[:, 2 * h:2 * h + 2], csum[:, 2 * h:2 * h + 2]))
                for t in range(2):
                    v = cprobs[:, h, t, :]
                    dve.tensor_scalar(v, v, crec[:, 2 * h + t:2 * h + t + 1], None, ALU.mult).then_inc(cprob_done, 1)

            def cross(h):
                b = wait_full(dve, f"cpv{h}")
                dve.wait_ge(cross_hi, h + 1)
                dve.tensor_tensor(actB_lo[:, 2 * h:2 * h + 2, :], b[:, :].rearrange("p (m s) -> p m s", m=2),
                                  actB_hi[:, 2 * h:2 * h + 2, :].bitcast(f32), ALU.subtract)\
                    .then_inc(freed(f"cpv{h}"), 1)

            lo_half(13, 0)
            piece(7, "xv11")
            cq(0)
            lo_half(13, 1)
            cq(1)
            cmaxes(0)
            cnorm(0)
            piece(4)
            piece(5)
            lo_half(14, 0)
            cq(2)
            cmaxes(1)
            cnorm(1)
            cT(0)
            lo_half(14, 1)
            cq(3)
            cmaxes(2)
            cT(1)
            cnorm(2)
            cross(0)
            cmaxes(3)
            cross(1)
            cnorm(3)
            cT(2)
            lo_half(15, 0)
            cross(2)
            cT(3)
            lo_half(15, 1)
            cross(3)
            lo_half(C_FF1_0, 0)

            def square(g2, f, n):
                dve.wait_ge(bank_free[2 * g2 + f], n)
                dve.tensor_tensor(relu[:, f, :], relu[:, f, :], relu[:, f, :], ALU.mult).then_inc(sq_done, 1)

            def hid(g2, f, n):
                dve.wait_ge(hid_hi, n)
                sl = (slice(None), slice(4 * g2 + 2 * f, 4 * g2 + 2 * f + 2), slice(None))
                dve.tensor_tensor(actB_lo[sl], relu[:, f, :].rearrange("p (m s) -> p m s", m=2),
                                  actB_hi[sl].bitcast(f32), ALU.subtract).then_inc(hid_lo, 1)

            def lo_loop(k, half, i):
                c = C_LOOP + k
                u = unit(c, half)
                dve.wait_ge(hi_done, i * 8 + hi_count(u))
                dve.tensor_tensor(w_lo[:, c % 2, half, :], raw[:, u % RAW, :], w_hi[:, c % 2, half, :].bitcast(f32),
                                  ALU.subtract).then_inc(lo_done, 1)

            def first_square(t):
                wait_out(dve, f"hid{t}")
                dve.tensor_tensor(relu[:, t, :], relu[:, t, :], relu[:, t, :], ALU.mult).then_inc(sq_done, 1)

            def first_hid(t):
                b = wait_full(dve, f"ht{t}")
                dve.wait_ge(hid_hi, t + 1)
                dve.tensor_tensor(actB_lo[:, 0:4, t * P:(t + 1) * P], b[:, :].rearrange("p (m s) -> p m s", m=4),
                                  actB_hi[:, 0:4, t * P:(t + 1) * P].bitcast(f32), ALU.subtract)\
                    .then_inc(freed(f"ht{t}"), 1)

            layer_norm(1, 0, front_banks(0, "xo"))
            add_half(1, 1, 0, front_banks(1, "xo"))
            xpose(4, "yt00")
            half_stats(1, 1, 0, front_banks(1, "xo"))
            add_half(1, 1, 1, front_banks(1, "xo"))
            half_stats(1, 1, 1, front_banks(1, "xo"))
            normalize(1, 1)
            xpose(6, "yt10")
            lo_half(C_FF1_1, 0)
            first_square(0)
            lo_half(C_FF1_1, 1)
            first_square(1)
            lo_half(C_FF2_0, 0)
            first_hid(0)
            first_hid(1)
            square(1, 0, FF_BASE[2] + 1)
            lo_half(C_FF2_0, 1)
            hid(1, 0, 3)
            square(1, 1, FF_BASE[3] + 1)
            lo_half(C_LOOP, 0)
            hid(1, 1, 4)
            lo_half(C_LOOP, 1)
            with dve.Fori(0, G // 2 - 1) as i:
                for g in range(2):
                    n = 4 + 2 * g
                    lo_loop(2 * g + 1, 0, i)
                    square(g, 0, i + (FF_BASE[2 * g] + 1 + g))
                    lo_loop(2 * g + 1, 1, i)
                    hid(g, 0, i * 4 + (n + 1))
                    square(g, 1, i + (FF_BASE[2 * g + 1] + 1 + g))
                    lo_loop(2 * g + 2, 0, i)
                    hid(g, 1, i * 4 + (n + 2))
                    lo_loop(2 * g + 2, 1, i)
            for t in range(2):
                layer_norm(2, t, [(bank[b], (bank_full[b], FF_BASE[b] + 1), bank_free[b])
                                  for b in (4 + 2 * t, 5 + 2 * t)])

        @block.tensor
        def _(pe):
            def begin(name):
                b, before = FILL[name]
                if before:
                    pe.wait_ge(bank_free[b], before)
                return bank[b]

            def full(name):
                return bank_full[FILL[name][0]]

            def three(dst, stat, mov, start, stop):
                pe.matmul(dst, stat[0], mov[0], start=start, stop=False)
                pe.matmul(dst, stat[0], mov[1], start=False, stop=False)
                return pe.matmul(dst, stat[1], mov[0], start=False, stop=stop)

            def weight(c, k, a, b):
                return [w[:, c % 2, k // 4, (k % 4) * 512 + a:(k % 4) * 512 + b] for w in (w_hi, w_lo)]

            def weight_rows(c, k, a, b):
                return [w[:, c % 2, k // 2, (k % 2) * 1024 + a:(k % 2) * 1024 + b] for w in (w_hi, w_lo)]

            A, B = (actA_hi, actA_lo), (actB_hi, actB_lo)

            def features(c, step, src, name, ready=None):
                b = begin(name)
                for m in range(2):
                    for k in range(8):
                        if step == 0 and m == 0 and k % 4 == 0:
                            wait_lo(pe, unit(c, k // 4))
                            if ready is not None:
                                ready(k // 4)
                        i = three(b[:, m * S:(m + 1) * S], weight(c, k, (2 * step + m) * P, (2 * step + m + 1) * P),
                                  [a[:, k, :] for a in src], k == 0, k == 7)
                i.then_inc(full(name), 1)

            def tokens(c, t, src, name, between={}):
                b = begin(name)
                for k in range(8):
                    if t == 0 and k % 4 == 0:
                        wait_lo(pe, unit(c, k // 4))
                    if k in between:
                        between[k]()
                    i = three(b[:, :], [a[:, k, t * P:(t + 1) * P] for a in src], weight(c, k, 0, 512), k == 0, k == 7)
                i.then_inc(full(name), 1)

            def rows(c, part, src, names, base, between={}):
                for t in range(2):
                    for n in range(2):
                        b = begin(names[2 * t + n]) if part == 0 else bank[FILL[names[2 * t + n]][0]]
                        for k in range(4):
                            if t == 0 and n == 0 and k % 2 == 0:
                                wait_lo(pe, unit(c, k // 2))
                            if (2 * t + n, k) in between:
                                between[2 * t + n, k]()
                            i = three(b[:, :], [a[:, base + k, t * P:(t + 1) * P] for a in src],
                                      weight_rows(c, k, n * 512, (n + 1) * 512), part == 0 and k == 0,
                                      part == 1 and k == 3)
                        if part == 1:
                            i.then_inc(full(names[2 * t + n]), 1)
                        elif t == 1 and n == 1:
                            i.then_inc(rows_used, 1)

            pe.wait_ge(reset_done, 1)
            for _ in range(WARM_UP):
                pe.matmul(bank[7][:, :], reset[:, 0:P], reset[:, :], start=True, stop=True)

            b = begin("glr")
            pe.wait_ge(wglr_in, 16)
            for k in range(8):
                if k % 4 == 0:
                    pe.wait_ge(early_in[k // 4], 16)
                i = pe.matmul(b[0:RANK, 0:S], wglr[:, k, :], raw[:, 0, k * S:(k + 1) * S], start=k == 0, stop=k == 7)
            i.then_inc(full("glr"), 1)
            banks = [begin("qg"), begin("kg")]
            for piece in range(4):
                if piece % 2 == 0:
                    wait_lo(pe, 0, piece // 2)
                wait_lo(pe, 1 + piece // 2, piece % 2)
                for m in range(4):
                    dst = banks[m // 2][:, (m % 2) * S:(m % 2 + 1) * S]
                    for k in range(2 * piece, 2 * piece + 2):
                        stat, mov = weight(0, k, m * P, (m + 1) * P), (actA_hi[:, k, :], actA_lo[:, k, :])
                        pe.matmul(dst, stat[0], mov[0], start=k == 0 and m % 2 == 0, stop=False, skip_group_check=True)
                        pe.matmul(dst, stat[0], mov[1], start=False, stop=False, skip_group_check=True)
                        i = pe.matmul(dst, stat[1], mov[0], start=False, stop=k == 7, skip_group_check=True)
                    if piece == 3 and m % 2 == 1:
                        i.then_inc(full(("qg", "kg")[m // 2]), 1)
            b = begin("z")
            wait_out(pe, "glr")
            pe.wait_ge(wgu_in, 16)
            for f in range(2):
                i = pe.matmul(b[:, f * S:(f + 1) * S], wgu[:, f * P:(f + 1) * P], glrT[:], start=True, stop=True)
            i.then_inc(full("z"), 1)
            features(1, 0, A, "qa0")
            features(1, 1, A, "qa1")
            features(2, 0, A, "ka0")
            features(2, 1, A, "ka1")

            def score(h):
                b = begin(f"score{h}")
                r = slice(64 * (h % 2), 64 * (h % 2) + 64)
                pe.matmul(b[:, 0:P], qaT[r, h // 2, 0:P], kaT[r, h // 2, 0:P], start=True, stop=True)
                pe.matmul(b[:, P:3 * P], qaT[r, h // 2, P:S], kaT[r, h // 2, :], start=True, stop=True)\
                    .then_inc(full(f"score{h}"), 1)

            def transpose_probs(h):
                b = begin(f"pt{h}")
                pe.wait_ge(prob_done, 2 * h + 2)
                for a in range(3):
                    i = pe.transpose(b[:, a * P:(a + 1) * P], probs[:, h * 384 + a * P:h * 384 + (a + 1) * P], ident)
                i.then_inc(full(f"pt{h}"), 1)

            tokens(3, 0, A, "va0")
            for name in ("qa0", "qa1", "ka0", "ka1"):
                wait_out(pe, name)
            for h in range(4):
                score(h)
            tokens(3, 1, A, "va1")
            tokens(4, 0, A, "vg0")
            for h in range(4, 8):
                score(h)
            tokens(4, 1, A, "vg1")
            for h in range(4):
                transpose_probs(h)
            tokens(5, 0, A, "rg0")
            for h in range(4, 8):
                transpose_probs(h)
            tokens(5, 1, A, "rg1")
            for name in ["va0", "va1"] + [f"pt{h}" for h in range(HA)]:
                wait_out(pe, name)
            for n in range(2):
                b = begin(f"pv{n}")
                for h in range(4 * n, 4 * n + 4):
                    r = slice(64 * (h % 2), 64 * (h % 2) + 64)
                    c = (h // 2 - 2 * n) * S
                    pe.matmul(b[r, c:c + S], va[:, 0, h * DA:(h + 1) * DA], probsT[:, h * 384:h * 384 + S],
                              start=True, stop=False)
                    i = pe.matmul(b[r, c + P:c + S], va[:, 1, h * DA:(h + 1) * DA],
                                  probsT[:, h * 384 + S:h * 384 + 384], start=False, stop=True)
                i.then_inc(full(f"pv{n}"), 1)
            b = begin("diag")
            pe.wait_ge(qkdiag_done, 1)
            pe.wait_ge(headsel_done, 2)
            for t in range(2):
                for f in range(2):
                    k = 4 * t + 2 * f
                    i = pe.matmul(b[:, k:k + 2], qkdiag[:, f * S + t * P:f * S + (t + 1) * P], headsel[:],
                                  start=True, stop=True)
            i.then_inc(full("diag"), 1)

            def level(n):
                pe.wait_ge(lev_done, 3 * n + 3)
                b = begin(f"lv{n}")
                for a in range(4):
                    t, f = divmod(a, 2)
                    i = pe.matmul(b[:, a * P:(a + 1) * P], lev[n % 2][:, f * S + t * P:f * S + (t + 1) * P],
                                  lev_q[n % 2][:, 2 * f + t, :, :], start=True, stop=True)
                i.then_inc(full(f"lv{n}"), 1)

            wait_lo(pe, MEM_UNIT)
            features(6, 0, B, "xk0")
            features(6, 1, B, "xk1")
            level(0)
            level(1)
            features(7, 0, B, "xk2")
            level(2)
            level(3)
            features(7, 1, B, "xk3")
            level(4)
            level(5)
            tokens(8, 0, B, "xv00")
            level(6)
            pe.wait_ge(lev_done, 3 * len(LEVELS) + 2)
            banks = [begin("off0"), begin("off1")]
            for f in range(2):
                for r in range(2):
                    v = lev[1][64 * r:64 * r + 64, f * S:(f + 1) * S]
                    i = pe.matmul(banks[r][:, f * P:(f + 1) * P], v[:, 0:P], v[:, P:S], start=True, stop=True)
                    if f == 1:
                        i.then_inc(full(f"off{r}"), 1)
            tokens(8, 1, B, "xv01")
            for name in ("vg0", "vg1", "off0", "off1", "lv6"):
                wait_out(pe, name)
            for t in range(2):
                b = begin(f"av{t}")
                for h in range(HG):
                    c = slice(h * DV, (h + 1) * DV)
                    if t == 1:
                        pe.matmul(b[:, c], attoff[:, h, :], vg[:, 0, c], start=True, stop=False)
                    i = pe.matmul(b[:, c], attT[:, t, h, :], vg[:, t, c], start=t == 0, stop=True)
                i.then_inc(full(f"av{t}"), 1)
            mo = ["mo00", "mo01", "mo10", "mo11"]
            wait_out(pe, "pv0")
            wait_out(pe, "pv1")

            def transpose_gla():
                for t in range(2):
                    b = begin(f"gt{t}")
                    pe.wait_ge(glao_done, 4 * t + 4)
                    for h in range(HG):
                        i = pe.transpose(b[:, h * P:(h + 1) * P], vg[:, t, h * DV:(h + 1) * DV], ident)
                    i.then_inc(full(f"gt{t}"), 1)

            rows(9, 0, A, mo, 0, between={(3, 0): transpose_gla})
            wait_out(pe, "gt0")
            wait_out(pe, "gt1")
            rows(10, 1, A, mo, 4)

            def transpose_x(n, t, name, halves=(0, 1)):
                for c in halves:
                    b = begin(f"{name}{t}{c}")
                    pe.wait_ge(ln_done, 4 * n + 2 * t + c + 1)
                    for m in range(4):
                        i = pe.transpose(b[:, m * P:(m + 1) * P], X[:, t, (4 * c + m) * P:(4 * c + m + 1) * P], ident)
                    i.then_inc(full(f"{name}{t}{c}"), 1)

            tokens(11, 0, B, "xv10")
            transpose_x(0, 0, "xt")
            tokens(11, 1, B, "xv11", between={4: lambda: transpose_x(0, 1, "xt")})

            def keys(h):
                return [v.rearrange("p (m s) -> p m s", m=2) for v in (mem_hi_pieces[h], mem_lo_pieces[h])]

            def cscore(h):
                b = begin(f"cs{h}")
                wait_out(pe, f"xq{h}")
                for t in range(2):
                    for d in range(2):
                        i = three(b[:, t * S:(t + 1) * S],
                                  [q[:, 2 * h + d, t * P:(t + 1) * P] for q in (cq_hi, cq_lo)],
                                  [k[:, d, :] for k in keys(h)], d == 0, d == 1)
                i.then_inc(full(f"cs{h}"), 1)

            def ctranspose(h):
                b = begin(f"cpt{h}")
                pe.wait_ge(cprob_done, 2 * h + 2)
                for m in range(2):
                    for t in range(2):
                        i = pe.transpose(b[:, m * S + t * P:m * S + (t + 1) * P], cprobs[:, h, t, m * P:(m + 1) * P], ident)
                i.then_inc(full(f"cpt{h}"), 1)

            def cvalues(h):
                b = begin(f"cpv{h}")
                wait_out(pe, f"cpt{h}")
                for d in range(2):
                    for m in range(2):
                        k, at = 4 + 2 * (h // 2) + m, h % 2 * DX + d * P
                        i = three(b[:, d * S:(d + 1) * S],
                                  [v[:, at:at + P] for v in (mem_hi_pieces[k], mem_lo_pieces[k])],
                                  [p[:, h, m, :] for p in (cprobsT_hi, cprobsT_lo)], m == 0, m == 1)
                i.then_inc(full(f"cpv{h}"), 1)


            def normed(name):
                return lambda c: [wait_out(pe, f"{name}{t}{c}") for t in range(2)]

            features(12, 0, A, "xq0", ready=normed("xt"))
            features(12, 1, A, "xq1")
            pe.wait_ge(mem_lo, 4)
            cscore(0)
            features(13, 0, A, "xq2")
            cscore(1)
            ctranspose(0)
            features(13, 1, A, "xq3")
            cscore(2)
            ctranspose(1)
            pe.wait_ge(mem_lo, 6)
            wait_out(pe, "xv10")
            wait_out(pe, "xv11")
            cvalues(0)
            cscore(3)
            cvalues(1)
            ctranspose(2)
            xo = ["xo00", "xo01", "xo10", "xo11"]

            def heads_2_3():
                cvalues(2)
                ctranspose(3)

            rows(14, 0, B, xo, 0, between={
                (0, 0): lambda: wait_out(pe, "cpv0"), (0, 2): lambda: wait_out(pe, "cpv1"),
                (1, 0): heads_2_3, (2, 0): lambda: cvalues(3)})
            wait_out(pe, "cpv2")
            wait_out(pe, "cpv3")
            rows(15, 1, B, xo, 4, between={(3, 3): lambda: transpose_x(1, 0, "yt", [0])})
            transpose_x(1, 0, "yt", [1])
            wait_out(pe, "yt00")
            tokens(C_FF1_0, 0, A, "hid0", between={4: lambda: pe.wait_ge(yT_lo, 1), 6: lambda: transpose_x(1, 1, "yt")})
            wait_out(pe, "yt10")
            tokens(C_FF1_0, 1, A, "hid1", between={4: lambda: pe.wait_ge(yT_lo, 2)})

            def transpose_hidden():
                for t in range(2):
                    b = begin(f"ht{t}")
                    pe.wait_ge(sq_done, t + 1)
                    for m in range(4):
                        i = pe.transpose(b[:, m * P:(m + 1) * P], relu[:, t, m * P:(m + 1) * P], ident)
                    i.then_inc(full(f"ht{t}"), 1)

            def ff1(g2, par, lo_need, free_need, between=None):
                for f in range(2):
                    b = bank[2 * g2 + f]
                    pe.wait_ge(bank_free[2 * g2 + f], free_need[f])
                    for m in range(2):
                        for k in range(8):
                            if f == 0 and m == 0 and k % 4 == 0:
                                pe.wait_ge(lo_done, lo_need[k // 4])
                            i = three(b[:, m * S:(m + 1) * S],
                                      [w[:, par, k // 4, (k % 4) * 512 + (2 * f + m) * P:(k % 4) * 512 + (2 * f + m + 1) * P]
                                       for w in (w_hi, w_lo)], [a[:, k, :] for a in A], k == 0, k == 7)
                    i.then_inc(bank_full[2 * g2 + f], 1)
                    if f == 0 and between is not None:
                        between()

            def ff2(g2, par, lo_need, hid_need=None, first=False, last=False):
                if not first:
                    pe.wait_ge(hid_lo, hid_need)
                for t in range(2):
                    for n in range(2):
                        b = bank[4 + 2 * t + n]
                        if first:
                            pe.wait_ge(bank_free[4 + 2 * t + n], FF_BASE[4 + 2 * t + n])
                        for k in range(4):
                            if t == 0 and n == 0 and k % 2 == 0:
                                pe.wait_ge(lo_done, lo_need[k // 2])
                            i = three(b[:, :], [a[:, 4 * g2 + k, t * P:(t + 1) * P] for a in B],
                                      [w[:, par, k // 2, (k % 2) * 1024 + n * 512:(k % 2) * 1024 + (n + 1) * 512]
                                       for w in (w_hi, w_lo)], first and k == 0, last and k == 3)
                        if last:
                            i.then_inc(bank_full[4 + 2 * t + n], 1)
                if not last:
                    i.then_inc(rows_used, 1)

            def need(c):
                return [lo_count(unit(c, half)) for half in range(2)]

            ff1(1, C_FF1_1 % 2, need(C_FF1_1), [FF_BASE[2], FF_BASE[3]], between=transpose_hidden)
            ff2(0, C_FF2_0 % 2, need(C_FF2_0), first=True)
            with pe.Fori(0, G // 2 - 1) as i:
                for g in range(2):
                    c = C_LOOP + 2 * g
                    ff1(g, c % 2, [i * 8 + n for n in need(c)],
                        [i + (FF_BASE[2 * g + f] + g) for f in range(2)])
                    ff2(1 - g, (c + 1) % 2, [i * 8 + n for n in need(c + 1)], i * 4 + (2 + 2 * g))
            ff2(1, C_LAST % 2, need(C_LAST), 2 * G - 2, last=True)


def kernel(**inputs):
    import concourse.bacc as bacc
    from concourse.bass_utils import run_bass_kernel_spmd

    names = ["x", "xT", "memT", "w_in", "w_gate_up", "b_gate", "gla_norm_g", "w_mix_o", "ln1_g", "ln1_b",
             "w_xq", "w_xkv", "w_xo", "ln2_g", "ln2_b", "w_ff1", "w_ff2", "ln3_g", "ln3_b"]
    laid = {n: np.asarray(a)[0] for n, a in inputs.items()}
    laid["b_gate"] = laid["b_gate"].reshape(2, P).T
    laid["xT"], laid["memT"] = laid["x"].T, laid["mem"].T
    arrays = {f"in_{n}": np.ascontiguousarray(laid[n]) for n in names}
    arrays["in_consts"] = shape_constants()
    nc = bacc.Bacc("TRN2", target_bir_lowering=False, num_devices=1)
    args = {n: nc.dram_tensor(f"in_{n}", arrays[f"in_{n}"].shape, mybir.dt.float32, kind="ExternalInput").ap()
            for n in names + ["consts"]}
    out = nc.dram_tensor("out", (S, D), mybir.dt.float32, kind="ExternalOutput").ap()
    build(nc, out=out, **args)
    result = run_bass_kernel_spmd(nc, [arrays], core_ids=[0]).results[0]["out"]
    return result.reshape(1, S, D)
```
